# Optimizing a Trainium2 kernel written in Bass

```python
import math
import jax, jax.numpy as jnp
from jax import lax
import numpy as np

D_MODEL = 1024
BATCH = 1
SEQ = 1024
DEPTH = 2

ALPHA = (2 * DEPTH) ** 0.25
BETA = (8 * DEPTH) ** -0.25
N_EVEN = (DEPTH + 1) // 2
N_ODD = DEPTH // 2

CHUNK = 128
A_WIDTH = D_MODEL // 2
A_GROUPS = 4
A_GROUP_DIM = A_WIDTH // A_GROUPS

B_HEADS = 8
B_KV_HEADS = 2
B_HEAD_DIM = (D_MODEL // 2) // B_HEADS
CMP_STRIDE = 16
CMP_BLOCK = 2 * CMP_STRIDE
SEL_BLOCK = 64
N_SELECT = 16
WINDOW = 512
Q_BLOCK = 128

N_BUCKETS = 32
MAX_DISTANCE = 1024

CONV_WIDTH = 31

FFN_HIDDEN = ((8 * D_MODEL // 3 + 255) // 256) * 256

PROJ_WIDTH = 2 * A_WIDTH + B_HEADS * B_HEAD_DIM + 6 * B_KV_HEADS * B_HEAD_DIM + 3 * B_HEADS

NEG_INF = -1e30
FORCE = 1e9

kernel_name = "hybrid_gmlp_nsa_conformer_deepnorm"

def layer_norm(x, g, b, eps=1e-5):
    xf = x.astype(jnp.float32)
    mu = jnp.mean(xf, axis=-1, keepdims=True)
    var = jnp.mean(jnp.square(xf - mu), axis=-1, keepdims=True)
    y = (xf - mu) * lax.rsqrt(var + eps)
    return (y * g.astype(jnp.float32) + b.astype(jnp.float32)).astype(x.dtype)

def t5_bucket(dist):
    n = jnp.maximum(dist, 0)
    max_exact = N_BUCKETS // 2
    nf = jnp.maximum(n, 1).astype(jnp.float32)
    large = max_exact + (jnp.log(nf / max_exact) / math.log(MAX_DISTANCE / max_exact)
                         * (N_BUCKETS - max_exact)).astype(jnp.int32)
    large = jnp.minimum(large, N_BUCKETS - 1)
    return jnp.where(n < max_exact, n, large)

def spatial_gating(u, v, ln_g, ln_b, w_s, b_s):
    B_, S, _ = v.shape
    v = layer_norm(v, ln_g, ln_b)
    vr = v.reshape(B_, S // CHUNK, CHUNK, A_GROUPS, A_GROUP_DIM)
    mask = jnp.tril(jnp.ones((CHUNK, CHUNK), dtype=bool))
    w = jnp.where(mask[None], w_s, jnp.zeros_like(w_s))
    s = jnp.einsum('gts,bcsgd->bctgd', w, vr) + b_s.T[None, None, :, :, None]
    return u * s.reshape(B_, S, A_WIDTH)

def compress(k, pe, w1, w2):
    B_, S, Hkv, dh = k.shape
    kr = k.reshape(B_, S // CMP_STRIDE, CMP_STRIDE, Hkv, dh)
    blocks = jnp.concatenate([kr[:, :-1], kr[:, 1:]], axis=2)
    blocks = blocks + pe[None, None, :, None, :]
    n_cmp = blocks.shape[1]
    flat = blocks.transpose(0, 1, 3, 2, 4).reshape(B_, n_cmp, Hkv, CMP_BLOCK * dh)
    return jax.nn.gelu(flat @ w1) @ w2

def nsa(q, k_cmp, v_cmp, k_slc, v_slc, k_win, v_win, gates, rel_bias,
        pe_k, w1_k, w2_k, pe_v, w1_v, w2_v):
    B_, S, H, dh = q.shape
    Hkv = k_cmp.shape[2]
    G = H // Hkv
    scale = dh ** -0.5

    kc = compress(k_cmp, pe_k, w1_k, w2_k)
    vc = compress(v_cmp, pe_v, w1_v, w2_v)
    n_cmp = kc.shape[1]
    cmp_start = jnp.arange(n_cmp, dtype=jnp.int32) * CMP_STRIDE
    cmp_end = cmp_start + CMP_BLOCK - 1

    n_sel = S // SEL_BLOCK
    ks_blk = k_slc.reshape(B_, n_sel, SEL_BLOCK, Hkv, dh).transpose(0, 3, 1, 2, 4)
    vs_blk = v_slc.reshape(B_, n_sel, SEL_BLOCK, Hkv, dh).transpose(0, 3, 1, 2, 4)
    sel_start = jnp.arange(n_sel, dtype=jnp.int32) * SEL_BLOCK
    overlap = ((cmp_start[:, None] < sel_start[None] + SEL_BLOCK)
               & (cmp_start[:, None] + CMP_BLOCK > sel_start[None])).astype(jnp.float32)
    n_top = min(N_SELECT, n_sel)

    kw_pad = jnp.pad(k_win, ((0, 0), (WINDOW, 0), (0, 0), (0, 0)))
    vw_pad = jnp.pad(v_win, ((0, 0), (WINDOW, 0), (0, 0), (0, 0)))

    tbl = rel_bias.reshape(N_BUCKETS, Hkv, G).transpose(1, 0, 2)
    b_idx = jnp.arange(B_)[:, None, None, None]
    h_idx = jnp.arange(Hkv)[None, :, None, None]

    n_blk = S // Q_BLOCK
    q_blocks = q.reshape(B_, n_blk, Q_BLOCK, Hkv, G, dh).transpose(1, 0, 2, 3, 4, 5)
    g_blocks = gates.reshape(B_, n_blk, Q_BLOCK, H, 3).transpose(1, 0, 2, 3, 4)

    def block_fn(args):
        qb, gb, ib = args
        t0 = ib * Q_BLOCK
        tq = t0 + jnp.arange(Q_BLOCK, dtype=jnp.int32)
        qh = qb.transpose(0, 2, 3, 1, 4) * scale

        dist_c = tq[:, None] - cmp_end[None]
        valid_c = dist_c >= 0
        bias_c = tbl[:, t5_bucket(dist_c), :].transpose(0, 3, 1, 2)
        lc = jnp.einsum('bhgqd,bchd->bhgqc', qh, kc).astype(jnp.float32)
        lc = jnp.where(valid_c, lc + bias_c.astype(jnp.float32), NEG_INF)
        pc = jax.nn.softmax(lc, axis=-1) * jnp.any(valid_c, axis=-1)[:, None].astype(jnp.float32)
        o_c = jnp.einsum('bhgqc,bchd->bhgqd', pc.astype(vc.dtype), vc)

        imp = jnp.einsum('bhgqc,cs->bhqs', pc, overlap)
        jq = (tq // SEL_BLOCK)[:, None]
        js = jnp.arange(n_sel, dtype=jnp.int32)[None]
        imp = jnp.where(js > jq, NEG_INF, imp)
        imp = jnp.where((js == 0) | (js == jq) | (js == jq - 1), FORCE, imp)
        _, idx = lax.top_k(imp, n_top)

        ks = ks_blk[b_idx, h_idx, idx].reshape(B_, Hkv, Q_BLOCK, n_top * SEL_BLOCK, dh)
        vs = vs_blk[b_idx, h_idx, idx].reshape(B_, Hkv, Q_BLOCK, n_top * SEL_BLOCK, dh)
        pos_s = (idx[..., None] * SEL_BLOCK + jnp.arange(SEL_BLOCK, dtype=jnp.int32)).reshape(
            B_, Hkv, Q_BLOCK, n_top * SEL_BLOCK)
        dist_s = tq[None, None, :, None] - pos_s
        bias_s = tbl[h_idx, t5_bucket(dist_s)].transpose(0, 1, 4, 2, 3)
        ls = jnp.einsum('bhgqd,bhqkd->bhgqk', qh, ks).astype(jnp.float32)
        ls = jnp.where((dist_s >= 0)[:, :, None], ls + bias_s.astype(jnp.float32), NEG_INF)
        o_s = jnp.einsum('bhgqk,bhqkd->bhgqd', jax.nn.softmax(ls, axis=-1).astype(vs.dtype), vs)

        kw = lax.dynamic_slice_in_dim(kw_pad, t0, Q_BLOCK + WINDOW, axis=1)
        vw = lax.dynamic_slice_in_dim(vw_pad, t0, Q_BLOCK + WINDOW, axis=1)
        pos_w = t0 - WINDOW + jnp.arange(Q_BLOCK + WINDOW, dtype=jnp.int32)
        dist_w = tq[:, None] - pos_w[None]
        valid_w = (dist_w >= 0) & (dist_w < WINDOW) & (pos_w[None] >= 0)
        bias_w = tbl[:, t5_bucket(dist_w), :].transpose(0, 3, 1, 2)
        lw = jnp.einsum('bhgqd,bkhd->bhgqk', qh, kw).astype(jnp.float32)
        lw = jnp.where(valid_w, lw + bias_w.astype(jnp.float32), NEG_INF)
        o_w = jnp.einsum('bhgqk,bkhd->bhgqd', jax.nn.softmax(lw, axis=-1).astype(vw.dtype), vw)

        g = gb.reshape(B_, Q_BLOCK, Hkv, G, 3).transpose(0, 2, 3, 1, 4)
        o = g[..., 0:1] * o_c + g[..., 1:2] * o_s + g[..., 2:3] * o_w
        return o.transpose(0, 3, 1, 2, 4).reshape(B_, Q_BLOCK, H * dh)

    out = lax.map(block_fn, (q_blocks, g_blocks, jnp.arange(n_blk, dtype=jnp.int32)))
    return out.transpose(1, 0, 2, 3).reshape(B_, S, H * dh)

def hybrid_mixer(x, w_in, w_out, ln_g, ln_b, w_s, b_s, rel_bias,
                 pe_k, w1_k, w2_k, pe_v, w1_v, w2_v):
    B_, S, _ = x.shape
    h = x @ w_in
    QW = B_HEADS * B_HEAD_DIM
    KV = B_KV_HEADS * B_HEAD_DIM
    uv = jax.nn.gelu(h[..., :2 * A_WIDTH])
    a_out = spatial_gating(uv[..., :A_WIDTH], uv[..., A_WIDTH:], ln_g, ln_b, w_s, b_s)
    o = 2 * A_WIDTH
    q = h[..., o:o + QW].reshape(B_, S, B_HEADS, B_HEAD_DIM)
    o += QW
    kvs = []
    for _ in range(6):
        kvs.append(h[..., o:o + KV].reshape(B_, S, B_KV_HEADS, B_HEAD_DIM))
        o += KV
    gates = jax.nn.sigmoid(h[..., o:o + 3 * B_HEADS]).reshape(B_, S, B_HEADS, 3)
    b_out = nsa(q, kvs[0], kvs[1], kvs[2], kvs[3], kvs[4], kvs[5], gates, rel_bias,
                pe_k, w1_k, w2_k, pe_v, w1_v, w2_v)
    return jnp.concatenate([a_out, b_out], axis=-1) @ w_out

def conv_module(x, w_in, b_in, dw_w, dw_b, ln_g, ln_b, w_out, b_out):
    C = w_out.shape[0]
    h = x @ w_in + b_in
    h = h[..., :C] * jax.nn.sigmoid(h[..., C:])
    h = lax.conv_general_dilated(h, dw_w[:, None, :], window_strides=(1,),
                                 padding=[(CONV_WIDTH - 1, 0)],
                                 dimension_numbers=('NWC', 'WIO', 'NWC'),
                                 feature_group_count=C) + dw_b
    h = jax.nn.silu(layer_norm(h, ln_g, ln_b))
    return h @ w_out + b_out

def swiglu(x, w_gate, w_up, w_down):
    return (jax.nn.silu(x @ w_gate) * (x @ w_up)) @ w_down

def setup_inputs(seed: int = 0) -> dict:
    key = jax.random.key(seed)
    keys = iter(jax.random.split(key, 40))

    def nrm(shape, scale):
        return jax.random.normal(next(keys), shape, jnp.float32) * scale

    D, A, dh = D_MODEL, A_WIDTH, B_HEAD_DIM
    return {
        "x": nrm((BATCH, SEQ, D), 1.0),
        "rel_bias": nrm((N_BUCKETS, B_HEADS), 0.5),
        "hyb_w_in": nrm((N_EVEN, D, PROJ_WIDTH), D ** -0.5),
        "hyb_w_out": nrm((N_EVEN, D, D), BETA * D ** -0.5),
        "gmlp_ln_g": 1.0 + nrm((N_EVEN, A), 0.01),
        "gmlp_ln_b": nrm((N_EVEN, A), 0.01),
        "gmlp_w_s": nrm((N_EVEN, A_GROUPS, CHUNK, CHUNK), CHUNK ** -0.5),
        "gmlp_b_s": 1.0 + nrm((N_EVEN, A_GROUPS, CHUNK), 0.1),
        "cmp_pe_k": nrm((N_EVEN, CMP_BLOCK, dh), 0.1),
        "cmp_w1_k": nrm((N_EVEN, CMP_BLOCK * dh, dh), (CMP_BLOCK * dh) ** -0.5),
        "cmp_w2_k": nrm((N_EVEN, dh, dh), dh ** -0.5),
        "cmp_pe_v": nrm((N_EVEN, CMP_BLOCK, dh), 0.1),
        "cmp_w1_v": nrm((N_EVEN, CMP_BLOCK * dh, dh), (CMP_BLOCK * dh) ** -0.5),
        "cmp_w2_v": nrm((N_EVEN, dh, dh), dh ** -0.5),
        "conv_w_in": nrm((N_ODD, D, 2 * D), D ** -0.5),
        "conv_b_in": nrm((N_ODD, 2 * D), 0.01),
        "conv_dw_w": nrm((N_ODD, CONV_WIDTH, D), CONV_WIDTH ** -0.5),
        "conv_dw_b": nrm((N_ODD, D), 0.01),
        "conv_ln_g": 1.0 + nrm((N_ODD, D), 0.01),
        "conv_ln_b": nrm((N_ODD, D), 0.01),
        "conv_w_out": nrm((N_ODD, D, D), BETA * D ** -0.5),
        "conv_b_out": nrm((N_ODD, D), 0.01),
        "ffn_w_gate": nrm((DEPTH, D, FFN_HIDDEN), D ** -0.5),
        "ffn_w_up": nrm((DEPTH, D, FFN_HIDDEN), D ** -0.5),
        "ffn_w_down": nrm((DEPTH, FFN_HIDDEN, D), BETA * FFN_HIDDEN ** -0.5),
        "norm_mix_g": 1.0 + nrm((DEPTH, D), 0.01),
        "norm_mix_b": nrm((DEPTH, D), 0.01),
        "norm_ffn_g": 1.0 + nrm((DEPTH, D), 0.01),
        "norm_ffn_b": nrm((DEPTH, D), 0.01),
    }

def reference(x, rel_bias, hyb_w_in, hyb_w_out, gmlp_ln_g, gmlp_ln_b, gmlp_w_s, gmlp_b_s,
              cmp_pe_k, cmp_w1_k, cmp_w2_k, cmp_pe_v, cmp_w1_v, cmp_w2_v,
              conv_w_in, conv_b_in, conv_dw_w, conv_dw_b, conv_ln_g, conv_ln_b,
              conv_w_out, conv_b_out, ffn_w_gate, ffn_w_up, ffn_w_down,
              norm_mix_g, norm_mix_b, norm_ffn_g, norm_ffn_b):
    for layer in range(DEPTH):
        i = layer // 2
        if layer % 2 == 0:
            y = hybrid_mixer(x, hyb_w_in[i], hyb_w_out[i], gmlp_ln_g[i], gmlp_ln_b[i],
                             gmlp_w_s[i], gmlp_b_s[i], rel_bias,
                             cmp_pe_k[i], cmp_w1_k[i], cmp_w2_k[i],
                             cmp_pe_v[i], cmp_w1_v[i], cmp_w2_v[i])
        else:
            y = conv_module(x, conv_w_in[i], conv_b_in[i], conv_dw_w[i], conv_dw_b[i],
                            conv_ln_g[i], conv_ln_b[i], conv_w_out[i], conv_b_out[i])
        x = layer_norm(ALPHA * x + y, norm_mix_g[layer], norm_mix_b[layer])
        f = swiglu(x, ffn_w_gate[layer], ffn_w_up[layer], ffn_w_down[layer])
        x = layer_norm(ALPHA * x + f, norm_ffn_g[layer], norm_ffn_b[layer])
    return x


_drawn_inputs = setup_inputs


def setup_inputs(seed=0):
    import zlib

    import numpy as np

    out = dict(_drawn_inputs(seed))
    spreads = {}
    factors = {'rel_bias': 3.994,
     'gmlp_ln_g': 49.567,
     'gmlp_ln_b': 44.466,
     'gmlp_b_s': 3.426,
     'cmp_pe_k': 8.0,
     'cmp_w1_k': 5.194,
     'cmp_w2_k': 5.17,
     'cmp_pe_v': 7.653,
     'conv_b_in': 30.857,
     'conv_dw_b': 24.778,
     'conv_ln_g': 200.0,
     'conv_ln_b': 200.0,
     'conv_b_out': 117.396,
     'norm_mix_g': 10.437,
     'norm_mix_b': 11.215,
     'norm_ffn_g': 13.68,
     'norm_ffn_b': 13.351}
    for name, (base, spread) in spreads.items():
        noise = np.random.default_rng([zlib.crc32(name.encode()), seed]).standard_normal(out[name].shape)
        drawn = base * np.exp(spread * noise) if base else spread * noise
        out[name] = __import__('jax').numpy.asarray(drawn.astype(out[name].dtype))
    for name, factor in factors.items():
        out[name] = (out[name] * factor).astype(out[name].dtype)
    return out
```

```python
from contextlib import ExitStack

import numpy as np

import concourse.bass as bass
import concourse.mybir as mybir
from concourse.alu_op_type import AluOpType as ALU

F32 = mybir.dt.float32
F32R = mybir.dt.float32r
BF16 = mybir.dt.bfloat16
ACT = mybir.ActivationFunctionType

P = 128
D = 1024
SEQ = 1024
KT = D // P
TT = SEQ // P
HALF = 512
DEPTH = 2
ALPHA = float((2 * DEPTH) ** 0.25)
EPS = 1e-5

A_WIDTH = D // 2
GROUPS = 4
HEADS = 8
KV_HEADS = 2
G = HEADS // KV_HEADS
DH = 64
SCALE = DH ** -0.5
CMP_STRIDE = 16
CMP_BLOCK = 32
N_CMP = SEQ // CMP_STRIDE - 1
WINDOW = 512
N_BUCKETS = 32
MAX_DISTANCE = 1024
BIG = 1.0e30

KV0 = 2 * A_WIDTH + HEADS * DH
COL_KCMP, COL_VCMP, COL_KSLC, COL_VSLC, COL_KWIN, COL_VWIN = (KV0 + P * n for n in range(6))
COL_Q = 2 * A_WIDTH
GATES = 3 * HEADS
VG = 2 * P + GATES

FFN = 2816
FT = FFN // P
FG = FT // 2
CONV_W = 31
PAD = CONV_W - 1

RING = 6
RAWS = 2
BIAS_ROW = 1152
FEATURE_COLS = [COL_KCMP, COL_VCMP, COL_KSLC, COL_KWIN] + [n * P for n in range(GROUPS)] + [
    COL_Q + n * P for n in range(4)]
F_U, F_Q = 4, 8


class Chunk:

    def __init__(self, slot, raw, number, landed, before):
        self.slot, self.raw, self.number, self.landed, self.before = slot, raw, number, landed, before
        self.used = before + 1


class Stream:

    def __init__(self):
        self.count, self.uses, self.landed = 0, [0] * RING, [0] * RAWS

    def take(self, slots, dmas=1):
        out = []
        for slot in slots:
            raw = self.count % RAWS
            self.landed[raw] += 16 * dmas
            self.count += 1
            out.append(Chunk(slot, raw, self.count, self.landed[raw], self.uses[slot]))
            self.uses[slot] += 1
        return out

    def loop(self, slots, trips):
        first = self.take(slots)
        for _ in range(trips - 1):
            self.take(slots)
        per = len(slots)
        assert per % RAWS == 0 and len(set(slots)) == per

        def trip(n):
            return [Chunk(c.slot, c.raw, per * n + c.number, (16 * per // RAWS) * n + c.landed, n + c.before)
                    for c in first]
        return trip


def plan():
    s = Stream()
    tail = [4, 5, 0, 1, 2, 3, 4, 5]
    r = {"v": s.take([0, 1, 2, 3]), "vg": s.take([4, 5, 0], 2), "feat": s.take([(1 + n) % RING for n in range(12)])}
    r["w_out"] = s.take(tail)
    for layer in range(DEPTH):
        if layer == 1:
            r["conv_in"] = s.loop([0, 1, 2, 3], KT // 2)
            r["conv_out"] = s.take(tail)
        r[f"ffn{layer}_first"] = s.take([0, 1, 2, 3])
        r[f"ffn{layer}"] = s.loop([0, 4, 5, 1, 2, 3], FG - 1)
        r[f"ffn{layer}_last"] = s.take([4, 5])
    return r


GROUP_COUNT = {"w_out": KT // 2, "ffn0": FG, "conv_out": KT // 2, "ffn1": FG}
NORM_OF = {"w_out": 1, "ffn0": 2, "conv_out": 3, "ffn1": 4}


UNITS = [(i, kv) for kv in range(KV_HEADS) for i in range(TT)]


def window(i):
    return max(0, i - WINDOW // P) * P, min(WINDOW // P + 1, i + 1) * P


def key_tiles():
    steps, of = [], []
    for u, (i, _) in enumerate(UNITS):
        first = len(steps)
        steps += [(u, j * P, P, "sel", j) for j in range(i + 1)]
        k0, nk = window(i)
        steps += [(u, SEQ + j * P, P, "win", k0 // P + j) for j in range(nk // P)]
        steps.append((u, SEQ + WINDOW + P, min(N_CMP, 8 * i + 7), "cmp", 0))
        of.append((first, len(steps)))
    return steps, of


STEPS, STEPS_OF = key_tiles()


def attention_order():
    def softmax(u):
        out = []
        for g in range(G):
            out += [("logits", u, g)] + ([("norm", u, g - 1)] if g else [])
        return out + [("norm", u, G - 1)]

    order = softmax(0)
    for u in range(len(UNITS)):
        nxt = softmax(u + 1) if u + 1 < len(UNITS) else []
        first, last = STEPS_OF[u]
        m, n = 0, last - first
        for k in range(n):
            order.append(("step", u, first + k))
            to = min(len(nxt), -(-len(nxt) * (k + 1) // max(1, n - 1)))
            order += nxt[m:to]
            m = to
        order += nxt[m:] + [("out", u, 0)]
    return order


def build(nc, a):
    ring = plan()
    at, here = {}, [(nc.sbuf_base + 63) // 64 * 64]

    def sb(name, shape, dt=F32, offset=None):
        size = int(np.prod(shape[1:])) * (2 if dt == BF16 else 4)
        if offset is None:
            offset = here[0]
            here[0] += (size + 31) // 32 * 32
        assert offset + size <= nc.sbuf_usable_end, name
        at[name] = offset
        return nc.alloc_sbuf_tensor_at(name, shape, dt, offset=offset)

    resid = sb("resid", [P, TT, D])
    xt_hi = sb("xt_hi", [P, KT, SEQ], F32R)
    xt_lo = sb("xt_lo", [P, KT, SEQ], F32R)
    wt_hi = sb("wt_hi", [P, RING, D], F32R)
    wt_lo = sb("wt_lo", [P, RING, D], F32R)
    wt_raw = sb("wt_raw", [P, RAWS, D])
    ident = sb("ident", [P, P])
    ident_b = sb("ident_b", [P, P], BF16)
    far_mask = sb("far_mask", [P, P], BF16)
    cols = sb("cols", [P, 40])
    eps_c = sb("eps_c", [P, 1])
    stats = sb("stats", [P, 2, 6])
    mv = sb("mv", [P, 2])
    rstd = sb("rstd", [P, 1])
    v_mean = sb("v_mean", [P, TT, 2])
    v_rstd = sb("v_rstd", [P, TT])
    v_stats = sb("v_stats", [P, TT, 6])
    w2 = sb("w2", [P, 2, DH])
    pe_col = sb("pe_col", [P, 2, CMP_BLOCK])
    hid = sb("hid", [P, 2, 64])
    pe_bias = sb("pe_bias", [P, 2])
    row_ok = sb("row_ok", [P, 1])
    q_t = sb("q_t", [P, 4, SEQ])
    ks = sb("ks", [P, KV_HEADS, 2, SEQ], F32R)
    vg = sb("vg", [P, TT, VG])
    cr = sb("cr", [P, 2, SEQ])
    low = sb("low", [P, 2, G, 3])
    den = sb("den", [P, 2, G, 3])
    inv = sb("inv", [P, 2, G, 3])
    kc = sb("kc", [P, KV_HEADS, 64], F32R)
    vc = sb("vc", [64, KV_HEADS, DH])
    o = at["q_t"]
    gmlp_g = sb("gmlp_g", [P, A_WIDTH], F32, o)
    gmlp_b = sb("gmlp_b", [P, A_WIDTH], F32, o + 2048)
    gmlp_bs = sb("gmlp_bs", [P, GROUPS, P], F32, o + 4096)
    ws = sb("ws", [P, GROUPS, P], F32, o + 6144)
    ws_t = sb("ws_t", [P, GROUPS, P], F32, o + 8192)
    onehot = sb("onehot", [N_BUCKETS, BIAS_ROW], F32, o + 10240)
    u_act = sb("u_act", [P, SEQ], F32, o + 10240)
    o = at["vg"]
    bias_row = sb("bias_row", [HEADS, BIAS_ROW], F32, o)
    rbias = sb("rbias", [N_BUCKETS, HEADS], F32, o + 4608)
    pe_row = sb("pe_row", [2 * CMP_BLOCK, P], F32, o + 4640)
    rows = sb("rows", [40, P], F32, o + 5152)
    qs = sb("qs", [P, 2, 2, G, P], F32R, at["cr"])
    o = at["resid"]
    mix_a = sb("mix_a", [P, GROUPS, SEQ], F32, o)
    v_tok = sb("v_tok", [P, TT, A_WIDTH], F32, o + 16384)
    w1 = sb("w1", [P, 2, CMP_BLOCK, DH], F32, o + 16384)
    nbias = sb("nbias", [P, HEADS, SEQ], F32, o)
    WIN0, CMP0 = SEQ, SEQ + WINDOW + P
    probs = sb("probs", [P, 2, G, CMP0 + 64], F32, at["wt_hi"])
    probs_t = [sb("probs_t0", [P, G, P]), sb("probs_t1", [P, G, P], F32, at["wt_hi"] + 2 * G * (CMP0 + 64) * 4)]
    misc = at["q_t"]
    h_hi_t = sb("h_hi_t", [P, 2, SEQ], F32R, misc)
    h_lo_t = sb("h_lo_t", [P, 2, SEQ], F32R, misc + 8192)
    gate_act = sb("gate_act", [P, SEQ], F32, misc + 16384)
    h_f = sb("h_f", [P, SEQ], F32, misc + 20480)
    ln_g = sb("ln_g", [P, D], F32, misc + 33792)
    ln_b = sb("ln_b", [P, D], F32, misc + 37888)
    acc = sb("acc", [P, KT, SEQ], F32, misc)
    taps = sb("taps", [P, KT, CONV_W], F32, misc + 32768)
    conv_x = sb("conv_x", [P, 2, PAD + SEQ], F32, misc + 33792)
    glu_g = sb("glu_g", [P, SEQ], F32, misc + 42240)
    out_b = sb("out_b", [P, D], F32, misc + 46336)
    tap_rows = sb("tap_rows", [CONV_W, D], F32, misc + 46336)
    square = sb("square", [P, SEQ], F32, misc + 42240)
    ones_m = sb("ones_m", [P, P], F32, misc + 33792)
    conv_rs = sb("conv_rs", [P, SEQ], F32, misc + 46336)
    ps = nc.alloc_psum_tensor("ps", [P, 8, HALF], F32)

    def sem(*names):
        made = [nc.alloc_semaphore(n) for n in names]
        return made if len(made) > 1 else made[0]

    def sems(name, keys):
        return {k: nc.alloc_semaphore(f"{name}_{k}") for k in keys}

    x_in, w_in, w_used = sems("x_in", range(TT)), sems("w_in", range(RAWS)), sems("w_used", range(RING))
    w_hi, w_lo = sem("w_hi", "w_lo")
    par_in, const_ok, small_t, small_c, ws_ok = sem("par_in", "const_ok", "small_t", "small_c", "ws_ok")
    bias_out, nb_ok, w1_in = sem("bias_out", "nb_ok", "w1_in")
    nb_in = sems("nb_in", range(KV_HEADS))
    ln_in, ln_mv, ln_sd, ln_done = sem("ln_in", "ln_mv", "ln_sd", "ln_done")
    turned, turned_hi, turned_lo, scaled = sem("turned", "turned_hi", "turned_lo", "scaled")
    v_step, g_step = sem("v_step", "g_step")
    v_done, v_gelu, v_mv, v_sd, v_norm = sem("v_done", "v_gelu", "v_mv", "v_sd", "v_norm")
    vg_done, vg_out, feat_act, feat_dve = sem("vg_done", "vg_out", "feat_act", "feat_dve")
    u_mul, mix_done, mix_add, a_hi, a_lo, gates_ok = sem("u_mul", "mix_done", "mix_add", "a_hi", "a_lo", "gates_ok")
    cmp_done, cmp_act, cmp_dve = sem("cmp_done", "cmp_act", "cmp_dve")
    qs_ok, s_done, s_min, p_exp, p_norm = sem("qs_ok", "s_done", "s_min", "p_exp", "p_norm")
    pt_done, pt_act, pt_dve, pv_done, o_hi, o_lo = sem("pt_done", "pt_act", "pt_dve", "pv_done", "o_hi", "o_lo")
    y_done, y_free = sems("y_done", GROUP_COUNT), sems("y_free", GROUP_COUNT)
    silu_done, h_prod, h_hi, h_lo = (sems(n, range(DEPTH)) for n in ("silu_done", "h_prod", "h_hi", "h_lo"))
    tap_in, tap_t, tap_ok, outb_in, outb_ok = sem("tap_in", "tap_t", "tap_ok", "outb_in", "outb_ok")
    glu_sig, glu_free, conv_v, pad_ok, ones_ok = sem("glu_sig", "glu_free", "conv_v", "pad_ok", "ones_ok")
    mean_ok, cen, sq_ok, sq_used, var_sd, nrm, act_ok, act_hi, act_lo = sem(
        "mean_ok", "cen", "sq_ok", "sq_used", "var_sd", "nrm", "act_ok", "act_hi", "act_lo")
    out_done = sem("out_done")

    w_in_ap, w_out_ap = a["hyb_w_in"], a["hyb_w_out"]
    PARAMS = 18

    def banks(b, n=2):
        return ps[:, b:b + n, :].rearrange("p b c -> p (b c)")

    def tile_cols(t):
        return slice(t * P, (t + 1) * P)

    def raw(c):
        return wt_raw[:, c.raw, :]

    def load_chunk(sp, c, pieces):
        if not (isinstance(c.number, int) and c.number <= RAWS):
            sp.wait_ge(w_lo, c.number - RAWS)
        for dst, src in pieces:
            sp.dma_start(dst, src).then_inc(w_in[c.raw], 16)

    def split_hi(act, c):
        act.wait_ge(w_in[c.raw], c.landed)
        if not (isinstance(c.before, int) and c.before == 0):
            act.wait_ge(w_used[c.slot], c.before)
        nc.scalar.copy(wt_hi[:, c.slot, :], raw(c)).then_inc(w_hi, 1)

    def split_lo(dve, c):
        dve.wait_ge(w_hi, c.number)
        nc.vector.tensor_tensor(wt_lo[:, c.slot, :], raw(c), wt_hi[:, c.slot, :], ALU.subtract).then_inc(w_lo, 1)

    def feature_product(pe, c, b):
        pe.wait_ge(w_lo, c.number)
        for k in range(KT):
            hi, lo = wt_hi[:, c.slot, tile_cols(k)], wt_lo[:, c.slot, tile_cols(k)]
            for n, (w, x) in enumerate(((hi, xt_hi), (hi, xt_lo), (lo, xt_hi))):
                for h in range(2):
                    last = nc.tensor.matmul(ps[:, b + h, :], w, x[:, k, h * HALF:(h + 1) * HALF],
                                            start=(k == 0 and n == 0), stop=(k == KT - 1 and n == 2))
        last.then_inc(w_used[c.slot], 1)

    def token_product(pe, name, cs, left, group, turn=False):
        pe.wait_ge(w_lo, cs[1].number)
        for t in range(TT):
            for h in range(2):
                q = 2 * t + h
                pe.wait_ge(y_free[name], 16 * group + (q + 1))
                cols_h = slice(h * HALF, (h + 1) * HALF)
                for j, c in enumerate(cs):
                    lh, ll = (x[:, tile_cols(t)] for x in left[j])
                    rh, rl = wt_hi[:, c.slot, cols_h], wt_lo[:, c.slot, cols_h]
                    bank = ps[:, 4 + q % 4, :]
                    nc.tensor.matmul(bank, lh, rh, start=(j == 0), stop=False)
                    nc.tensor.matmul(bank, lh, rl, start=False, stop=False)
                    last = nc.tensor.matmul(bank, ll, rh, start=False, stop=(j == 1))
                    if q == 15:
                        last.then_inc(w_used[c.slot], 1)
                if q < 15:
                    last.then_inc(y_done[name], 1)
            if turn and t >= 2:
                turn_tile(pe, NORM_OF[name], t - 2)
        if turn:
            turn_tile(pe, NORM_OF[name], TT - 2)
            turn_tile(pe, NORM_OF[name], TT - 1)
            pe.wait_ge(turned_lo, TT * (NORM_OF[name] + 1))

    def add_bank(dve, name, c, group, q):
        if q < 15:
            dve.wait_ge(y_done[name], 15 * group + (q + 1))
        else:
            dve.wait_ge(w_used[c.slot], c.used)
        r = resid[:, q // 2, (q % 2) * HALF:(q % 2 + 1) * HALF]
        nc.vector.tensor_tensor(r, r, ps[:, 4 + q % 4, :], ALU.add).then_inc(y_free[name], 1)

    steps_of_v = [0]

    def v_wait(dve, *made):
        for ins in made:
            ins.then_inc(v_step, 1)
        steps_of_v[0] += len(made)
        dve.wait_ge(v_step, steps_of_v[0])

    def norm_tile(dve, name, t):
        e = TT * (NORM_OF[name] - 1) + t
        x = resid[:, t, :]
        dve.wait_ge(y_free[name], 4 + 16 * (GROUP_COUNT[name] - 1) + 2 * t + 2)
        v_wait(dve, nc.vector.bn_stats(stats[:, 0, :], x[:, 0:HALF]), nc.vector.bn_stats(stats[:, 1, :], x[:, HALF:D]))
        nc.vector.bn_aggr(mv[:], stats[:]).then_inc(ln_mv, 1)
        dve.wait_ge(ln_sd, e + 1)
        v_wait(dve, nc.vector.reciprocal(rstd[:], rstd[:]))
        v_wait(dve, nc.vector.tensor_scalar(x, x, mv[:, 0:1], rstd[:, 0:1], ALU.subtract, ALU.mult))
        if t == 0:
            dve.wait_ge(ln_in, 32 * NORM_OF[name])
        v_wait(dve, nc.vector.tensor_tensor(x, x, ln_g[:], ALU.mult))
        nc.vector.tensor_tensor(x, x, ln_b[:], ALU.add).then_inc(ln_done, 1)

    def turn_tile(pe, event, t):
        if event == 0:
            pe.wait_ge(x_in[t], 16)
        else:
            pe.wait_ge(ln_done, TT * (event - 1) + t + 1)
        if t >= 2:
            pe.wait_ge(turned_lo, TT * event + t - 1)
        for k in range(KT):
            last = nc.tensor.transpose(ps[:, 2 * (t % 2) + k // 4, tile_cols(k % 4)], resid[:, t, tile_cols(k)], ident[:])
        last.then_inc(turned, 1)

    def turned_view(t):
        return ps[:, 2 * (t % 2):2 * (t % 2) + 2, :].rearrange("p b (k c) -> p (b k) c", c=P)

    def turn_hi(act, event, t):
        act.wait_ge(turned, TT * event + t + 1)
        nc.scalar.copy(xt_hi[:, :, tile_cols(t)], turned_view(t)).then_inc(turned_hi, 1)

    def turn_lo(dve, event, t):
        dve.wait_ge(turned_hi, TT * event + t + 1)
        nc.vector.tensor_tensor(xt_lo[:, :, tile_cols(t)], turned_view(t), xt_hi[:, :, tile_cols(t)],
                                ALU.subtract).then_inc(turned_lo, 1)

    def scale_tile(act, t):
        nc.scalar.mul(resid[:, t, :], resid[:, t, :], ALPHA).then_inc(scaled, 1)

    def norm_act(act, name, turn=True):
        e = NORM_OF[name]
        for t in range(TT + 1):
            if t < TT:
                act.wait_ge(ln_mv, TT * (e - 1) + t + 1)
                nc.scalar.activation(rstd[:], mv[:, 1:2], ACT.Sqrt, bias=eps_c[:, 0:1]).then_inc(ln_sd, 1)
            if t and turn:
                turn_hi(act, e, t - 1)
                scale_tile(act, t - 1)

    def norm_dve(dve, name, c, turn=True):
        for t in range(TT + 1):
            if t < TT:
                add_bank(dve, name, c, GROUP_COUNT[name] - 1, 2 * t)
                add_bank(dve, name, c, GROUP_COUNT[name] - 1, 2 * t + 1)
                norm_tile(dve, name, t)
            if t and turn:
                turn_lo(dve, NORM_OF[name], t - 1)

    def load_small(act):
        def par(dst, src):
            act.dma_start(dst, src).then_inc(par_in, 16)
        par(ws[:], a["gmlp_w_s"].rearrange("g t s -> t g s"))
        par(rbias[:], a["rel_bias"])
        par(onehot[:], a["bucket_onehot"])
        for dst, name, n in ((gmlp_g[:], "gmlp_ln_g", A_WIDTH), (gmlp_b[:], "gmlp_ln_b", A_WIDTH),
                             (gmlp_bs[:], "gmlp_b_s", A_WIDTH)):
            src = bass.AP(a[name].tensor, 0, [[0, P], [1, n]])
            par(dst.rearrange("p g t -> p (g t)") if name == "gmlp_b_s" else dst, src)
        for kv, n in enumerate("kv"):
            for h in range(2):
                par(pe_row[kv * CMP_BLOCK:(kv + 1) * CMP_BLOCK, h * DH:(h + 1) * DH], a[f"cmp_pe_{n}"])
                par(w2[h * DH:(h + 1) * DH, kv, :], a[f"cmp_w2_{n}"])
        r = 0
        for n, k in (("conv_b_in", 2 * KT), ("conv_dw_b", KT)):
            par(rows[r:r + k, :], a[n].rearrange("(k p) -> k p", p=P))
            r += k
        par(rows[r:r + KT, :], a["conv_ln_g"].rearrange("(k p) -> k p", p=P))
        par(rows[r + KT:r + 2 * KT, :], a["conv_ln_b"].rearrange("(k p) -> k p", p=P))

    def norm_params(sp, name):
        layer, kind = divmod(NORM_OF[name] - 1, 2)
        for dst, n in ((ln_g, "g"), (ln_b, "b")):
            src = bass.AP(a[f"norm_{('mix', 'ffn')[kind]}_{n}"].tensor, layer * D, [[0, P], [1, D]])
            sp.dma_start(dst[:], src).then_inc(ln_in, 16)

    def ffn_loads(sp, layer):
        wg, wu, wd = (a[n][layer] for n in ("ffn_w_gate", "ffn_w_up", "ffn_w_down"))

        def columns(c, w, f):
            load_chunk(sp, c, [(raw(c).rearrange("p (k n) -> p k n", k=KT),
                                w[:, bass.ds(f * P, P)].rearrange("(k p) n -> p k n", p=P))])

        def down(c, f):
            load_chunk(sp, c, [(raw(c), wd[bass.ds(f * P, P), :])])

        c = ring[f"ffn{layer}_first"]
        columns(c[0], wg, 0)
        columns(c[1], wu, 0)
        columns(c[2], wg, 1)
        columns(c[3], wu, 1)
        if layer == 1:
            sp.wait_ge(act_ok, KT)
            norm_params(sp, "conv_out")
        sp.wait_ge(ln_done, TT * (2 * layer + 1))
        norm_params(sp, f"ffn{layer}")
        with sp.Fori(0, FG - 1) as n:
            c = ring[f"ffn{layer}"](n)
            columns(c[0], wg, 2 * n + 2)
            down(c[1], 2 * n)
            down(c[2], 2 * n + 1)
            columns(c[3], wu, 2 * n + 2)
            columns(c[4], wg, 2 * n + 3)
            columns(c[5], wu, 2 * n + 3)
        c = ring[f"ffn{layer}_last"]
        down(c[0], FT - 2)
        down(c[1], FT - 1)

    def sync_program(sp):
        for t in range(TT):
            sp.dma_start(resid[:, t, :], a["x"][tile_cols(t), :]).then_inc(x_in[t], 16)
        for j, c in enumerate(ring["v"]):
            src = w_in_ap[2 * j * P:(2 * j + 2) * P, A_WIDTH:2 * A_WIDTH]
            load_chunk(sp, c, [(raw(c).rearrange("p (k n) -> p k n", k=2), src.rearrange("(k p) n -> p k n", p=P))])
        for j, c in enumerate(ring["vg"]):
            nk = min(3, KT - 3 * j)
            dst = raw(c)[:, 0:nk * VG].rearrange("p (k n) -> p k n", k=nk)
            k0 = slice(3 * j * P, (3 * j + nk) * P)
            load_chunk(sp, c, [
                (dst[:, :, 0:P], w_in_ap[k0, COL_VSLC:COL_VSLC + P].rearrange("(k p) n -> p k n", p=P)),
                (dst[:, :, P:VG], w_in_ap[k0, COL_VWIN:COL_VWIN + P + GATES].rearrange("(k p) n -> p k n", p=P))])
        for n, (c, col) in enumerate(zip(ring["feat"], FEATURE_COLS)):
            load_chunk(sp, c, [(raw(c).rearrange("p (k n) -> p k n", k=KT),
                                w_in_ap[:, col:col + P].rearrange("(k p) n -> p k n", p=P))])
            if n == 7:
                sp.wait_ge(mix_done, 8)
                for kv, name in enumerate("kv"):
                    for h in range(2):
                        sp.dma_start(w1[h * DH:(h + 1) * DH, kv, :, :],
                                     a[f"cmp_w1_{name}"].rearrange("(j d) m -> d j m", d=DH)).then_inc(w1_in, 16)
        sp.wait_ge(bias_out, 16)
        sp.wait_ge(a_lo, GROUPS)
        for h0 in (0, G):
            if h0:
                sp.wait_ge(cmp_done, 3)
            src = bass.AP(a["bias_scratch"].tensor, h0 * P * BIAS_ROW + P - 1,
                          [[BIAS_ROW - 1, P], [P * BIAS_ROW, G], [1, SEQ]])
            sp.dma_start(nbias[:, h0:h0 + G, :], src).then_inc(nb_in[h0 // G], 16)
        sp.wait_ge(o_lo, 2 * len(UNITS))
        sp.wait_ge(pv_done, len(STEPS))
        sp.wait_ge(p_norm, G * len(UNITS))
        for k, c in enumerate(ring["w_out"]):
            load_chunk(sp, c, [(raw(c), w_out_ap[tile_cols(k), :])])
            sp.dma_start(resid[:, k, :], a["x"][tile_cols(k), :]).then_inc(x_in[k], 16)
            if k == 1:
                norm_params(sp, "w_out")
                sp.dma_start(tap_rows[:], a["conv_dw_w"]).then_inc(tap_in, 16)
        sp.wait_ge(tap_ok, 1)
        sp.dma_start(out_b[:], bass.AP(a["conv_b_out"].tensor, 0, [[0, P], [1, D]])).then_inc(outb_in, 16)
        ffn_loads(sp, 0)
        with sp.Fori(0, KT // 2) as n:
            for j, c in enumerate(ring["conv_in"](n)):
                src = a["conv_w_in"][:, bass.ds((j % 2) * D + (2 * n + j // 2) * P, P)]
                load_chunk(sp, c, [(raw(c).rearrange("p (k n) -> p k n", k=KT), src.rearrange("(k p) n -> p k n", p=P))])
        for k, c in enumerate(ring["conv_out"]):
            load_chunk(sp, c, [(raw(c), a["conv_w_out"][tile_cols(k), :])])
        ffn_loads(sp, 1)
        for t in range(TT):
            sp.wait_ge(ln_done, 3 * TT + t + 1)
            sp.dma_start(a["out"][tile_cols(t), :], resid[:, t, :]).then_inc(out_done, 16)
        sp.wait_ge(out_done, 16 * TT)

    def ffn_pe(pe, layer):
        name = f"ffn{layer}"

        def gate(c, f):
            if not (isinstance(f, int) and f == 0):
                pe.wait_ge(silu_done[layer], f)
            feature_product(pe, c, 0)

        def up(c, f):
            if not (isinstance(f, int) and f == 0):
                pe.wait_ge(h_prod[layer], f)
            feature_product(pe, c, 2)

        def down(cs, group, turn=False):
            pe.wait_ge(h_lo[layer], 2 * group + 2)
            token_product(pe, name, cs, [(h_hi_t[:, j], h_lo_t[:, j]) for j in range(2)], group, turn)

        c = ring[name + "_first"]
        for f in range(2):
            gate(c[2 * f], f)
            up(c[2 * f + 1], f)

        def trip(n):
            c = ring[name](n)
            gate(c[0], 2 * n + 2)
            down(c[1:3], n)
            up(c[3], 2 * n + 2)
            gate(c[4], 2 * n + 3)
            up(c[5], 2 * n + 3)
        with pe.Fori(0, FG - 2) as n:
            trip(n)
        trip(FG - 2)
        down(ring[name + "_last"], FG - 1, turn=layer == 0)

    def attention_pe(pe):
        def logits(u, g, branch):
            i, kv = UNITS[u]
            piece = (u * G + g) * 2 + branch
            b = 2 * (piece % 2)
            if g == 0 and branch == 0:
                pe.wait_ge(qs_ok, u + 1)
            if piece >= 2:
                pe.wait_ge(s_min, 3 * ((piece - 2) // 2) + (1 if branch == 0 else 3))
            qh, ql = qs[:, u % 2, 0, g, :], qs[:, u % 2, 1, g, :]
            k0, nk = (0, (i + 1) * P) if branch == 0 else window(i)
            for c0 in range(0, nk, HALF):
                n = min(HALF, nk - c0)
                out, keys = ps[:, b + c0 // HALF, 0:n], ks[:, kv, branch, k0 + c0:k0 + c0 + n]
                far = branch == 1 and c0 == 0 and nk > WINDOW
                nc.tensor.matmul(out, qh, keys, start=True, stop=False)
                last = nc.tensor.matmul(out, ql, keys, start=False, stop=not far)
                if far:
                    nc.tensor.matmul(ps[:, b, 0:P], ident_b[:], far_mask[:], start=False, stop=True)
            if branch == 1:
                n = 8 * i + 8
                out = ps[:, b + 1, P:P + n]
                nc.tensor.matmul(out, qh, kc[:, kv, 0:n], start=True, stop=False)
                last = nc.tensor.matmul(out, ql, kc[:, kv, 0:n], start=False, stop=True)
            last.then_inc(s_done, 1)

        def turn(s):
            u, col, n, _, _ = STEPS[s]
            if s == STEPS_OF[u][0]:
                pe.wait_ge(p_norm, G * (u + 1))
            if s >= 2:
                pe.wait_ge(pt_act if s % 2 == 0 else pt_dve, s // 2)
            for g in range(G):
                last = nc.tensor.transpose(ps[0:n, 4 + s % 2, tile_cols(g)], probs[:, u % 2, g, col:col + n], ident[:])
            last.then_inc(pt_done, 1)

        def values(s):
            u, _, n, branch, j = STEPS[s]
            _, kv = UNITS[u]
            pe.wait_ge(pt_act if s % 2 == 0 else pt_dve, s // 2 + 1)
            if s == STEPS_OF[u][0] and u >= 2:
                pe.wait_ge(o_lo, 2 * (u - 1))
            c0 = (P if branch == "win" else 0) + kv * DH
            v = vc[0:n, kv, :] if branch == "cmp" else vg[:, j, c0:c0 + DH]
            rhs = probs_t[s % 2][0:n].rearrange("p g q -> p (g q)")
            nc.tensor.matmul(ps[0:DH, 6 + u % 2, :], v, rhs, start=(s == STEPS_OF[u][0]),
                             stop=(s == STEPS_OF[u][1] - 1)).then_inc(pv_done, 1)

        for what, u, n in attention_order():
            if what == "logits":
                logits(u, n, 0)
                logits(u, n, 1)
            elif what == "step":
                turn(n)
                if n:
                    values(n - 1)
        values(len(STEPS) - 1)

    def tensor_program(pe):
        pe.wait_ge(const_ok, 2)
        for t in range(TT):
            turn_tile(pe, 0, t)
        pe.wait_ge(par_in, 16 * PARAMS)
        for g in range(GROUPS):
            nc.tensor.transpose(ps[:, 4, tile_cols(g)], ws[:, g, :], ident[:]).then_inc(small_t, 1)
        nc.tensor.transpose(ps[:, 5, 0:40], rows[:], ident[0:40, 0:40]).then_inc(small_t, 1)
        nc.tensor.transpose(ps[:, 5, 64:128], pe_row[:], ident[0:64, 0:64]).then_inc(small_t, 1)
        third = BIAS_ROW // 3
        for n, out in enumerate((ps[0:HEADS, 6, 0:third], ps[0:HEADS, 7, 0:third], ps[0:HEADS, 5, P:P + third])):
            nc.tensor.matmul(out, rbias[:], onehot[:, n * third:(n + 1) * third], start=True, stop=True).then_inc(small_t, 1)
        pe.wait_ge(small_c, 6)
        c = ring["v"]
        pe.wait_ge(w_lo, c[3].number)
        pe.wait_ge(turned_lo, TT)
        for t in range(TT):
            if t >= 4:
                pe.wait_ge(v_gelu, t - 3)
            for k in range(KT):
                s, cut = c[k // 2].slot, slice((k % 2) * HALF, (k % 2 + 1) * HALF)
                xh, xl = xt_hi[:, k, tile_cols(t)], xt_lo[:, k, tile_cols(t)]
                out = ps[:, 4 + t % 4, :]
                nc.tensor.matmul(out, xh, wt_hi[:, s, cut], start=(k == 0), stop=False)
                nc.tensor.matmul(out, xh, wt_lo[:, s, cut], start=False, stop=False)
                last = nc.tensor.matmul(out, xl, wt_hi[:, s, cut], start=False, stop=(k == KT - 1))
                if t == TT - 1 and k % 2:
                    last.then_inc(w_used[s], 1)
            if t < TT - 1:
                last.then_inc(v_done, 1)
        c = ring["vg"]
        pe.wait_ge(w_lo, c[2].number)
        for t in range(TT):
            if t >= 4:
                pe.wait_ge(vg_out, t - 3)
            for k in range(KT):
                s, cut = c[k // 3].slot, slice((k % 3) * VG, (k % 3 + 1) * VG)
                xh, xl = xt_hi[:, k, tile_cols(t)], xt_lo[:, k, tile_cols(t)]
                out = ps[:, t % 4, 0:VG]
                nc.tensor.matmul(out, xh, wt_hi[:, s, cut], start=(k == 0), stop=False)
                nc.tensor.matmul(out, xh, wt_lo[:, s, cut], start=False, stop=False)
                last = nc.tensor.matmul(out, xl, wt_hi[:, s, cut], start=False, stop=(k == KT - 1))
                if t == TT - 1 and k in (2, 5, 7):
                    last.then_inc(w_used[s], 1)
            if t < TT - 1:
                last.then_inc(vg_done, 1)

        def features(n):
            if n == 0:
                pe.wait_ge(vg_out, TT)
            if n >= 2:
                pe.wait_ge(feat_act, n - 1)
            if n in (4, 5):
                pe.wait_ge(feat_dve, n - 3)
            feature_product(pe, ring["feat"][n], 2 * (n % 2))
        features(0)
        features(1)
        pe.wait_ge(v_norm, TT)
        pe.wait_ge(ws_ok, 1)
        for g in range(GROUPS):
            for h in range(2):
                n = 2 * g + h
                if n >= 4:
                    pe.wait_ge(mix_add, n - 3)
                for m in range(4):
                    last = nc.tensor.matmul(ps[:, 4 + n % 4, tile_cols(m)], v_tok[:, 4 * h + m, tile_cols(g)],
                                            ws_t[:, g, :], start=True, stop=True)
                last.then_inc(mix_done, 1)
        for n in range(2, len(FEATURE_COLS)):
            features(n)
        pe.wait_ge(w1_in, 64)
        pe.wait_ge(feat_act, len(FEATURE_COLS))
        for kv in range(2):
            for h in range(KV_HEADS):
                part = slice(h * DH, (h + 1) * DH)
                for j in range(CMP_BLOCK):
                    nc.tensor.matmul(ps[part, kv, 0:N_CMP], w1[part, kv, j, :],
                                     cr[part, kv, j:j + CMP_STRIDE * (N_CMP - 1) + 1:CMP_STRIDE],
                                     start=(j == 0), stop=(j == CMP_BLOCK - 1))
                for j in range(CMP_BLOCK):
                    last = nc.tensor.matmul(ps[part, 2 + kv, 0:1], w1[part, kv, j, :], pe_col[part, kv, j:j + 1],
                                            start=(j == 0), stop=(j == CMP_BLOCK - 1))
            last.then_inc(cmp_done, 1)
        pe.wait_ge(cmp_act, 4)
        for h in range(KV_HEADS):
            part = slice(h * DH, (h + 1) * DH)
            nc.tensor.matmul(ps[part, 4, 0:64], w2[part, 0, :], hid[part, 0, :], start=True, stop=True)
            last = nc.tensor.matmul(ps[0:64, 5 + h, 0:DH], hid[part, 1, :], w2[part, 1, :], start=True, stop=True)
        last.then_inc(cmp_done, 1)
        pe.wait_ge(cmp_act, 6)
        pe.wait_ge(cmp_dve, 4)
        attention_pe(pe)
        pe.wait_ge(o_lo, 2 * len(UNITS))
        pe.wait_ge(a_lo, GROUPS)

        def out_product(name):
            for n in range(GROUP_COUNT[name]):
                token_product(pe, name, ring[name][2 * n:2 * n + 2],
                              [(xt_hi[:, k], xt_lo[:, k]) for k in (2 * n, 2 * n + 1)], n,
                              turn=n == GROUP_COUNT[name] - 1)
        pe.wait_ge(tap_in, 16)
        for k in range(KT):
            last = nc.tensor.transpose(ps[:, 0, k * 32:k * 32 + CONV_W], tap_rows[:, tile_cols(k)], ident[0:CONV_W, 0:CONV_W])
        last.then_inc(tap_t, 1)
        out_product("w_out")
        ffn_pe(pe, 0)
        conv = ring["conv_in"]
        with pe.Fori(0, KT // 2) as n:
            c = conv(n)
            for j in range(4):
                if j % 2 == 0:
                    pe.wait_ge(glu_free, 2 * n + (j // 2 + 1))
                feature_product(pe, c[j], 2 * j)
        pe.wait_ge(ones_ok, 1)
        for k in range(KT):
            for h in range(2):
                last = nc.tensor.matmul(ps[:, h, :], ones_m[:], acc[:, k, h * HALF:(h + 1) * HALF],
                                        start=(k == 0), stop=(k == KT - 1))
        last.then_inc(mean_ok, 1)
        for k in range(KT):
            pe.wait_ge(sq_ok, k + 1)
            for h in range(2):
                last = nc.tensor.matmul(ps[:, 2 + h, :], ones_m[:], square[:, h * HALF:(h + 1) * HALF],
                                        start=(k == 0), stop=(k == KT - 1))
            last.then_inc(sq_used, 1)
        pe.wait_ge(act_lo, KT)
        out_product("conv_out")
        ffn_pe(pe, 1)

    def ffn_act(act, layer):
        name = f"ffn{layer}"

        def silu(c, f):
            act.wait_ge(w_used[c.slot], c.used)
            if not (isinstance(f, int) and f == 0):
                act.wait_ge(h_prod[layer], f)
            nc.scalar.activation(gate_act[:], banks(0), ACT.Silu).then_inc(silu_done[layer], 1)

        def hi(f, j):
            act.wait_ge(h_prod[layer], f + 1)
            nc.scalar.copy(h_hi_t[:, j, :], h_f[:]).then_inc(h_hi[layer], 1)

        c = ring[name + "_first"]
        silu(c[0], 0)
        split_hi(act, ring[name](0)[0])
        hi(0, 0)
        silu(c[2], 1)
        hi(1, 1)

        def trip(n, more):
            c = ring[name](n)
            for j in (1, 2, 3):
                split_hi(act, c[j])
            silu(c[0], 2 * n + 2)
            split_hi(act, c[4])
            hi(2 * n + 2, 0)
            split_hi(act, c[5])
            silu(c[4], 2 * n + 3)
            if more:
                split_hi(act, ring[name](n + 1)[0])
            hi(2 * n + 3, 1)
        with act.Fori(0, FG - 2) as n:
            trip(n, True)
        trip(FG - 2, False)
        for c in ring[name + "_last"]:
            split_hi(act, c)

    def attention_act(act):
        for what, u, n in attention_order():
            i, kv = UNITS[u]
            if what == "logits":
                k0, nk = window(i)
                pr = probs[:, u % 2, n]
                for b, part in ((1, pr[:, 0:(i + 1) * P]), (2, pr[:, WIN0:WIN0 + nk]),
                                (0, pr[:, CMP0:CMP0 + min(N_CMP, 8 * i + 7)])):
                    act.wait_ge(s_min, 3 * (u * G + n) + {1: 1, 2: 2, 0: 3}[b])
                    nc.scalar.activation(part, part, ACT.Exp, bias=low[:, u % 2, n, b:b + 1], scale=-1.0,
                                         accum_out=den[:, u % 2, n, b:b + 1]).then_inc(p_exp, 1)
            elif what == "step" and n % 2 == 0:
                keys = STEPS[n][2]
                act.wait_ge(pt_done, n + 1)
                if n >= 2:
                    act.wait_ge(pv_done, n - 1)
                nc.scalar.copy(probs_t[0][0:keys].rearrange("p g q -> p (g q)"), ps[0:keys, 4, :]).then_inc(pt_act, 1)
            elif what == "out":
                act.wait_ge(pv_done, STEPS_OF[u][1])
                out = ps[0:DH, 6 + u % 2, :].rearrange("p (t r q) -> p r t q", r=2, q=P)
                for r in range(2):
                    nc.scalar.copy(xt_hi[r * DH:(r + 1) * DH, 4 + 2 * kv:6 + 2 * kv, tile_cols(i)], out[:, r]).then_inc(o_hi, 1)

    def scalar_program(act):
        load_small(act)
        for t in range(TT):
            turn_hi(act, 0, t)
        for c in ring["v"] + ring["vg"][:2]:
            split_hi(act, c)
        act.wait_ge(small_c, 6)
        act.dma_start(a["bias_scratch"], bias_row[:].unsqueeze(1).broadcast_to([HEADS, P, BIAS_ROW])).then_inc(bias_out, 16)
        for t in range(TT):
            if t < TT - 1:
                act.wait_ge(v_done, t + 1)
            else:
                act.wait_ge(w_used[ring["v"][3].slot], ring["v"][3].used)
            nc.scalar.activation(v_tok[:, t, :], ps[:, 4 + t % 4, :], ACT.Gelu_apprx_tanh).then_inc(v_gelu, 1)
        feat = ring["feat"]
        for c in [ring["vg"][2]] + feat[:3]:
            split_hi(act, c)
        act.wait_ge(v_mv, TT)
        nc.scalar.activation(v_rstd[:], v_mean[:, :, 1], ACT.Sqrt, bias=eps_c[:, 0:1]).then_inc(v_sd, 1)
        for c in feat[3:6]:
            split_hi(act, c)
        for n, c in enumerate(feat):
            act.wait_ge(w_used[c.slot], c.used)
            got = banks(2 * (n % 2))
            if n < 2:
                last = nc.scalar.copy(cr[:, n, :], got)
            elif n < F_U:
                for kv in range(KV_HEADS):
                    last = nc.scalar.copy(ks[0:DH, kv, n - 2, :], got[kv * DH:(kv + 1) * DH, :])
            elif n < F_Q:
                if n > F_U:
                    act.wait_ge(u_mul, n - F_U)
                last = nc.scalar.activation(u_act[:], got, ACT.Gelu_apprx_tanh)
            else:
                if n == F_Q:
                    act.wait_ge(u_mul, GROUPS)
                last = nc.scalar.mul(q_t[:, n - F_Q, :], got, -SCALE)
            last.then_inc(feat_act, 1)
            if n + 6 < len(feat):
                split_hi(act, feat[n + 6])
        for g in range(GROUPS):
            nc.scalar.copy(xt_hi[:, g, :], mix_a[:, g, :]).then_inc(a_hi, 1)
        for kv in range(2):
            act.wait_ge(cmp_done, kv + 1)
            nc.scalar.copy(pe_bias[:, kv:kv + 1], ps[:, 2 + kv, 0:1]).then_inc(cmp_act, 1)
            act.wait_ge(cmp_act, 2 * kv + 1)
            nc.scalar.activation(hid[:, kv, 0:N_CMP], ps[:, kv, 0:N_CMP], ACT.Gelu_apprx_tanh,
                                 bias=pe_bias[:, kv:kv + 1]).then_inc(cmp_act, 1)
        act.wait_ge(cmp_done, 3)
        for kv in range(KV_HEADS):
            nc.scalar.copy(kc[0:DH, kv, :], ps[kv * DH:(kv + 1) * DH, 4, 0:64]).then_inc(cmp_act, 1)
        act.wait_ge(vg_out, TT)
        gates = vg[:, :, 2 * P:VG]
        nc.scalar.activation(gates, gates, ACT.Sigmoid).then_inc(gates_ok, 1)
        attention_act(act)

        def out_act(name, done, following):
            cs = ring[name]
            for k in range(KT):
                if done <= k < 6:
                    split_hi(act, cs[k])
                if name == "w_out":
                    act.wait_ge(x_in[k], 32)
                    scale_tile(act, k)
            for c in cs[6:] + following:
                split_hi(act, c)

        act.wait_ge(pt_done, len(STEPS))
        out_act("w_out", 0, ring["ffn0_first"])
        norm_act(act, "w_out")
        ffn_act(act, 0)
        for c in ring["conv_in"](0):
            split_hi(act, c)
        norm_act(act, "ffn0")

        def conv_trip(n, more):
            c, nxt = ring["conv_in"](n), ring["conv_in"](n + 1) if more else None
            for j in range(2):
                act.wait_ge(w_used[c[2 * j + 1].slot], c[2 * j + 1].used)
                act.wait_ge(glu_free, 2 * n + (j + 2))
                act.nop()
                nc.scalar.activation(glu_g[:], banks(4 * j + 2), ACT.Sigmoid,
                                     bias=cols[:, bass.ds(2 * n + (KT + j), 1)]).then_inc(glu_sig, 1)
                if more:
                    split_hi(act, nxt[2 * j])
                    split_hi(act, nxt[2 * j + 1])
        with act.Fori(0, KT // 2 - 1) as n:
            conv_trip(n, True)
        conv_trip(KT // 2 - 1, False)
        for c in ring["conv_out"][:6]:
            split_hi(act, c)
        for k in range(KT):
            act.wait_ge(cen, k + 1)
            if k:
                act.wait_ge(sq_used, k)
            nc.scalar.activation(square[:], acc[:, k, :], ACT.Square).then_inc(sq_ok, 1)
        act.wait_ge(sq_used, KT)
        act.wait_ge(outb_ok, TT)
        nc.scalar.activation(conv_rs[:], banks(2), ACT.Sqrt, bias=eps_c[:, 0:1]).then_inc(var_sd, 1)
        for k in range(KT):
            act.wait_ge(nrm, k + 1)
            nc.scalar.activation(acc[:, k, :], acc[:, k, :], ACT.Silu, scale=cols[:, 3 * KT + k:3 * KT + k + 1],
                                 bias=cols[:, 4 * KT + k:4 * KT + k + 1]).then_inc(act_ok, 1)
            act.wait_ge(act_ok, k + 1)
            nc.scalar.copy(xt_hi[:, k, :], acc[:, k, :]).then_inc(act_hi, 1)
        out_act("conv_out", 6, ring["ffn1_first"])
        norm_act(act, "conv_out")
        ffn_act(act, 1)
        norm_act(act, "ffn1", turn=False)

    def ffn_dve(dve, layer):
        name = f"ffn{layer}"

        def prod(c, f):
            dve.wait_ge(w_used[c.slot], c.used)
            dve.wait_ge(silu_done[layer], f + 1)
            if not (isinstance(f, int) and f == 0):
                dve.wait_ge(h_lo[layer], f)
            nc.vector.tensor_tensor(h_f[:], banks(2), gate_act[:], ALU.mult).then_inc(h_prod[layer], 1)

        def lo(f, j):
            dve.wait_ge(h_hi[layer], f + 1)
            nc.vector.tensor_tensor(h_lo_t[:, j, :], h_f[:], h_hi_t[:, j, :], ALU.subtract).then_inc(h_lo[layer], 1)

        dve.sem_inc(y_free[name], 4)
        c = ring[name + "_first"]
        split_lo(dve, ring[name](0)[0])
        for f in range(2):
            prod(c[2 * f + 1], f)
            lo(f, f)
        dve.wait_ge(scaled, TT * NORM_OF[name])

        def trip(n, more):
            c = ring[name](n)
            for j in (1, 2, 3):
                split_lo(dve, c[j])
            for q in range(16):
                add_bank(dve, name, c[2], n, q)
            split_lo(dve, c[4])
            prod(c[3], 2 * n + 2)
            lo(2 * n + 2, 0)
            split_lo(dve, c[5])
            if more:
                split_lo(dve, ring[name](n + 1)[0])
            prod(c[5], 2 * n + 3)
            lo(2 * n + 3, 1)
        with dve.Fori(0, FG - 2) as n:
            trip(n, True)
        trip(FG - 2, False)
        for c in ring[name + "_last"]:
            split_lo(dve, c)

    def attention_dve(dve):
        for what, u, n in attention_order():
            i, kv = UNITS[u]
            par = u % 2
            if what == "logits":
                g, h = n, kv * G + n
                k0, nk = window(i)
                nc_ = min(N_CMP, 8 * i + 7)
                if g == 0 and u >= 2:
                    dve.wait_ge(pt_done, STEPS_OF[u - 2][1])
                if i == 0 and g == 0:
                    dve.wait_ge(nb_ok, kv + 1)
                pr = probs[:, par, g]
                for branch in range(2):
                    piece = (u * G + g) * 2 + branch
                    b = 2 * (piece % 2)
                    dve.wait_ge(s_done, piece + 1)
                    s = banks(b)
                    todo = [(1, pr[:, 0:(i + 1) * P], s[:, 0:(i + 1) * P], nbias[:, h, SEQ - (i + 1) * P:SEQ])]
                    if branch:
                        c0 = SEQ - P - P * i + CMP_BLOCK - 1
                        todo = [(2, pr[:, WIN0:WIN0 + nk], s[:, 0:nk], nbias[:, h, SEQ - nk:SEQ]),
                                (0, pr[:, CMP0:CMP0 + nc_], s[:, HALF + P:HALF + P + nc_],
                                 nbias[:, h, c0:c0 + CMP_STRIDE * (nc_ - 1) + 1:CMP_STRIDE])]
                    for col, out, logit, bias in todo:
                        nc.vector.tensor_tensor_reduce(out, logit, bias, 1.0, 3.0e38, ALU.add, ALU.min,
                                                       low[:, par, g, col:col + 1]).then_inc(s_min, 1)
            elif what == "norm":
                g, h = n, kv * G + n
                k0, nk = window(i)
                nc_ = min(N_CMP, 8 * i + 7)
                r = inv[:, par, g, :]
                dve.wait_ge(p_exp, 3 * (u * G + g) + 3)
                v_wait(dve, nc.vector.reciprocal(r, den[:, par, g, :]))
                if u == 0 and g == 0:
                    dve.wait_ge(gates_ok, 1)
                v_wait(dve, nc.vector.tensor_tensor(r, r, vg[:, i, 2 * P + 3 * h:2 * P + 3 * h + 3], ALU.mult))
                if i == 0:
                    v_wait(dve, nc.vector.tensor_tensor(r[:, 0:1], r[:, 0:1], row_ok[:], ALU.mult))
                pr = probs[:, par, g]
                for col, part in ((1, pr[:, 0:(i + 1) * P]), (2, pr[:, WIN0:WIN0 + nk]), (0, pr[:, CMP0:CMP0 + nc_])):
                    last = nc.vector.tensor_scalar(part, part, r[:, col:col + 1], None, ALU.mult)
                last.then_inc(p_norm, 1)
            elif what == "step" and n % 2 == 1:
                keys = STEPS[n][2]
                dve.wait_ge(pt_done, n + 1)
                if n >= 2:
                    dve.wait_ge(pv_done, n - 1)
                nc.vector.tensor_copy(probs_t[1][0:keys].rearrange("p g q -> p (g q)"), ps[0:keys, 5, :]).then_inc(pt_dve, 1)
            elif what == "out":
                out = ps[0:DH, 6 + par, :].rearrange("p (t r q) -> p r t q", r=2, q=P)
                for r in range(2):
                    dve.wait_ge(o_hi, 2 * u + 2)
                    to = (slice(r * DH, (r + 1) * DH), slice(4 + 2 * kv, 6 + 2 * kv), tile_cols(i))
                    nc.vector.tensor_tensor(xt_lo[to], out[:, r], xt_hi[to], ALU.subtract).then_inc(o_lo, 1)

    def vector_program(dve):
        for t in range(TT):
            turn_lo(dve, 0, t)
        third = BIAS_ROW // 3
        dve.wait_ge(small_t, 4)
        nc.vector.tensor_copy(ws_t[:].rearrange("p g t -> p (g t)"), ps[:, 4, :]).then_inc(small_c, 1)
        dve.wait_ge(small_t, 9)
        nc.vector.tensor_copy(cols[:], ps[:, 5, 0:40]).then_inc(small_c, 1)
        nc.vector.tensor_copy(pe_col[:].rearrange("p k j -> p (k j)"), ps[:, 5, 64:128]).then_inc(small_c, 1)
        for n, src in enumerate((ps[0:HEADS, 6, 0:third], ps[0:HEADS, 7, 0:third], ps[0:HEADS, 5, P:P + third])):
            nc.vector.tensor_scalar(bias_row[:, n * third:(n + 1) * third], src, -1.0, None, ALU.mult).then_inc(small_c, 1)
        for c in ring["v"] + ring["vg"][:2]:
            split_lo(dve, c)
        for t in range(TT):
            dve.wait_ge(v_gelu, t + 1)
            v_wait(dve, nc.vector.bn_stats(v_stats[:, t, :], v_tok[:, t, :]))
            nc.vector.bn_aggr(v_mean[:, t, :], v_stats[:, t, :]).then_inc(v_mv, 1)
        feat = ring["feat"]
        for c in [ring["vg"][2]] + feat[:3]:
            split_lo(dve, c)
        dve.wait_ge(v_sd, 1)
        v_wait(dve, nc.vector.reciprocal(v_rstd[:], v_rstd[:]))
        for t in range(TT):
            x = v_tok[:, t, :]
            v_wait(dve, nc.vector.tensor_scalar(x, x, v_mean[:, t, 0:1], v_rstd[:, t:t + 1], ALU.subtract, ALU.mult))
            v_wait(dve, nc.vector.tensor_tensor(x, x, gmlp_g[:], ALU.mult))
            nc.vector.tensor_tensor(x, x, gmlp_b[:], ALU.add).then_inc(v_norm, 1)
        dve.wait_ge(bias_out, 16)
        for t in range(TT):
            if t < TT - 1:
                dve.wait_ge(vg_done, t + 1)
            else:
                dve.wait_ge(w_used[ring["vg"][2].slot], ring["vg"][2].used)
            nc.vector.tensor_copy(vg[:, t, :], ps[:, t % 4, 0:VG]).then_inc(vg_out, 1)
        for c in feat[3:8]:
            split_lo(dve, c)
        for g in range(GROUPS):
            for h in range(2):
                n = 2 * g + h
                dve.wait_ge(mix_done, n + 1)
                nc.vector.tensor_tensor(mix_a[:, g, h * HALF:(h + 1) * HALF].rearrange("p (m t) -> p m t", t=P),
                                        ps[:, 4 + n % 4, :].rearrange("p (m t) -> p m t", t=P),
                                        gmlp_bs[:, g:g + 1, :].broadcast_to([P, 4, P]), ALU.add).then_inc(mix_add, 1)
        for n in range(2, F_Q):
            dve.wait_ge(feat_act, n + 1)
            if n < F_U:
                for kv in range(KV_HEADS):
                    last = nc.vector.tensor_tensor(ks[DH:P, kv, n - 2, :], banks(2 * (n % 2))[kv * DH:(kv + 1) * DH, :],
                                                   ks[0:DH, kv, n - 2, :], ALU.subtract)
                last.then_inc(feat_dve, 1)
            else:
                x = mix_a[:, n - F_U, :]
                if n == F_U:
                    dve.wait_ge(mix_add, 2 * GROUPS)
                nc.vector.tensor_tensor(x, x, u_act[:], ALU.mult).then_inc(u_mul, 1)
            if n + 6 < len(feat):
                split_lo(dve, feat[n + 6])
        for g in range(GROUPS):
            dve.wait_ge(a_hi, g + 1)
            nc.vector.tensor_tensor(xt_lo[:, g, :], mix_a[:, g, :], xt_hi[:, g, :], ALU.subtract).then_inc(a_lo, 1)
        for kv in range(KV_HEADS):
            dve.wait_ge(cmp_act, 5 + kv)
            nc.vector.tensor_tensor(kc[DH:P, kv, :], ps[kv * DH:(kv + 1) * DH, 4, 0:64], kc[0:DH, kv, :],
                                    ALU.subtract).then_inc(cmp_dve, 1)
        for kv in range(KV_HEADS):
            nc.vector.tensor_copy(vc[:, kv, :], ps[0:64, 5 + kv, 0:DH]).then_inc(cmp_dve, 1)
        attention_dve(dve)
        dve.wait_ge(tap_t, 1)
        nc.vector.tensor_copy(taps[:], ps[:, 0, 0:KT * 32].rearrange("p (k j) -> p k j", j=32)[:, :, 0:CONV_W]).then_inc(tap_ok, 1)

        def out_dve(name, done, following):
            cs = ring[name]
            dve.sem_inc(y_free[name], 4)
            for c in cs[done:2]:
                split_lo(dve, c)
            for t in range(TT):
                if name == "w_out":
                    dve.wait_ge(scaled, t + 1)
                elif t == 0:
                    dve.wait_ge(outb_ok, TT)
                for h in range(2):
                    add_bank(dve, name, cs[1], 0, 2 * t + h)
                if max(2, done) <= t + 2 < 6:
                    split_lo(dve, cs[t + 2])
            for n in (1, 2):
                for c in (cs[6:] if n == 1 else following[:2]):
                    split_lo(dve, c)
                for q in range(16):
                    add_bank(dve, name, cs[2 * n + 1], n, q)
            for c in following[2:]:
                split_lo(dve, c)
            norm_dve(dve, name, cs[7])

        out_dve("w_out", 0, ring["ffn0_first"])
        ffn_dve(dve, 0)
        for c in ring["conv_in"](0):
            split_lo(dve, c)
        norm_dve(dve, "ffn0", ring["ffn0_last"][1])
        dve.sem_inc(glu_free, 2)
        dve.wait_ge(pad_ok, 2)

        def tap(n, m, j):
            out, x = acc[:, bass.ds(2 * n + m, 1), :], conv_x[:, m:m + 1, j:j + SEQ]
            w = taps[:, bass.ds(2 * n + m, 1), j]
            if j == 0:
                nc.vector.tensor_scalar(out, x, w, cols[:, bass.ds(2 * n + (2 * KT + m), 1)], ALU.mult, ALU.add).then_inc(conv_v, 1)
            else:
                nc.vector.scalar_tensor_tensor(out=out, in0=x, scalar=w, in1=out, op0=ALU.mult, op1=ALU.add).then_inc(conv_v, 1)
            dve.wait_ge(conv_v, 2 * CONV_W * n + (CONV_W * m + j + 1))

        def conv_trip(n, more):
            c, nxt = ring["conv_in"](n), ring["conv_in"](n + 1) if more else None
            for j in range(2):
                dve.wait_ge(glu_sig, 2 * n + (j + 1))
                nc.vector.scalar_tensor_tensor(out=conv_x[:, j, PAD:], in0=banks(4 * j),
                                               scalar=cols[:, bass.ds(2 * n + j, 1)], in1=glu_g[:],
                                               op0=ALU.add, op1=ALU.mult).then_inc(glu_free, 1)
                if more:
                    split_lo(dve, nxt[2 * j])
                    split_lo(dve, nxt[2 * j + 1])
                dve.wait_ge(glu_free, 2 * n + (j + 3))
                for m in range(CONV_W):
                    tap(n, j, m)
        with dve.Fori(0, KT // 2 - 1) as n:
            conv_trip(n, True)
        conv_trip(KT // 2 - 1, False)
        for c in ring["conv_out"][:6]:
            split_lo(dve, c)
        dve.wait_ge(mean_ok, 1)
        for k in range(KT):
            nc.vector.tensor_tensor(acc[:, k, :], acc[:, k, :], banks(0), ALU.subtract).then_inc(cen, 1)
        dve.wait_ge(var_sd, 1)
        v_wait(dve, nc.vector.reciprocal(conv_rs[:], conv_rs[:]))
        for k in range(KT + 1):
            if k < KT:
                nc.vector.tensor_tensor(acc[:, k, :], acc[:, k, :], conv_rs[:], ALU.mult).then_inc(nrm, 1)
            if k:
                dve.wait_ge(act_hi, k)
                nc.vector.tensor_tensor(xt_lo[:, k - 1, :], acc[:, k - 1, :], xt_hi[:, k - 1, :], ALU.subtract).then_inc(act_lo, 1)
        out_dve("conv_out", 6, ring["ffn1_first"])
        ffn_dve(dve, 1)
        norm_dve(dve, "ffn1", ring["ffn1_last"][1], turn=False)

    def pool_program(pool):
        steps = [0]

        def g_wait(ins):
            ins.then_inc(g_step, 1)
            steps[0] += 1
            pool.wait_ge(g_step, steps[0])

        g_wait(nc.gpsimd.memset(ident[:], 0.0))
        nc.gpsimd.affine_select(out=ident[:], in_=ident[:], compare_op=ALU.not_equal, fill=1.0, base=0,
                                pattern=[[-1, P]], channel_multiplier=1).then_inc(const_ok, 1)
        pool.wait_ge(const_ok, 1)
        nc.gpsimd.memset(eps_c[:], EPS).then_inc(const_ok, 1)
        pool.wait_ge(const_ok, 2)
        g_wait(nc.gpsimd.tensor_copy(ident_b[:], ident[:]))
        g_wait(nc.gpsimd.memset(far_mask[:], 0.0))
        g_wait(nc.gpsimd.affine_select(out=far_mask[:], in_=far_mask[:], compare_op=ALU.is_ge, fill=BIG, base=-1,
                                       pattern=[[1, P]], channel_multiplier=-1))
        g_wait(nc.gpsimd.memset(row_ok[:], 1.0))
        g_wait(nc.gpsimd.affine_select(out=row_ok[:], in_=row_ok[:], compare_op=ALU.is_ge, fill=0.0,
                                       base=1 - CMP_BLOCK, pattern=[[0, 1]], channel_multiplier=1))
        g_wait(nc.gpsimd.memset(hid[:], 0.0))
        pool.wait_ge(small_c, 1)
        nc.gpsimd.affine_select(out=ws_t[:], in_=ws_t[:], compare_op=ALU.is_ge, fill=0.0, base=0,
                                pattern=[[0, GROUPS], [1, P]], channel_multiplier=-1).then_inc(ws_ok, 1)
        pool.wait_ge(ws_ok, 1)

        def causal(kv):
            pool.wait_ge(nb_in[kv], 16)
            x = nbias[:, kv * G:(kv + 1) * G, SEQ - P:]
            nc.gpsimd.affine_select(out=x, in_=x, compare_op=ALU.is_ge, fill=BIG, base=0,
                                    pattern=[[0, G], [-1, P]], channel_multiplier=1).then_inc(nb_ok, 1)
            pool.wait_ge(nb_ok, kv + 1)

        causal(0)
        pool.wait_ge(cmp_done, 2)
        pool.wait_ge(feat_act, len(FEATURE_COLS))
        for u, (i, kv) in enumerate(UNITS):
            if u >= 2:
                pool.wait_ge(s_done, 2 * G * (u - 1))
            for r in range(2):
                src = q_t[r * DH:(r + 1) * DH, 2 * kv:2 * kv + 2, tile_cols(i)]
                dst = qs[:, u % 2].rearrange("p l (t r) q -> p l r t q", r=2)
                for half in range(2):
                    g_wait(nc.gpsimd.tensor_copy(dst[half * DH:(half + 1) * DH, 0, r], src))
                for half in range(2):
                    ins = nc.gpsimd.tensor_tensor(dst[half * DH:(half + 1) * DH, 1, r], src,
                                                  dst[r * DH:(r + 1) * DH, 0, r], ALU.subtract)
                    if r and half:
                        ins.then_inc(qs_ok, 1)
                        pool.wait_ge(qs_ok, u + 1)
                    else:
                        g_wait(ins)
            if u == 0:
                causal(1)
        pool.wait_ge(ln_done, 2 * TT)
        nc.gpsimd.memset(conv_x[:, 0, 0:PAD], 0.0).then_inc(pad_ok, 1)
        pool.wait_ge(pad_ok, 1)
        nc.gpsimd.memset(conv_x[:, 1, 0:PAD], 0.0).then_inc(pad_ok, 1)
        pool.wait_ge(pad_ok, 2)
        pool.wait_ge(outb_in, 16)
        for t in range(TT):
            pool.wait_ge(scaled, 2 * TT + t + 1)
            nc.gpsimd.tensor_tensor(resid[:, t, :], resid[:, t, :], out_b[:], ALU.add).then_inc(outb_ok, 1)
            pool.wait_ge(outb_ok, t + 1)
        pool.wait_ge(conv_v, CONV_W * KT)
        nc.gpsimd.memset(ones_m[:], 1.0 / D).then_inc(ones_ok, 1)

    with nc.Block() as block:
        @block.sync
        def _(sp):
            sync_program(sp)

        @block.scalar
        def _(act):
            scalar_program(act)

        @block.vector
        def _(dve):
            vector_program(dve)

        @block.tensor
        def _(pe):
            tensor_program(pe)

        @block.gpsimd
        def _(pool):
            pool_program(pool)


def bucket_onehot():
    n = np.maximum(np.arange(SEQ - 1, SEQ - 1 - BIAS_ROW, -1), 0)
    exact = N_BUCKETS // 2
    nf = np.maximum(n, 1).astype(np.float32)
    ratio = np.log(nf / np.float32(exact)) / np.float32(np.log(MAX_DISTANCE / exact))
    large = np.minimum(exact + (ratio * np.float32(N_BUCKETS - exact)).astype(np.int32), N_BUCKETS - 1)
    bucket = np.where(n < exact, n, large)
    return (bucket[None, :] == np.arange(N_BUCKETS)[:, None]).astype(np.float32)


def kernel(**inputs):
    import concourse.bacc as bacc
    from concourse.bass_utils import run_bass_kernel_spmd

    nc = bacc.Bacc("TRN2", target_bir_lowering=False, num_devices=1)
    arrays, aps = {}, {}
    for name, x in {**inputs, "bucket_onehot": bucket_onehot()}.items():
        x = np.ascontiguousarray(x)
        if x.shape[0] == 1:
            x = x.reshape(x.shape[1:])
        arrays[f"in_{name}"] = x
        aps[name] = nc.dram_tensor(f"in_{name}", x.shape, mybir.dt.from_np(x.dtype), kind="ExternalInput").ap()
    aps["out"] = nc.dram_tensor("out_y", [SEQ, D], F32, kind="ExternalOutput").ap()
    aps["bias_scratch"] = nc.dram_tensor("bias_scratch", [HEADS, P, BIAS_ROW], F32, kind="Internal").ap()
    build(nc, aps)
    result = run_bass_kernel_spmd(nc, [arrays], core_ids=[0])
    return result.results[0]["out_y"].reshape(1, SEQ, D)
```

```python
from contextlib import ExitStack

import numpy as np

import concourse.bass as bass
import concourse.mybir as mybir
from concourse.alu_op_type import AluOpType as ALU

F32 = mybir.dt.float32
F32R = mybir.dt.float32r
BF16 = mybir.dt.bfloat16
ACT = mybir.ActivationFunctionType

P = 128
D = 1024
SEQ = 1024
KT = D // P
TT = SEQ // P
HALF = 512
DEPTH = 2
ALPHA = float((2 * DEPTH) ** 0.25)
EPS = 1e-5

A_WIDTH = D // 2
GROUPS = 4
HEADS = 8
KV_HEADS = 2
G = HEADS // KV_HEADS
DH = 64
SCALE = DH ** -0.5
CMP_STRIDE = 16
CMP_BLOCK = 32
N_CMP = SEQ // CMP_STRIDE - 1
WINDOW = 512
N_BUCKETS = 32
MAX_DISTANCE = 1024
BIG = 1.0e30

KV0 = 2 * A_WIDTH + HEADS * DH
COL_KCMP, COL_VCMP, COL_KSLC, COL_VSLC, COL_KWIN, COL_VWIN = (KV0 + P * n for n in range(6))
COL_Q = 2 * A_WIDTH
GATES = 3 * HEADS
VG = 2 * P + GATES

FFN = 2816
FT = FFN // P
FG = FT // 2
CONV_W = 31
PAD = CONV_W - 1
PE_TAPS = 7
DVE_TAPS = CONV_W - PE_TAPS

RING = 6
RAWS = 2
V_SPLITS = [2, 3, 6, 7]
BIAS_ROW = 1152
FEATURE_COLS = [COL_KCMP, COL_VCMP, COL_KSLC, COL_KWIN] + [n * P for n in range(GROUPS)] + [
    COL_Q + n * P for n in range(4)]
F_U, F_Q = 4, 8


class Chunk:

    def __init__(self, slot, raw, number, landed, before):
        self.slot, self.raw, self.number, self.landed, self.before = slot, raw, number, landed, before
        self.used = before + 1


class Stream:

    def __init__(self):
        self.count, self.uses, self.landed = 0, [0] * RING, [0] * RAWS

    def take(self, slots, dmas=1):
        out = []
        for slot in slots:
            raw = (self.count + 1) % RAWS
            self.landed[raw] += 16 * dmas
            self.count += 1
            out.append(Chunk(slot, raw, self.count, self.landed[raw], self.uses[slot]))
            self.uses[slot] += 1
        return out

    def loop(self, slots, trips):
        first = self.take(slots)
        for _ in range(trips - 1):
            self.take(slots)
        per = len(slots)
        assert per % RAWS == 0 and len(set(slots)) == per

        def trip(n):
            return [Chunk(c.slot, c.raw, per * n + c.number, (16 * per // RAWS) * n + c.landed, n + c.before)
                    for c in first]
        return trip


def plan():
    s = Stream()
    tail = [4, 5, 0, 1, 2, 3, 4, 5]
    r = {"v": s.take([0, 1, 2, 3]), "vg": s.take([4, 5, 0], 2), "feat": s.take([(1 + n) % RING for n in range(12)])}
    r["w_out"] = s.take(tail)
    for layer in range(DEPTH):
        if layer == 1:
            r["conv_in"] = s.loop([0, 1, 2, 3], KT // 2)
            r["conv_out"] = s.take(tail)
        r[f"ffn{layer}_first"] = s.take([0, 1, 2, 3])
        r[f"ffn{layer}"] = s.loop([0, 4, 5, 1, 2, 3], FG - 1)
        r[f"ffn{layer}_last"] = s.take([4, 5])
    return r


GROUP_COUNT = {"w_out": KT // 2, "ffn0": FG, "conv_out": KT // 2, "ffn1": FG}
NORM_OF = {"w_out": 1, "ffn0": 2, "conv_out": 3, "ffn1": 4}


UNITS = [(i, kv) for kv in range(KV_HEADS) for i in range(TT)]


def window(i):
    return max(0, i - WINDOW // P) * P, min(WINDOW // P + 1, i + 1) * P


LAG = 2
BUFS = LAG + 1
LEAD = 3


def key_tiles():
    steps, of = [], []
    for u, (i, _) in enumerate(UNITS):
        first = len(steps)
        steps += [(u, j * P, P, "sel", j) for j in range(i + 1)]
        k0, nk = window(i)
        steps += [(u, SEQ + j * P, P, "win", k0 // P + j) for j in range(nk // P)]
        steps.append((u, SEQ + WINDOW + P, min(N_CMP, 8 * i + 7), "cmp", 0))
        of.append((first, len(steps)))
    return steps, of


STEPS, STEPS_OF = key_tiles()


def attention_order():
    def softmax(u):
        out = []
        for g in range(G):
            out += [("logits", u, g)] + ([("norm", u, g - 1)] if g else [])
        return out + [("norm", u, G - 1)]

    order = softmax(0)
    for u in range(len(UNITS)):
        nxt = softmax(u + 1) if u + 1 < len(UNITS) else []
        first, last = STEPS_OF[u]
        m, n = 0, last - first
        for k in range(n):
            order.append(("step", u, first + k))
            to = min(len(nxt), -(-len(nxt) * (k + 1) // max(1, n - LEAD)))
            order += nxt[m:to]
            m = to
            if k == LAG and u:
                order.append(("out", u - 1, 0))
        order += nxt[m:]
    return order + [("out", len(UNITS) - 1, 0)]


def build(nc, a):
    ring = plan()
    at, here = {}, [(nc.sbuf_base + 63) // 64 * 64]

    def sb(name, shape, dt=F32, offset=None):
        size = int(np.prod(shape[1:])) * (2 if dt == BF16 else 4)
        if offset is None:
            offset = here[0]
            here[0] += (size + 31) // 32 * 32
        assert offset + size <= nc.sbuf_usable_end, name
        at[name] = offset
        return nc.alloc_sbuf_tensor_at(name, shape, dt, offset=offset)

    resid = sb("resid", [P, TT, D])
    xt_hi = sb("xt_hi", [P, KT, SEQ], F32R)
    xt_lo = sb("xt_lo", [P, KT, SEQ], F32R)
    wt_hi = sb("wt_hi", [P, RING, D], F32R)
    wt_lo = sb("wt_lo", [P, RING, D], F32R)
    wt_raw = sb("wt_raw", [P, RAWS, D])
    ident = sb("ident", [P, P])
    ident_b = sb("ident_b", [P, P], BF16)
    ones_m = sb("ones_m", [P, P])
    far_mask = sb("far_mask", [P, P], BF16)
    cols = sb("cols", [P, 40])
    eps_c = sb("eps_c", [P, 1])
    sums = sb("sums", [P, 2, 2])
    neg_mean = sb("neg_mean", [P, 2])
    sq_sum = sb("sq_sum", [P, 2])
    rstd = sb("rstd", [P, 2])
    v_mean = sb("v_mean", [P, TT, 2])
    v_rstd = sb("v_rstd", [P, TT])
    v_stats = sb("v_stats", [P, TT, 6])
    w2 = sb("w2", [P, 2, DH])
    pe_col = sb("pe_col", [P, 2, CMP_BLOCK])
    hid = sb("hid", [P, 2, 64])
    pe_bias = sb("pe_bias", [P, 2])
    row_ok = sb("row_ok", [P, 1])
    q_t = sb("q_t", [P, 4, SEQ])
    ks = sb("ks", [P, KV_HEADS, 2, SEQ], F32R)
    vg = sb("vg", [P, TT, VG])
    cr = sb("cr", [P, 2, SEQ])
    low = sb("low", [P, 2, G, 3])
    den = sb("den", [P, 2, G, 3])
    inv = sb("inv", [P, 2, G, 3])
    kc = sb("kc", [P, KV_HEADS, 64], F32R)
    vc = sb("vc", [64, KV_HEADS, DH])
    o = at["q_t"]
    gmlp_g = sb("gmlp_g", [P, A_WIDTH], F32, o)
    gmlp_b = sb("gmlp_b", [P, A_WIDTH], F32, o + 2048)
    gmlp_bs = sb("gmlp_bs", [P, GROUPS, P], F32, o + 4096)
    ws = sb("ws", [P, GROUPS, P], F32, o + 6144)
    ws_t = sb("ws_t", [P, GROUPS, P], F32, o + 8192)
    onehot = sb("onehot", [N_BUCKETS, BIAS_ROW], F32, o + 10240)
    u_act = sb("u_act", [P, SEQ], F32, o + 10240)
    o = at["vg"]
    bias_row = sb("bias_row", [HEADS, BIAS_ROW], F32, o)
    rbias = sb("rbias", [N_BUCKETS, HEADS], F32, o + 4608)
    pe_row = sb("pe_row", [2 * CMP_BLOCK, P], F32, o + 4640)
    rows = sb("rows", [40, P], F32, o + 5152)
    qs = sb("qs", [P, 2, 2, G, P], F32R, at["cr"])
    o = at["resid"]
    mix_a = sb("mix_a", [P, GROUPS, SEQ], F32, o)
    v_tok = sb("v_tok", [P, TT, A_WIDTH], F32, o + 16384)
    w1 = sb("w1", [P, 2, CMP_BLOCK, DH], F32, o + 16384)
    nbias = sb("nbias", [P, HEADS, SEQ], F32, o)
    WIN0, CMP0 = SEQ, SEQ + WINDOW + P
    probs_o = sb("probs", [P, 2, G, CMP0 + 64], F32, at["wt_hi"] + G * P * 4)
    probs = [probs_o[:, (u + 1) % 2] for u in range(2)]
    assert all((u - i) % 2 == 0 for u, (i, _) in enumerate(UNITS))
    probs_t = [sb("probs_t0", [P, G, P]), sb("probs_t1", [P, G, P], F32, at["wt_hi"]),
               probs[0][:, :, SEQ - P:SEQ]]
    misc = at["q_t"]
    h_hi_t = sb("h_hi_t", [P, 2, SEQ], F32R, misc)
    h_lo_t = sb("h_lo_t", [P, 2, SEQ], F32R, misc + 8192)
    gate_act = sb("gate_act", [P, SEQ], F32, misc + 16384)
    h_f = sb("h_f", [P, SEQ], F32, misc + 20480)
    ln_g = sb("ln_g", [P, D], F32, misc + 33792)
    ln_b = sb("ln_b", [P, D], F32, misc + 37888)
    acc = sb("acc", [P, KT, SEQ], F32, misc)
    taps = sb("taps", [P, KT, CONV_W], F32, misc + 32768)
    conv_x = sb("conv_x", [P, 2, PAD + SEQ], F32, misc + 33792)
    glu_g = sb("glu_g", [P, SEQ], F32, misc + 42240)
    out_b = sb("out_b", [P, D], F32, misc + 46336)
    tap_rows = sb("tap_rows", [CONV_W, D], F32, misc + 45056)
    square = sb("square", [P, 2, SEQ], F32, misc + 42240)
    conv_rs = sb("conv_rs", [P, SEQ], F32, misc + 33792)
    tap_sum = sb("tap_sum", [P, 2, SEQ], F32, at["wt_lo"] + 4 * D * 4)
    tap_w = sb("tap_w", [P, CONV_W + 1], F32, at["wt_hi"] + 4 * D * 4 + 2 * PE_TAPS * P * 4)
    diag = sb("diag", [P, 2, PE_TAPS, P], F32, at["wt_hi"] + 4 * D * 4)
    ps = nc.alloc_psum_tensor("ps", [P, 8, HALF], F32)

    def sem(*names):
        made = [nc.alloc_semaphore(n) for n in names]
        return made if len(made) > 1 else made[0]

    def sems(name, keys):
        return {k: nc.alloc_semaphore(f"{name}_{k}") for k in keys}

    x_in, w_in, w_used = sems("x_in", range(TT)), sems("w_in", range(RAWS)), sems("w_used", range(RING))
    w_hi, w_lo = sem("w_hi", "w_lo")
    par_in, const_ok, small_t, small_c, ws_ok = sem("par_in", "const_ok", "small_t", "small_c", "ws_ok")
    bias_out, nb_ok, w1_in = sem("bias_out", "nb_ok", "w1_in")
    nb_in = sems("nb_in", range(KV_HEADS))
    ln_in, ln_mean, ln_sq, ln_sd, ln_done = sem("ln_in", "ln_mean", "ln_sq", "ln_sd", "ln_done")
    turned, turned_hi, turned_lo, scaled = sem("turned", "turned_hi", "turned_lo", "scaled")
    v_step, g_step = sem("v_step", "g_step")
    v_done, v_gelu, v_mv, v_sd, v_norm = sem("v_done", "v_gelu", "v_mv", "v_sd", "v_norm")
    vg_done, vg_out, feat_act, feat_dve = sem("vg_done", "vg_out", "feat_act", "feat_dve")
    u_mul, mix_done, mix_add, a_hi, a_lo, gates_ok = sem("u_mul", "mix_done", "mix_add", "a_hi", "a_lo", "gates_ok")
    cmp_done, cmp_act, cmp_dve = sem("cmp_done", "cmp_act", "cmp_dve")
    qs_ok, s_done, s_min, p_exp, p_norm = sem("qs_ok", "s_done", "s_min", "p_exp", "p_norm")
    pt_done, pt_copied, pv_done, o_hi, o_lo = sem("pt_done", "pt_copied", "pv_done", "o_hi", "o_lo")
    y_done, y_free = sems("y_done", GROUP_COUNT), sems("y_free", GROUP_COUNT)
    silu_done, h_prod, h_hi, h_lo = (sems(n, range(DEPTH)) for n in ("silu_done", "h_prod", "h_hi", "h_lo"))
    tap_in, tap_t, tap_ok, outb_in, outb_ok = sem("tap_in", "tap_t", "tap_ok", "outb_in", "outb_ok")
    glu_sig, glu_free, conv_v, pad_ok = sem("glu_sig", "glu_free", "conv_v", "pad_ok")
    diag_ok, part_done, part_added, tap_w_ok = sem("diag_ok", "part_done", "part_added", "tap_w_ok")
    mean_ok, cen, sq_ok, sq_used, var_sd, nrm, act_ok, act_hi, act_lo = sem(
        "mean_ok", "cen", "sq_ok", "sq_used", "var_sd", "nrm", "act_ok", "act_hi", "act_lo")
    out_done = sem("out_done")

    w_in_ap, w_out_ap = a["hyb_w_in"], a["hyb_w_out"]
    PARAMS = 18

    def banks(b, n=2):
        return ps[:, b:b + n, :].rearrange("p b c -> p (b c)")

    def tile_cols(t):
        return slice(t * P, (t + 1) * P)

    def raw(c):
        return wt_raw[:, c.raw, :]

    def load_chunk(sp, c, pieces):
        if not (isinstance(c.number, int) and c.number <= RAWS):
            sp.wait_ge(w_lo, c.number - RAWS)
        for dst, src in pieces:
            sp.dma_start(dst, src).then_inc(w_in[c.raw], 16)

    def split_hi(act, c):
        act.wait_ge(w_in[c.raw], c.landed)
        if not (isinstance(c.before, int) and c.before == 0):
            act.wait_ge(w_used[c.slot], c.before)
        nc.scalar.copy(wt_hi[:, c.slot, :], raw(c)).then_inc(w_hi, 1)

    def split_lo(dve, c):
        dve.wait_ge(w_hi, c.number)
        nc.vector.tensor_tensor(wt_lo[:, c.slot, :], raw(c), wt_hi[:, c.slot, :], ALU.subtract).then_inc(w_lo, 1)

    def feature_product(pe, c, b):
        pe.wait_ge(w_lo, c.number)
        for k in range(KT):
            hi, lo = wt_hi[:, c.slot, tile_cols(k)], wt_lo[:, c.slot, tile_cols(k)]
            for n, (w, x) in enumerate(((hi, xt_hi), (hi, xt_lo), (lo, xt_hi))):
                for h in range(2):
                    last = nc.tensor.matmul(ps[:, b + h, :], w, x[:, k, h * HALF:(h + 1) * HALF],
                                            start=(k == 0 and n == 0), stop=(k == KT - 1 and n == 2))
        last.then_inc(w_used[c.slot], 1)

    def token_product(pe, name, cs, left, group, turn=False):
        pe.wait_ge(w_lo, cs[1].number)
        for t in range(TT):
            for h in range(2):
                q = 2 * t + h
                pe.wait_ge(y_free[name], 16 * group + (q + 1))
                cols_h = slice(h * HALF, (h + 1) * HALF)
                for j, c in enumerate(cs):
                    lh, ll = (x[:, tile_cols(t)] for x in left[j])
                    rh, rl = wt_hi[:, c.slot, cols_h], wt_lo[:, c.slot, cols_h]
                    bank = ps[:, 4 + q % 4, :]
                    nc.tensor.matmul(bank, lh, rh, start=(j == 0), stop=False)
                    nc.tensor.matmul(bank, lh, rl, start=False, stop=False)
                    last = nc.tensor.matmul(bank, ll, rh, start=False, stop=(j == 1))
                    if q == 15:
                        last.then_inc(w_used[c.slot], 1)
                if q < 15:
                    last.then_inc(y_done[name], 1)
            if turn and t >= 2:
                turn_tile(pe, NORM_OF[name], t - 2)
        if turn:
            turn_tile(pe, NORM_OF[name], TT - 2)
            turn_tile(pe, NORM_OF[name], TT - 1)
            pe.wait_ge(turned_lo, TT * (NORM_OF[name] + 1))

    def add_bank(dve, name, c, group, q, total=None):
        if q < 15:
            dve.wait_ge(y_done[name], 15 * group + (q + 1))
        else:
            dve.wait_ge(w_used[c.slot], c.used)
        r = resid[:, q // 2, (q % 2) * HALF:(q % 2 + 1) * HALF]
        if total is None:
            nc.vector.tensor_tensor(r, r, ps[:, 4 + q % 4, :], ALU.add).then_inc(y_free[name], 1)
        else:
            nc.vector.tensor_tensor_reduce(r, r, ps[:, 4 + q % 4, :], 1.0, 0.0, ALU.add, ALU.add,
                                           total).then_inc(y_free[name], 1)

    steps_of_v = [0]

    def v_wait(dve, *made):
        for ins in made:
            ins.then_inc(v_step, 1)
        steps_of_v[0] += len(made)
        dve.wait_ge(v_step, steps_of_v[0])

    def turn_tile(pe, event, t):
        if event == 0:
            pe.wait_ge(x_in[t], 16)
        else:
            pe.wait_ge(ln_done, TT * (event - 1) + t + 1)
        if t >= 2:
            pe.wait_ge(turned_lo, TT * event + t - 1)
        for k in range(KT):
            last = nc.tensor.transpose(ps[:, 2 * (t % 2) + k // 4, tile_cols(k % 4)], resid[:, t, tile_cols(k)], ident[:])
        last.then_inc(turned, 1)

    def turned_view(t):
        return ps[:, 2 * (t % 2):2 * (t % 2) + 2, :].rearrange("p b (k c) -> p (b k) c", c=P)

    def turn_hi(act, event, t):
        act.wait_ge(turned, TT * event + t + 1)
        nc.scalar.copy(xt_hi[:, :, tile_cols(t)], turned_view(t)).then_inc(turned_hi, 1)

    def turn_lo(dve, event, t):
        dve.wait_ge(turned_hi, TT * event + t + 1)
        nc.vector.tensor_tensor(xt_lo[:, :, tile_cols(t)], turned_view(t), xt_hi[:, :, tile_cols(t)],
                                ALU.subtract).then_inc(turned_lo, 1)

    def scale_tile(act, t):
        nc.scalar.mul(resid[:, t, :], resid[:, t, :], ALPHA).then_inc(scaled, 1)

    def norm_act(act, name, turn=True):
        e = NORM_OF[name]
        for t in range(TT + 2):
            if t < TT:
                b, n = t % 2, TT * (e - 1) + t
                act.wait_ge(ln_mean, n + 1)
                if t >= 2:
                    act.wait_ge(ln_done, n - 1)
                nc.scalar.activation(gate_act[:], resid[:, t, :], ACT.Square, bias=neg_mean[:, b:b + 1],
                                     accum_out=sq_sum[:, b:b + 1]).then_inc(ln_sq, 1)
                act.wait_ge(ln_sq, n + 1)
                nc.scalar.activation(rstd[:, b:b + 1], sq_sum[:, b:b + 1], ACT.Sqrt, bias=eps_c[:, 0:1],
                                     scale=1.0 / D).then_inc(ln_sd, 1)
            if t >= 2 and turn:
                turn_hi(act, e, t - 2)
                scale_tile(act, t - 2)

    def norm_dve(dve, name, c, turn=True):
        e = NORM_OF[name]
        for t in range(TT + 2):
            if t < TT:
                b = t % 2
                for h in range(2):
                    add_bank(dve, name, c, GROUP_COUNT[name] - 1, 2 * t + h, sums[:, b, h:h + 1])
                dve.wait_ge(y_free[name], 4 + 16 * (GROUP_COUNT[name] - 1) + 2 * t + 2)
                nc.vector.tensor_scalar(neg_mean[:, b:b + 1], sums[:, b, 0:1], sums[:, b, 1:2], -1.0 / D,
                                        ALU.add, ALU.mult).then_inc(ln_mean, 1)
            if 1 <= t <= TT:
                b, x, n = (t - 1) % 2, resid[:, t - 1, :], TT * (e - 1) + t - 1
                if t == 1:
                    dve.wait_ge(ln_in, 32 * e)
                dve.wait_ge(ln_sd, n + 1)
                nc.vector.reciprocal(rstd[:, b:b + 1], rstd[:, b:b + 1]).then_inc(v_step, 1)
                dve.wait_ge(ln_mean, n + 1)
                nc.vector.scalar_tensor_tensor(out=x, in0=x, scalar=neg_mean[:, b:b + 1], in1=ln_g[:],
                                               op0=ALU.add, op1=ALU.mult).then_inc(v_step, 1)
                steps_of_v[0] += 2
                dve.wait_ge(v_step, steps_of_v[0])
                nc.vector.scalar_tensor_tensor(out=x, in0=x, scalar=rstd[:, b:b + 1], in1=ln_b[:],
                                               op0=ALU.mult, op1=ALU.add).then_inc(ln_done, 1)
            if t >= 2 and turn:
                turn_lo(dve, e, t - 2)

    def load_small(pool):
        def par(dst, src):
            pool.dma_start(dst, src).then_inc(par_in, 16)
        par(ws[:], a["gmlp_w_s"].rearrange("g t s -> t g s"))
        par(rbias[:], a["rel_bias"])
        par(onehot[:], a["bucket_onehot"])
        for dst, name, n in ((gmlp_g[:], "gmlp_ln_g", A_WIDTH), (gmlp_b[:], "gmlp_ln_b", A_WIDTH),
                             (gmlp_bs[:], "gmlp_b_s", A_WIDTH)):
            src = bass.AP(a[name].tensor, 0, [[0, P], [1, n]])
            par(dst.rearrange("p g t -> p (g t)") if name == "gmlp_b_s" else dst, src)
        for kv, n in enumerate("kv"):
            for h in range(2):
                par(pe_row[kv * CMP_BLOCK:(kv + 1) * CMP_BLOCK, h * DH:(h + 1) * DH], a[f"cmp_pe_{n}"])
                par(w2[h * DH:(h + 1) * DH, kv, :], a[f"cmp_w2_{n}"])
        r = 0
        for n, k in (("conv_b_in", 2 * KT), ("conv_dw_b", KT)):
            par(rows[r:r + k, :], a[n].rearrange("(k p) -> k p", p=P))
            r += k
        par(rows[r:r + KT, :], a["conv_ln_g"].rearrange("(k p) -> k p", p=P))
        par(rows[r + KT:r + 2 * KT, :], a["conv_ln_b"].rearrange("(k p) -> k p", p=P))

    def norm_params(sp, name):
        layer, kind = divmod(NORM_OF[name] - 1, 2)
        for dst, n in ((ln_g, "g"), (ln_b, "b")):
            src = bass.AP(a[f"norm_{('mix', 'ffn')[kind]}_{n}"].tensor, layer * D, [[0, P], [1, D]])
            sp.dma_start(dst[:], src).then_inc(ln_in, 16)

    def ffn_loads(sp, layer):
        wg, wu, wd = (a[n][layer] for n in ("ffn_w_gate", "ffn_w_up", "ffn_w_down"))

        def columns(c, w, f):
            load_chunk(sp, c, [(raw(c).rearrange("p (k n) -> p k n", k=KT),
                                w[:, bass.ds(f * P, P)].rearrange("(k p) n -> p k n", p=P))])

        def down(c, f):
            load_chunk(sp, c, [(raw(c), wd[bass.ds(f * P, P), :])])

        c = ring[f"ffn{layer}_first"]
        columns(c[0], wg, 0)
        columns(c[1], wu, 0)
        columns(c[2], wg, 1)
        columns(c[3], wu, 1)
        if layer == 1:
            sp.wait_ge(act_ok, KT)
            norm_params(sp, "conv_out")
        sp.wait_ge(ln_done, TT * (2 * layer + 1))
        norm_params(sp, f"ffn{layer}")
        with sp.Fori(0, FG - 1) as n:
            c = ring[f"ffn{layer}"](n)
            columns(c[0], wg, 2 * n + 2)
            down(c[1], 2 * n)
            down(c[2], 2 * n + 1)
            columns(c[3], wu, 2 * n + 2)
            columns(c[4], wg, 2 * n + 3)
            columns(c[5], wu, 2 * n + 3)
        c = ring[f"ffn{layer}_last"]
        down(c[0], FT - 2)
        down(c[1], FT - 1)

    def sync_program(sp):
        def v_chunk(j):
            c, src = ring["v"][j], w_in_ap[2 * j * P:(2 * j + 2) * P, A_WIDTH:2 * A_WIDTH]
            load_chunk(sp, c, [(raw(c).rearrange("p (k n) -> p k n", k=2), src.rearrange("(k p) n -> p k n", p=P))])

        for t in range(TT):
            sp.dma_start(resid[:, t, :], a["x"][tile_cols(t), :]).then_inc(x_in[t], 16)
            if t in (3, 4):
                v_chunk(t - 3)
        v_chunk(2)
        v_chunk(3)
        for j, c in enumerate(ring["vg"]):
            nk = min(3, KT - 3 * j)
            dst = raw(c)[:, 0:nk * VG].rearrange("p (k n) -> p k n", k=nk)
            k0 = slice(3 * j * P, (3 * j + nk) * P)
            load_chunk(sp, c, [
                (dst[:, :, 0:P], w_in_ap[k0, COL_VSLC:COL_VSLC + P].rearrange("(k p) n -> p k n", p=P)),
                (dst[:, :, P:VG], w_in_ap[k0, COL_VWIN:COL_VWIN + P + GATES].rearrange("(k p) n -> p k n", p=P))])
        for n, (c, col) in enumerate(zip(ring["feat"], FEATURE_COLS)):
            load_chunk(sp, c, [(raw(c).rearrange("p (k n) -> p k n", k=KT),
                                w_in_ap[:, col:col + P].rearrange("(k p) n -> p k n", p=P))])
            if n == 7:
                sp.wait_ge(mix_done, 8)
                for kv, name in enumerate("kv"):
                    for h in range(2):
                        sp.dma_start(w1[h * DH:(h + 1) * DH, kv, :, :],
                                     a[f"cmp_w1_{name}"].rearrange("(j d) m -> d j m", d=DH)).then_inc(w1_in, 16)
        sp.wait_ge(bias_out, 16)
        sp.wait_ge(a_lo, GROUPS)
        for h0 in (0, G):
            if h0:
                sp.wait_ge(cmp_done, 3)
            src = bass.AP(a["bias_scratch"].tensor, h0 * P * BIAS_ROW + P - 1,
                          [[BIAS_ROW - 1, P], [P * BIAS_ROW, G], [1, SEQ]])
            sp.dma_start(nbias[:, h0:h0 + G, :], src).then_inc(nb_in[h0 // G], 16)
        sp.wait_ge(s_min, 3 * G * len(UNITS))
        sp.dma_start(tap_rows[:], a["conv_dw_w"]).then_inc(tap_in, 16)
        for k in range(TT):
            sp.dma_start(resid[:, k, :], a["x"][tile_cols(k), :]).then_inc(x_in[k], 16)
        sp.wait_ge(pt_done, STEPS_OF[-2][1])
        for k, c in enumerate(ring["w_out"]):
            if k == 1:
                sp.wait_ge(pv_done, len(STEPS))
            load_chunk(sp, c, [(raw(c), w_out_ap[tile_cols(k), :])])
            if k == 1:
                norm_params(sp, "w_out")
        sp.wait_ge(tap_ok, 1)
        sp.dma_start(out_b[:], bass.AP(a["conv_b_out"].tensor, 0, [[0, P], [1, D]])).then_inc(outb_in, 16)
        ffn_loads(sp, 0)
        with sp.Fori(0, KT // 2) as n:
            for j, c in enumerate(ring["conv_in"](n)):
                src = a["conv_w_in"][:, bass.ds((j % 2) * D + (2 * n + j // 2) * P, P)]
                load_chunk(sp, c, [(raw(c).rearrange("p (k n) -> p k n", k=KT), src.rearrange("(k p) n -> p k n", p=P))])
        for k, c in enumerate(ring["conv_out"]):
            load_chunk(sp, c, [(raw(c), a["conv_w_out"][tile_cols(k), :])])
        ffn_loads(sp, 1)
        for t in range(TT):
            sp.wait_ge(ln_done, 3 * TT + t + 1)
            sp.dma_start(a["out"][tile_cols(t), :], resid[:, t, :]).then_inc(out_done, 16)
        sp.wait_ge(out_done, 16 * TT)

    def ffn_pe(pe, layer):
        name = f"ffn{layer}"

        def gate(c, f):
            if not (isinstance(f, int) and f == 0):
                pe.wait_ge(silu_done[layer], f)
            feature_product(pe, c, 0)

        def up(c, f):
            if not (isinstance(f, int) and f == 0):
                pe.wait_ge(h_prod[layer], f)
            feature_product(pe, c, 2)

        def down(cs, group, turn=False):
            pe.wait_ge(h_lo[layer], 2 * group + 2)
            token_product(pe, name, cs, [(h_hi_t[:, j], h_lo_t[:, j]) for j in range(2)], group, turn)

        c = ring[name + "_first"]
        for f in range(2):
            gate(c[2 * f], f)
            up(c[2 * f + 1], f)

        def trip(n):
            c = ring[name](n)
            gate(c[0], 2 * n + 2)
            down(c[1:3], n)
            up(c[3], 2 * n + 2)
            gate(c[4], 2 * n + 3)
            up(c[5], 2 * n + 3)
        with pe.Fori(0, FG - 2) as n:
            trip(n)
        trip(FG - 2)
        down(ring[name + "_last"], FG - 1, turn=layer == 0)

    def attention_pe(pe):
        def logits(u, g, branch):
            i, kv = UNITS[u]
            piece = (u * G + g) * 2 + branch
            b = 2 * (piece % 2)
            if g == 0 and branch == 0:
                pe.wait_ge(qs_ok, u + 1)
            if piece >= 2:
                pe.wait_ge(s_min, 3 * ((piece - 2) // 2) + (1 if branch == 0 else 3))
            qh, ql = qs[:, u % 2, 0, g, :], qs[:, u % 2, 1, g, :]
            k0, nk = (0, (i + 1) * P) if branch == 0 else window(i)
            for c0 in range(0, nk, HALF):
                n = min(HALF, nk - c0)
                out, keys = ps[:, b + c0 // HALF, 0:n], ks[:, kv, branch, k0 + c0:k0 + c0 + n]
                far = branch == 1 and c0 == 0 and nk > WINDOW
                nc.tensor.matmul(out, qh, keys, start=True, stop=False)
                last = nc.tensor.matmul(out, ql, keys, start=False, stop=not far)
                if far:
                    nc.tensor.matmul(ps[:, b, 0:P], ident_b[:], far_mask[:], start=False, stop=True)
            if branch == 1:
                n = 8 * i + 8
                out = ps[:, b + 1, P:P + n]
                nc.tensor.matmul(out, qh, kc[:, kv, 0:n], start=True, stop=False)
                last = nc.tensor.matmul(out, ql, kc[:, kv, 0:n], start=False, stop=True)
            last.then_inc(s_done, 1)

        def turn(s):
            u, col, n, _, _ = STEPS[s]
            if s == STEPS_OF[u][0]:
                pe.wait_ge(p_norm, G * (u + 1))
            if s >= BUFS:
                copied(s - BUFS)
            for g in range(G):
                last = nc.tensor.transpose(ps[0:n, 4 + s % BUFS, tile_cols(g)], probs[u % 2][:, g, col:col + n], ident[:])
            last.then_inc(pt_done, 1)

        def copied(s):
            pe.wait_ge(pt_copied, s + 1)

        def values(s):
            u, _, n, branch, j = STEPS[s]
            _, kv = UNITS[u]
            copied(s)
            if s == STEPS_OF[u][0] and u >= 2:
                pe.wait_ge(o_lo, 2 * (u - 1))
            c0 = (P if branch == "win" else 0) + kv * DH
            v = vc[0:n, kv, :] if branch == "cmp" else vg[:, j, c0:c0 + DH]
            half = slice((u % 2) * DH, (u % 2 + 1) * DH)
            nc.tensor.matmul(ps[half, 7, :], v, probs_t[s % BUFS][0:n], start=(s == STEPS_OF[u][0]),
                             stop=(s == STEPS_OF[u][1] - 1)).then_inc(pv_done, 1)

        for what, u, n in attention_order():
            if what == "logits":
                logits(u, n, 0)
                logits(u, n, 1)
            elif what == "step":
                turn(n)
                if n >= LAG:
                    values(n - LAG)
        for n in range(len(STEPS) - LAG, len(STEPS)):
            values(n)

    def tensor_program(pe):
        pe.wait_ge(const_ok, 2)
        for t in range(TT):
            turn_tile(pe, 0, t)
        pe.wait_ge(par_in, 16 * PARAMS)
        for g in range(GROUPS):
            nc.tensor.transpose(ps[:, 4, tile_cols(g)], ws[:, g, :], ident[:]).then_inc(small_t, 1)
        nc.tensor.transpose(ps[:, 5, 0:40], rows[:], ident[0:40, 0:40]).then_inc(small_t, 1)
        nc.tensor.transpose(ps[:, 5, 64:128], pe_row[:], ident[0:64, 0:64]).then_inc(small_t, 1)
        third = BIAS_ROW // 3
        for n, out in enumerate((ps[0:HEADS, 6, 0:third], ps[0:HEADS, 7, 0:third], ps[0:HEADS, 5, P:P + third])):
            nc.tensor.matmul(out, rbias[:], onehot[:, n * third:(n + 1) * third], start=True, stop=True).then_inc(small_t, 1)
        pe.wait_ge(small_c, 6)
        c = ring["v"]
        pe.wait_ge(w_lo, c[3].number)
        pe.wait_ge(turned_lo, TT)
        for t in range(TT):
            if t >= 4:
                pe.wait_ge(v_gelu, t - 3)
            for k in range(KT):
                s, cut = c[k // 2].slot, slice((k % 2) * HALF, (k % 2 + 1) * HALF)
                xh, xl = xt_hi[:, k, tile_cols(t)], xt_lo[:, k, tile_cols(t)]
                out = ps[:, 4 + t % 4, :]
                nc.tensor.matmul(out, xh, wt_hi[:, s, cut], start=(k == 0), stop=False)
                nc.tensor.matmul(out, xh, wt_lo[:, s, cut], start=False, stop=False)
                last = nc.tensor.matmul(out, xl, wt_hi[:, s, cut], start=False, stop=(k == KT - 1))
                if t == TT - 1 and k % 2:
                    last.then_inc(w_used[s], 1)
            if t < TT - 1:
                last.then_inc(v_done, 1)
        c = ring["vg"]
        pe.wait_ge(w_lo, c[1].number)

        def vg_product(t, ks_):
            for k in ks_:
                s, cut = c[k // 3].slot, slice((k % 3) * VG, (k % 3 + 1) * VG)
                xh, xl = xt_hi[:, k, tile_cols(t)], xt_lo[:, k, tile_cols(t)]
                out = ps[:, t % 4, 0:VG]
                nc.tensor.matmul(out, xh, wt_hi[:, s, cut], start=(k == 0), stop=False)
                nc.tensor.matmul(out, xh, wt_lo[:, s, cut], start=False, stop=False)
                last = nc.tensor.matmul(out, xl, wt_hi[:, s, cut], start=False, stop=(k == KT - 1))
                if t == TT - 1 and k in (2, 5, 7):
                    last.then_inc(w_used[s], 1)
            if t < TT - 1 and k == KT - 1:
                last.then_inc(vg_done, 1)
        for t in range(4):
            vg_product(t, range(6))
        pe.wait_ge(w_lo, c[2].number)
        for t in range(4):
            vg_product(t, range(6, KT))
        for t in range(4, TT):
            pe.wait_ge(vg_out, t - 3)
            vg_product(t, range(KT))

        def features(n):
            if n == 0:
                pe.wait_ge(vg_out, TT)
            if n >= 2:
                pe.wait_ge(feat_act, n - 1)
            if n in (4, 5):
                pe.wait_ge(feat_dve, n - 3)
            feature_product(pe, ring["feat"][n], 2 * (n % 2))
        features(0)
        features(1)
        pe.wait_ge(v_norm, TT)
        pe.wait_ge(ws_ok, 1)
        for g in range(GROUPS):
            for h in range(2):
                n = 2 * g + h
                if n >= 4:
                    pe.wait_ge(mix_add, n - 3)
                for m in range(4):
                    last = nc.tensor.matmul(ps[:, 4 + n % 4, tile_cols(m)], v_tok[:, 4 * h + m, tile_cols(g)],
                                            ws_t[:, g, :], start=True, stop=True)
                last.then_inc(mix_done, 1)
        for n in range(2, len(FEATURE_COLS)):
            features(n)
        pe.wait_ge(w1_in, 64)
        pe.wait_ge(feat_act, len(FEATURE_COLS))
        for kv in range(2):
            for h in range(KV_HEADS):
                part = slice(h * DH, (h + 1) * DH)
                for j in range(CMP_BLOCK):
                    nc.tensor.matmul(ps[part, kv, 0:N_CMP], w1[part, kv, j, :],
                                     cr[part, kv, j:j + CMP_STRIDE * (N_CMP - 1) + 1:CMP_STRIDE],
                                     start=(j == 0), stop=(j == CMP_BLOCK - 1))
                for j in range(CMP_BLOCK):
                    last = nc.tensor.matmul(ps[part, 2 + kv, 0:1], w1[part, kv, j, :], pe_col[part, kv, j:j + 1],
                                            start=(j == 0), stop=(j == CMP_BLOCK - 1))
            last.then_inc(cmp_done, 1)
        pe.wait_ge(cmp_act, 4)
        for h in range(KV_HEADS):
            part = slice(h * DH, (h + 1) * DH)
            nc.tensor.matmul(ps[part, 4, 0:64], w2[part, 0, :], hid[part, 0, :], start=True, stop=True)
            last = nc.tensor.matmul(ps[0:64, 5 + h, 0:DH], hid[part, 1, :], w2[part, 1, :], start=True, stop=True)
        last.then_inc(cmp_done, 1)
        pe.wait_ge(cmp_act, 6)
        pe.wait_ge(cmp_dve, 4)
        attention_pe(pe)
        pe.wait_ge(o_lo, 2 * len(UNITS))
        pe.wait_ge(a_lo, GROUPS)

        def out_product(name):
            for n in range(GROUP_COUNT[name]):
                if name == "conv_out":
                    pe.wait_ge(act_lo, 2 * n + 2)
                token_product(pe, name, ring[name][2 * n:2 * n + 2],
                              [(xt_hi[:, k], xt_lo[:, k]) for k in (2 * n, 2 * n + 1)], n,
                              turn=n == GROUP_COUNT[name] - 1)
        pe.wait_ge(tap_in, 16)
        for k in range(KT):
            last = nc.tensor.transpose(ps[:, 0, k * 32:k * 32 + CONV_W], tap_rows[:, tile_cols(k)], ident[0:CONV_W, 0:CONV_W])
        last.then_inc(tap_t, 1)
        out_product("w_out")
        ffn_pe(pe, 0)
        conv = ring["conv_in"]

        def values_and_gates(T, c):
            if not (isinstance(T, int) and T == 0):
                pe.wait_ge(glu_free, T)
            feature_product(pe, c[0], 0)
            feature_product(pe, c[1], 2)

        def tap_products(T, m, count=PE_TAPS):
            if not (isinstance(T, int) and T == 0):
                pe.wait_ge(part_added, T)
            pe.wait_ge(diag_ok, T + 1)
            pe.wait_ge(glu_free, T + 1)
            for j in range(count):
                if j == PE_TAPS:
                    pe.wait_ge(diag_ok, KT + 1)
                place = diag[:, (m + j // PE_TAPS) % 2, j % PE_TAPS, :]
                for h in range(2):
                    last = nc.tensor.matmul(ps[:, 4 + h, :], place, conv_x[:, m, h * HALF + j:(h + 1) * HALF + j],
                                            start=(j == 0), stop=(j == count - 1))
            last.then_inc(part_done, 1)

        def mean_share(T, first=False, last=False):
            pe.wait_ge(part_added, T + 1)
            for h in range(2):
                ins = nc.tensor.matmul(ps[:, 6 + h, :], ones_m[:], acc[:, T:T + 1, h * HALF:(h + 1) * HALF]
                                       if isinstance(T, int) else acc[:, bass.ds(T, 1), h * HALF:(h + 1) * HALF],
                                       start=first, stop=last)
            if last:
                ins.then_inc(mean_ok, 1)

        def conv_trip(n):
            c = conv(n)
            for j in range(2):
                T = 2 * n + j
                values_and_gates(T, c[2 * j:2 * j + 2])
                if isinstance(T, int):
                    if T >= 1:
                        tap_products(T - 1, (j + 1) % 2)
                else:
                    mean_share(T - 2)
                    tap_products(T - 1, (j + 1) % 2)
        conv_trip(0)
        values_and_gates(2, conv(1)[0:2])
        mean_share(0, first=True)
        tap_products(1, 1)
        values_and_gates(3, conv(1)[2:4])
        mean_share(1)
        tap_products(2, 0)
        with pe.Fori(2, KT // 2) as n:
            conv_trip(n)
        tap_products(KT - 1, 1, 2 * PE_TAPS)
        mean_share(KT - 2)
        mean_share(KT - 1, last=True)
        for k in range(KT):
            pe.wait_ge(sq_ok, k + 1)
            for h in range(2):
                last = nc.tensor.matmul(ps[:, 2 + h, :], ones_m[:], square[:, k % 2, h * HALF:(h + 1) * HALF],
                                        start=(k == 0), stop=(k == KT - 1))
            last.then_inc(sq_used, 1)
        out_product("conv_out")
        ffn_pe(pe, 1)

    def ffn_act(act, layer):
        name = f"ffn{layer}"

        def silu(c, f):
            act.wait_ge(w_used[c.slot], c.used)
            if not (isinstance(f, int) and f == 0):
                act.wait_ge(h_prod[layer], f)
            nc.scalar.activation(gate_act[:], banks(0), ACT.Silu).then_inc(silu_done[layer], 1)

        def hi(f, j):
            act.wait_ge(h_prod[layer], f + 1)
            nc.scalar.copy(h_hi_t[:, j, :], h_f[:]).then_inc(h_hi[layer], 1)

        c = ring[name + "_first"]
        silu(c[0], 0)
        split_hi(act, ring[name](0)[0])
        hi(0, 0)
        silu(c[2], 1)
        hi(1, 1)

        def trip(n, more):
            c = ring[name](n)
            for j in (1, 2, 3):
                split_hi(act, c[j])
            silu(c[0], 2 * n + 2)
            split_hi(act, c[4])
            hi(2 * n + 2, 0)
            split_hi(act, c[5])
            silu(c[4], 2 * n + 3)
            if more:
                split_hi(act, ring[name](n + 1)[0])
            hi(2 * n + 3, 1)
        with act.Fori(0, FG - 2) as n:
            trip(n, True)
        trip(FG - 2, False)
        for c in ring[name + "_last"]:
            split_hi(act, c)

    def turned_probs(s):
        return ps[0:STEPS[s][2], 4 + s % BUFS, :].rearrange("p (g q) -> p g q", q=P)

    def unit_out(u):
        return ps[(u % 2) * DH:(u % 2 + 1) * DH, 7, :].rearrange("p (t r q) -> p r t q", r=2, q=P)

    def attention_act(act):
        for what, u, n in attention_order():
            i, kv = UNITS[u]
            if what == "logits":
                k0, nk = window(i)
                pr = probs[u % 2][:, n]
                for b, part in ((1, pr[:, 0:(i + 1) * P]), (2, pr[:, WIN0:WIN0 + nk]),
                                (0, pr[:, CMP0:CMP0 + min(N_CMP, 8 * i + 7)])):
                    act.wait_ge(s_min, 3 * (u * G + n) + {1: 1, 2: 2, 0: 3}[b])
                    nc.scalar.activation(part, part, ACT.Exp, bias=low[:, u % 2, n, b:b + 1], scale=-1.0,
                                         accum_out=den[:, u % 2, n, b:b + 1]).then_inc(p_exp, 1)
            elif what == "step":
                keys = STEPS[n][2]
                act.wait_ge(pt_done, n + 1)
                if n >= BUFS:
                    act.wait_ge(pv_done, n - BUFS + 1)
                nc.scalar.copy(probs_t[n % BUFS][0:keys], turned_probs(n)).then_inc(pt_copied, 1)
            elif what == "out":
                act.wait_ge(pv_done, STEPS_OF[u][1])
                out = unit_out(u)
                for r in range(2):
                    nc.scalar.copy(xt_hi[r * DH:(r + 1) * DH, 4 + 2 * kv:6 + 2 * kv, tile_cols(i)], out[:, r]).then_inc(o_hi, 1)

    def scalar_program(act):
        for t in range(TT):
            turn_hi(act, 0, t)
            if t in V_SPLITS:
                split_hi(act, ring["v"][V_SPLITS.index(t)])
        for c in ring["vg"][:2]:
            split_hi(act, c)
        act.wait_ge(small_c, 6)
        act.dma_start(a["bias_scratch"], bias_row[:].unsqueeze(1).broadcast_to([HEADS, P, BIAS_ROW])).then_inc(bias_out, 16)
        for t in range(TT):
            if t < TT - 1:
                act.wait_ge(v_done, t + 1)
            else:
                act.wait_ge(w_used[ring["v"][3].slot], ring["v"][3].used)
            nc.scalar.activation(v_tok[:, t, :], ps[:, 4 + t % 4, :], ACT.Gelu_apprx_tanh).then_inc(v_gelu, 1)
        feat = ring["feat"]
        split_hi(act, ring["vg"][2])
        act.wait_ge(v_mv, TT)
        nc.scalar.activation(v_rstd[:], v_mean[:, :, 1], ACT.Sqrt, bias=eps_c[:, 0:1]).then_inc(v_sd, 1)
        for c in feat[:6]:
            split_hi(act, c)
        for n, c in enumerate(feat):
            act.wait_ge(w_used[c.slot], c.used)
            got = banks(2 * (n % 2))
            if n < 2:
                last = nc.scalar.copy(cr[:, n, :], got)
            elif n < F_U:
                for kv in range(KV_HEADS):
                    last = nc.scalar.copy(ks[0:DH, kv, n - 2, :], got[kv * DH:(kv + 1) * DH, :])
            elif n < F_Q:
                if n > F_U:
                    act.wait_ge(u_mul, n - F_U)
                last = nc.scalar.activation(u_act[:], got, ACT.Gelu_apprx_tanh)
            else:
                if n == F_Q:
                    act.wait_ge(u_mul, GROUPS)
                last = nc.scalar.mul(q_t[:, n - F_Q, :], got, -SCALE)
            last.then_inc(feat_act, 1)
            if n + 6 < len(feat):
                split_hi(act, feat[n + 6])
        for g in range(GROUPS):
            nc.scalar.copy(xt_hi[:, g, :], mix_a[:, g, :]).then_inc(a_hi, 1)
        for kv in range(2):
            act.wait_ge(cmp_done, kv + 1)
            nc.scalar.copy(pe_bias[:, kv:kv + 1], ps[:, 2 + kv, 0:1]).then_inc(cmp_act, 1)
            act.wait_ge(cmp_act, 2 * kv + 1)
            nc.scalar.activation(hid[:, kv, 0:N_CMP], ps[:, kv, 0:N_CMP], ACT.Gelu_apprx_tanh,
                                 bias=pe_bias[:, kv:kv + 1]).then_inc(cmp_act, 1)
        act.wait_ge(cmp_done, 3)
        for kv in range(KV_HEADS):
            nc.scalar.copy(kc[0:DH, kv, :], ps[kv * DH:(kv + 1) * DH, 4, 0:64]).then_inc(cmp_act, 1)
        act.wait_ge(vg_out, TT)
        gates = vg[:, :, 2 * P:VG]
        nc.scalar.activation(gates, gates, ACT.Sigmoid).then_inc(gates_ok, 1)
        attention_act(act)

        def out_act(name, done, following):
            cs = ring[name]
            for k in range(KT):
                if done <= k < 6:
                    split_hi(act, cs[k])
                if name == "w_out":
                    act.wait_ge(x_in[k], 32)
                    scale_tile(act, k)
            for c in cs[6:] + following:
                split_hi(act, c)

        act.wait_ge(pv_done, len(STEPS))
        out_act("w_out", 0, ring["ffn0_first"])
        norm_act(act, "w_out")
        ffn_act(act, 0)
        for c in ring["conv_in"](0):
            split_hi(act, c)
        norm_act(act, "ffn0")

        def conv_trip(n, more):
            c, nxt = ring["conv_in"](n), ring["conv_in"](n + 1) if more else None
            for j in range(2):
                act.wait_ge(w_used[c[2 * j + 1].slot], c[2 * j + 1].used)
                if not (isinstance(n, int) and 2 * n + j == 0):
                    act.wait_ge(glu_free, 2 * n + j)
                act.nop()
                nc.scalar.activation(glu_g[:], banks(2), ACT.Sigmoid,
                                     bias=cols[:, bass.ds(2 * n + (KT + j), 1)]).then_inc(glu_sig, 1)
                if more:
                    split_hi(act, nxt[2 * j])
                    split_hi(act, nxt[2 * j + 1])
        conv_trip(0, True)
        with act.Fori(1, KT // 2 - 1) as n:
            conv_trip(n, True)
        conv_trip(KT // 2 - 1, False)
        act.wait_ge(part_done, KT)
        for k in range(KT):
            act.wait_ge(cen, k + 1)
            if k >= 2:
                act.wait_ge(sq_used, k - 1)
            nc.scalar.activation(square[:, k % 2, :], acc[:, k, :], ACT.Square).then_inc(sq_ok, 1)
            if k < 6:
                split_hi(act, ring["conv_out"][k])
        act.wait_ge(sq_used, KT)
        nc.scalar.activation(conv_rs[:], banks(2), ACT.Sqrt, bias=eps_c[:, 0:1]).then_inc(var_sd, 1)
        for k in range(KT):
            act.wait_ge(nrm, k + 1)
            nc.scalar.activation(acc[:, k, :], acc[:, k, :], ACT.Silu, scale=cols[:, 3 * KT + k:3 * KT + k + 1],
                                 bias=cols[:, 4 * KT + k:4 * KT + k + 1]).then_inc(act_ok, 1)
            act.wait_ge(act_ok, k + 1)
            nc.scalar.copy(xt_hi[:, k, :], acc[:, k, :]).then_inc(act_hi, 1)
        out_act("conv_out", 6, ring["ffn1_first"])
        norm_act(act, "conv_out")
        ffn_act(act, 1)
        norm_act(act, "ffn1", turn=False)

    def ffn_dve(dve, layer):
        name = f"ffn{layer}"

        def prod(c, f):
            dve.wait_ge(w_used[c.slot], c.used)
            dve.wait_ge(silu_done[layer], f + 1)
            if not (isinstance(f, int) and f == 0):
                dve.wait_ge(h_lo[layer], f)
            nc.vector.tensor_tensor(h_f[:], banks(2), gate_act[:], ALU.mult).then_inc(h_prod[layer], 1)

        def lo(f, j):
            dve.wait_ge(h_hi[layer], f + 1)
            nc.vector.tensor_tensor(h_lo_t[:, j, :], h_f[:], h_hi_t[:, j, :], ALU.subtract).then_inc(h_lo[layer], 1)

        dve.sem_inc(y_free[name], 4)
        c = ring[name + "_first"]
        split_lo(dve, ring[name](0)[0])
        for f in range(2):
            prod(c[2 * f + 1], f)
            lo(f, f)
        dve.wait_ge(scaled, TT * NORM_OF[name])

        def trip(n, more):
            c = ring[name](n)
            for j in (1, 2, 3):
                split_lo(dve, c[j])
            for q in range(16):
                add_bank(dve, name, c[2], n, q)
            split_lo(dve, c[4])
            prod(c[3], 2 * n + 2)
            lo(2 * n + 2, 0)
            split_lo(dve, c[5])
            if more:
                split_lo(dve, ring[name](n + 1)[0])
            prod(c[5], 2 * n + 3)
            lo(2 * n + 3, 1)
        with dve.Fori(0, FG - 2) as n:
            trip(n, True)
        trip(FG - 2, False)
        for c in ring[name + "_last"]:
            split_lo(dve, c)

    def attention_dve(dve):
        for what, u, n in attention_order():
            i, kv = UNITS[u]
            par = u % 2
            if what == "logits":
                g, h = n, kv * G + n
                k0, nk = window(i)
                nc_ = min(N_CMP, 8 * i + 7)
                if g == 0 and u >= 2:
                    dve.wait_ge(pt_done, STEPS_OF[u - 2][1])
                if i == 0 and g == 0:
                    dve.wait_ge(nb_ok, kv + 1)
                pr = probs[par][:, g]
                for branch in range(2):
                    piece = (u * G + g) * 2 + branch
                    b = 2 * (piece % 2)
                    dve.wait_ge(s_done, piece + 1)
                    s = banks(b)
                    todo = [(1, pr[:, 0:(i + 1) * P], s[:, 0:(i + 1) * P], nbias[:, h, SEQ - (i + 1) * P:SEQ])]
                    if branch:
                        c0 = SEQ - P - P * i + CMP_BLOCK - 1
                        todo = [(2, pr[:, WIN0:WIN0 + nk], s[:, 0:nk], nbias[:, h, SEQ - nk:SEQ]),
                                (0, pr[:, CMP0:CMP0 + nc_], s[:, HALF + P:HALF + P + nc_],
                                 nbias[:, h, c0:c0 + CMP_STRIDE * (nc_ - 1) + 1:CMP_STRIDE])]
                    for col, out, logit, bias in todo:
                        nc.vector.tensor_tensor_reduce(out, logit, bias, 1.0, 3.0e38, ALU.add, ALU.min,
                                                       low[:, par, g, col:col + 1]).then_inc(s_min, 1)
            elif what == "norm":
                g, h = n, kv * G + n
                k0, nk = window(i)
                nc_ = min(N_CMP, 8 * i + 7)
                r = inv[:, par, g, :]
                dve.wait_ge(p_exp, 3 * (u * G + g) + 3)
                v_wait(dve, nc.vector.reciprocal(r, den[:, par, g, :]))
                if u == 0 and g == 0:
                    dve.wait_ge(gates_ok, 1)
                v_wait(dve, nc.vector.tensor_tensor(r, r, vg[:, i, 2 * P + 3 * h:2 * P + 3 * h + 3], ALU.mult))
                if i == 0:
                    v_wait(dve, nc.vector.tensor_tensor(r[:, 0:1], r[:, 0:1], row_ok[:], ALU.mult))
                pr = probs[par][:, g]
                for col, part in ((1, pr[:, 0:(i + 1) * P]), (2, pr[:, WIN0:WIN0 + nk]), (0, pr[:, CMP0:CMP0 + nc_])):
                    last = nc.vector.tensor_scalar(part, part, r[:, col:col + 1], None, ALU.mult)
                last.then_inc(p_norm, 1)
            elif what == "out":
                out = unit_out(u)
                for r in range(2):
                    dve.wait_ge(o_hi, 2 * u + 2)
                    to = (slice(r * DH, (r + 1) * DH), slice(4 + 2 * kv, 6 + 2 * kv), tile_cols(i))
                    nc.vector.tensor_tensor(xt_lo[to], out[:, r], xt_hi[to], ALU.subtract).then_inc(o_lo, 1)

    def vector_program(dve):
        for t in range(TT):
            turn_lo(dve, 0, t)
            if t in V_SPLITS:
                split_lo(dve, ring["v"][V_SPLITS.index(t)])
        third = BIAS_ROW // 3
        dve.wait_ge(small_t, 4)
        nc.vector.tensor_copy(ws_t[:].rearrange("p g t -> p (g t)"), ps[:, 4, :]).then_inc(small_c, 1)
        dve.wait_ge(small_t, 9)
        nc.vector.tensor_copy(cols[:], ps[:, 5, 0:40]).then_inc(small_c, 1)
        nc.vector.tensor_copy(pe_col[:].rearrange("p k j -> p (k j)"), ps[:, 5, 64:128]).then_inc(small_c, 1)
        for n, src in enumerate((ps[0:HEADS, 6, 0:third], ps[0:HEADS, 7, 0:third], ps[0:HEADS, 5, P:P + third])):
            nc.vector.tensor_scalar(bias_row[:, n * third:(n + 1) * third], src, -1.0, None, ALU.mult).then_inc(small_c, 1)
        for c in ring["vg"][:2]:
            split_lo(dve, c)
        for t in range(TT):
            dve.wait_ge(v_gelu, t + 1)
            v_wait(dve, nc.vector.bn_stats(v_stats[:, t, :], v_tok[:, t, :]))
            nc.vector.bn_aggr(v_mean[:, t, :], v_stats[:, t, :]).then_inc(v_mv, 1)
        feat = ring["feat"]
        split_lo(dve, ring["vg"][2])
        dve.wait_ge(v_sd, 1)
        v_wait(dve, nc.vector.reciprocal(v_rstd[:], v_rstd[:]))
        dve.wait_ge(bias_out, 16)
        for t in range(TT):
            if t < TT - 1:
                dve.wait_ge(vg_done, t + 1)
            else:
                dve.wait_ge(w_used[ring["vg"][2].slot], ring["vg"][2].used)
            nc.vector.tensor_copy(vg[:, t, :], ps[:, t % 4, 0:VG]).then_inc(vg_out, 1)
            x = v_tok[:, t, :]
            v_wait(dve, nc.vector.tensor_scalar(x, x, v_mean[:, t, 0:1], v_rstd[:, t:t + 1], ALU.subtract, ALU.mult))
            v_wait(dve, nc.vector.tensor_tensor(x, x, gmlp_g[:], ALU.mult))
            nc.vector.tensor_tensor(x, x, gmlp_b[:], ALU.add).then_inc(v_norm, 1)
            if t < 3:
                split_lo(dve, feat[t])
        for c in feat[3:8]:
            split_lo(dve, c)
        for g in range(GROUPS):
            for h in range(2):
                n = 2 * g + h
                dve.wait_ge(mix_done, n + 1)
                nc.vector.tensor_tensor(mix_a[:, g, h * HALF:(h + 1) * HALF].rearrange("p (m t) -> p m t", t=P),
                                        ps[:, 4 + n % 4, :].rearrange("p (m t) -> p m t", t=P),
                                        gmlp_bs[:, g:g + 1, :].broadcast_to([P, 4, P]), ALU.add).then_inc(mix_add, 1)
        for n in range(2, F_Q):
            dve.wait_ge(feat_act, n + 1)
            if n < F_U:
                for kv in range(KV_HEADS):
                    last = nc.vector.tensor_tensor(ks[DH:P, kv, n - 2, :], banks(2 * (n % 2))[kv * DH:(kv + 1) * DH, :],
                                                   ks[0:DH, kv, n - 2, :], ALU.subtract)
                last.then_inc(feat_dve, 1)
            else:
                x = mix_a[:, n - F_U, :]
                if n == F_U:
                    dve.wait_ge(mix_add, 2 * GROUPS)
                nc.vector.tensor_tensor(x, x, u_act[:], ALU.mult).then_inc(u_mul, 1)
            if n + 6 < len(feat):
                split_lo(dve, feat[n + 6])
        for g in range(GROUPS):
            dve.wait_ge(a_hi, g + 1)
            nc.vector.tensor_tensor(xt_lo[:, g, :], mix_a[:, g, :], xt_hi[:, g, :], ALU.subtract).then_inc(a_lo, 1)
        for kv in range(KV_HEADS):
            dve.wait_ge(cmp_act, 5 + kv)
            nc.vector.tensor_tensor(kc[DH:P, kv, :], ps[kv * DH:(kv + 1) * DH, 4, 0:64], kc[0:DH, kv, :],
                                    ALU.subtract).then_inc(cmp_dve, 1)
        for kv in range(KV_HEADS):
            nc.vector.tensor_copy(vc[:, kv, :], ps[0:64, 5 + kv, 0:DH]).then_inc(cmp_dve, 1)
        attention_dve(dve)
        dve.wait_ge(tap_t, 1)
        nc.vector.tensor_copy(taps[:], ps[:, 0, 0:KT * 32].rearrange("p (k j) -> p k j", j=32)[:, :, 0:CONV_W]).then_inc(tap_ok, 1)

        def out_dve(name, done, following, added=0):
            cs = ring[name]
            if name == "w_out":
                dve.sem_inc(y_free[name], 4)
            for c in cs[done:2]:
                split_lo(dve, c)
            for t in range(TT):
                if name == "w_out":
                    dve.wait_ge(scaled, t + 1)
                for q in range(max(added, 2 * t), 2 * t + 2):
                    add_bank(dve, name, cs[1], 0, q)
                if max(2, done) <= t + 2 < 6:
                    split_lo(dve, cs[t + 2])
            for n in (1, 2):
                for c in (cs[6:] if n == 1 else following[:2]):
                    split_lo(dve, c)
                for q in range(16):
                    add_bank(dve, name, cs[2 * n + 1], n, q)
            for c in following[2:]:
                split_lo(dve, c)
            norm_dve(dve, name, cs[7])

        out_dve("w_out", 0, ring["ffn0_first"])
        ffn_dve(dve, 0)
        for c in ring["conv_in"](0):
            split_lo(dve, c)
        norm_dve(dve, "ffn0", ring["ffn0_last"][1])
        dve.wait_ge(pad_ok, 2)

        def tap(n, m, j, first):
            out, x, w = tap_sum[:, m, :], conv_x[:, m, j:j + SEQ], tap_w[:, j:j + 1]
            if j == first:
                nc.vector.tensor_scalar(out, x, w, tap_w[:, CONV_W:], ALU.mult, ALU.add).then_inc(conv_v, 1)
            else:
                nc.vector.scalar_tensor_tensor(out=out, in0=x, scalar=w, in1=out, op0=ALU.mult, op1=ALU.add).then_inc(conv_v, 1)
            dve.wait_ge(conv_v, 2 * DVE_TAPS * n + (DVE_TAPS * m + j - first + 1))

        def add_part(T, m):
            dve.wait_ge(part_done, T + 1)
            nc.vector.tensor_tensor(acc[:, bass.ds(T, 1), :], tap_sum[:, m:m + 1, :], banks(4).unsqueeze(1),
                                    ALU.add).then_inc(part_added, 1)

        def conv_trip(n, more):
            c, nxt = ring["conv_in"](n), ring["conv_in"](n + 1) if more else None
            for j in range(2):
                dve.wait_ge(glu_sig, 2 * n + (j + 1))
                if not (isinstance(n, int) and n == 0):
                    dve.wait_ge(part_done, 2 * n + (j - 1))
                nc.vector.scalar_tensor_tensor(out=conv_x[:, j, PAD:], in0=banks(0),
                                               scalar=cols[:, bass.ds(2 * n + j, 1)], in1=glu_g[:],
                                               op0=ALU.add, op1=ALU.mult).then_inc(glu_free, 1)
                if more:
                    split_lo(dve, nxt[2 * j])
                    split_lo(dve, nxt[2 * j + 1])
                nc.vector.tensor_copy(tap_w[:, 0:CONV_W].unsqueeze(1), taps[:, bass.ds(2 * n + j, 1), :]).then_inc(tap_w_ok, 1)
                nc.vector.tensor_copy(tap_w[:, CONV_W:], cols[:, bass.ds(2 * n + (2 * KT + j), 1)]).then_inc(tap_w_ok, 1)
                dve.wait_ge(tap_w_ok, 4 * n + (2 * j + 2))
                dve.wait_ge(glu_free, 2 * n + (j + 1))
                first = PE_TAPS if more or j == 0 else 2 * PE_TAPS
                for m in range(first, CONV_W):
                    tap(n, j, m, first)
                    if m == first + 8 and not (isinstance(n, int) and 2 * n + j == 0):
                        add_part(2 * n + (j - 1), 1 - j)
        conv_trip(0, True)
        with dve.Fori(1, KT // 2 - 1) as n:
            conv_trip(n, True)
        conv_trip(KT // 2 - 1, False)
        add_part(KT - 1, 1)
        dve.wait_ge(mean_ok, 1)
        for k in range(KT):
            nc.vector.tensor_tensor(acc[:, k, :], acc[:, k, :], banks(6), ALU.subtract).then_inc(cen, 1)
            if k >= 2:
                split_lo(dve, ring["conv_out"][k - 2])
        dve.wait_ge(cen, KT)
        dve.sem_inc(y_free["conv_out"], 4)
        dve.wait_ge(outb_ok, TT)
        dve.wait_ge(var_sd, 1)
        v_wait(dve, nc.vector.reciprocal(conv_rs[:], conv_rs[:]))
        added = 0
        for k in range(KT + 1):
            if k < KT:
                nc.vector.tensor_tensor(acc[:, k, :], acc[:, k, :], conv_rs[:], ALU.mult).then_inc(nrm, 1)
            if k:
                dve.wait_ge(act_hi, k)
                nc.vector.tensor_tensor(xt_lo[:, k - 1, :], acc[:, k - 1, :], xt_hi[:, k - 1, :], ALU.subtract).then_inc(act_lo, 1)
            if k >= 3:
                for _ in range(2):
                    add_bank(dve, "conv_out", ring["conv_out"][1], 0, added)
                    added += 1
        out_dve("conv_out", 6, ring["ffn1_first"], added)
        ffn_dve(dve, 1)
        norm_dve(dve, "ffn1", ring["ffn1_last"][1], turn=False)

    def pool_program(pool):
        steps = [0]

        def g_wait(ins):
            ins.then_inc(g_step, 1)
            steps[0] += 1
            pool.wait_ge(g_step, steps[0])

        g_wait(nc.gpsimd.memset(ident[:], 0.0))
        nc.gpsimd.affine_select(out=ident[:], in_=ident[:], compare_op=ALU.not_equal, fill=1.0, base=0,
                                pattern=[[-1, P]], channel_multiplier=1).then_inc(const_ok, 1)
        pool.wait_ge(const_ok, 1)
        nc.gpsimd.memset(eps_c[:], EPS).then_inc(const_ok, 1)
        pool.wait_ge(const_ok, 2)
        load_small(pool)
        g_wait(nc.gpsimd.tensor_copy(ident_b[:], ident[:]))
        g_wait(nc.gpsimd.memset(far_mask[:], 0.0))
        g_wait(nc.gpsimd.affine_select(out=far_mask[:], in_=far_mask[:], compare_op=ALU.is_ge, fill=BIG, base=-1,
                                       pattern=[[1, P]], channel_multiplier=-1))
        g_wait(nc.gpsimd.memset(row_ok[:], 1.0))
        g_wait(nc.gpsimd.affine_select(out=row_ok[:], in_=row_ok[:], compare_op=ALU.is_ge, fill=0.0,
                                       base=1 - CMP_BLOCK, pattern=[[0, 1]], channel_multiplier=1))
        g_wait(nc.gpsimd.memset(hid[:], 0.0))
        pool.wait_ge(small_c, 1)
        nc.gpsimd.affine_select(out=ws_t[:], in_=ws_t[:], compare_op=ALU.is_ge, fill=0.0, base=0,
                                pattern=[[0, GROUPS], [1, P]], channel_multiplier=-1).then_inc(ws_ok, 1)
        pool.wait_ge(ws_ok, 1)

        def causal(kv):
            pool.wait_ge(nb_in[kv], 16)
            x = nbias[:, kv * G:(kv + 1) * G, SEQ - P:]
            nc.gpsimd.affine_select(out=x, in_=x, compare_op=ALU.is_ge, fill=BIG, base=0,
                                    pattern=[[0, G], [-1, P]], channel_multiplier=1).then_inc(nb_ok, 1)
            pool.wait_ge(nb_ok, kv + 1)

        causal(0)
        pool.wait_ge(cmp_done, 2)
        pool.wait_ge(feat_act, len(FEATURE_COLS))
        for u, (i, kv) in enumerate(UNITS):
            if u >= 2:
                pool.wait_ge(s_done, 2 * G * (u - 1))
            for r in range(2):
                src = q_t[r * DH:(r + 1) * DH, 2 * kv:2 * kv + 2, tile_cols(i)]
                dst = qs[:, u % 2].rearrange("p l (t r) q -> p l r t q", r=2)
                for half in range(2):
                    g_wait(nc.gpsimd.tensor_copy(dst[half * DH:(half + 1) * DH, 0, r], src))
                for half in range(2):
                    ins = nc.gpsimd.tensor_tensor(dst[half * DH:(half + 1) * DH, 1, r], src,
                                                  dst[r * DH:(r + 1) * DH, 0, r], ALU.subtract)
                    if r and half:
                        ins.then_inc(qs_ok, 1)
                        pool.wait_ge(qs_ok, u + 1)
                    else:
                        g_wait(ins)
            if u == 0:
                causal(1)
        pool.wait_ge(ln_done, 2 * TT)
        nc.gpsimd.memset(conv_x[:, 0, 0:PAD], 0.0).then_inc(pad_ok, 1)
        pool.wait_ge(pad_ok, 1)
        nc.gpsimd.memset(conv_x[:, 1, 0:PAD], 0.0).then_inc(pad_ok, 1)
        pool.wait_ge(pad_ok, 2)
        g_wait(nc.gpsimd.memset(ones_m[:], 1.0 / D))

        def diagonals(T):
            if T >= 2:
                pool.wait_ge(part_done, T - 1)
            tap0 = 0 if T < KT else PE_TAPS
            nc.gpsimd.tensor_tensor(diag[:, T % 2], ident[:].unsqueeze(1).broadcast_to([P, PE_TAPS, P]),
                                    taps[:, min(T, KT - 1), tap0:tap0 + PE_TAPS].unsqueeze(2).broadcast_to([P, PE_TAPS, P]),
                                    ALU.mult).then_inc(diag_ok, 1)
            pool.wait_ge(diag_ok, T + 1)
        for c in ring["ffn0_last"]:
            pool.wait_ge(w_used[c.slot], c.used)
        diagonals(0)
        diagonals(1)
        pool.wait_ge(outb_in, 16)
        for t in range(TT):
            pool.wait_ge(scaled, 2 * TT + t + 1)
            nc.gpsimd.tensor_tensor(resid[:, t, :], resid[:, t, :], out_b[:], ALU.add).then_inc(outb_ok, 1)
            pool.wait_ge(outb_ok, t + 1)
        for T in range(2, KT + 1):
            diagonals(T)

    with nc.Block() as block:
        @block.sync
        def _(sp):
            sync_program(sp)

        @block.scalar
        def _(act):
            scalar_program(act)

        @block.vector
        def _(dve):
            vector_program(dve)

        @block.tensor
        def _(pe):
            tensor_program(pe)

        @block.gpsimd
        def _(pool):
            pool_program(pool)


def bucket_onehot():
    n = np.maximum(np.arange(SEQ - 1, SEQ - 1 - BIAS_ROW, -1), 0)
    exact = N_BUCKETS // 2
    nf = np.maximum(n, 1).astype(np.float32)
    ratio = np.log(nf / np.float32(exact)) / np.float32(np.log(MAX_DISTANCE / exact))
    large = np.minimum(exact + (ratio * np.float32(N_BUCKETS - exact)).astype(np.int32), N_BUCKETS - 1)
    bucket = np.where(n < exact, n, large)
    return (bucket[None, :] == np.arange(N_BUCKETS)[:, None]).astype(np.float32)


def kernel(**inputs):
    import concourse.bacc as bacc
    from concourse.bass_utils import run_bass_kernel_spmd

    nc = bacc.Bacc("TRN2", target_bir_lowering=False, num_devices=1)
    arrays, aps = {}, {}
    for name, x in {**inputs, "bucket_onehot": bucket_onehot()}.items():
        x = np.ascontiguousarray(x)
        if x.shape[0] == 1:
            x = x.reshape(x.shape[1:])
        arrays[f"in_{name}"] = x
        aps[name] = nc.dram_tensor(f"in_{name}", x.shape, mybir.dt.from_np(x.dtype), kind="ExternalInput").ap()
    aps["out"] = nc.dram_tensor("out_y", [SEQ, D], F32, kind="ExternalOutput").ap()
    aps["bias_scratch"] = nc.dram_tensor("bias_scratch", [HEADS, P, BIAS_ROW], F32, kind="Internal").ap()
    build(nc, aps)
    result = run_bass_kernel_spmd(nc, [arrays], core_ids=[0])
    return result.results[0]["out_y"].reshape(1, SEQ, D)
```

```python
from contextlib import ExitStack

import numpy as np

import concourse.bass as bass
import concourse.mybir as mybir
from concourse.alu_op_type import AluOpType as ALU

F32 = mybir.dt.float32
F32R = mybir.dt.float32r
BF16 = mybir.dt.bfloat16
ACT = mybir.ActivationFunctionType

P = 128
D = 1024
SEQ = 1024
KT = D // P
TT = SEQ // P
HALF = 512
DEPTH = 2
ALPHA = float((2 * DEPTH) ** 0.25)
EPS = 1e-5

A_WIDTH = D // 2
GROUPS = 4
HEADS = 8
KV_HEADS = 2
G = HEADS // KV_HEADS
DH = 64
SCALE = DH ** -0.5
CMP_STRIDE = 16
CMP_BLOCK = 32
N_CMP = SEQ // CMP_STRIDE - 1
WINDOW = 512
N_BUCKETS = 32
MAX_DISTANCE = 1024
BIG = 1.0e30

KV0 = 2 * A_WIDTH + HEADS * DH
COL_KCMP, COL_VCMP, COL_KSLC, COL_VSLC, COL_KWIN, COL_VWIN = (KV0 + P * n for n in range(6))
COL_Q = 2 * A_WIDTH
GATES = 3 * HEADS
VG = 2 * P + GATES

FFN = 2816
FT = FFN // P
FG = FT // 2
CONV_W = 31
PAD = CONV_W - 1
PE_TAPS = 7
DVE_TAPS = CONV_W - PE_TAPS
LAST_PE_TAPS = [11, 13]

RING = 6
RAWS = 2
V_SPLITS = [2, 3, 6, 7]
BIAS_ROW = 1152
FEATURE_COLS = [COL_KCMP, COL_VCMP, COL_KSLC, COL_KWIN] + [n * P for n in range(GROUPS)] + [
    COL_Q + n * P for n in range(4)]
F_U, F_Q = 4, 8


class Chunk:

    def __init__(self, slot, raw, number, landed, before):
        self.slot, self.raw, self.number, self.landed, self.before = slot, raw, number, landed, before
        self.used = before + 1


class Stream:

    def __init__(self):
        self.count, self.uses, self.landed = 0, [0] * RING, [0] * RAWS

    def take(self, slots, dmas=1):
        out = []
        for slot in slots:
            raw = (self.count + 1) % RAWS
            self.landed[raw] += 16 * dmas
            self.count += 1
            out.append(Chunk(slot, raw, self.count, self.landed[raw], self.uses[slot]))
            self.uses[slot] += 1
        return out

    def loop(self, slots, trips):
        first = self.take(slots)
        for _ in range(trips - 1):
            self.take(slots)
        per = len(slots)
        assert per % RAWS == 0 and len(set(slots)) == per

        def trip(n):
            return [Chunk(c.slot, c.raw, per * n + c.number, (16 * per // RAWS) * n + c.landed, n + c.before)
                    for c in first]
        return trip


def plan():
    s = Stream()
    tail = [4, 5, 0, 1, 2, 3, 4, 5]
    r = {"v": s.take([0, 1, 2, 3]), "vg": s.take([4, 5, 0], 2), "feat": s.take([(1 + n) % RING for n in range(12)])}
    r["w_out"] = s.take(tail)
    for layer in range(DEPTH):
        if layer == 1:
            r["conv_in"] = s.loop([0, 1, 2, 3], KT // 2)
            r["conv_out"] = s.take(tail)
        r[f"ffn{layer}_first"] = s.take([0, 1, 2, 3])
        r[f"ffn{layer}"] = s.loop([0, 4, 5, 1, 2, 3], FG - 1)
        r[f"ffn{layer}_last"] = s.take([4, 5])
    return r


GROUP_COUNT = {"w_out": KT // 2, "ffn0": FG, "conv_out": KT // 2, "ffn1": FG}
NORM_OF = {"w_out": 1, "ffn0": 2, "conv_out": 3, "ffn1": 4}


UNITS = [(i, kv) for kv in range(KV_HEADS) for i in range(TT)]


def window(i):
    return max(0, i - WINDOW // P) * P, min(WINDOW // P + 1, i + 1) * P


STAGED = 2
LAG = 2
BUFS = LAG + 1
LEAD = 3


def key_tiles():
    steps, of = [], []
    for u, (i, _) in enumerate(UNITS):
        first = len(steps)
        steps += [(u, j * P, P, "sel", j) for j in range(i + 1)]
        k0, nk = window(i)
        steps += [(u, SEQ + j * P, P, "win", k0 // P + j) for j in range(nk // P)]
        steps.append((u, SEQ + WINDOW + P, min(N_CMP, 8 * i + 7), "cmp", 0))
        of.append((first, len(steps)))
    return steps, of


STEPS, STEPS_OF = key_tiles()


def attention_order():
    def softmax(u):
        out = []
        for g in range(G):
            out += [("logits", u, g)] + ([("norm", u, g - 1)] if g else [])
        return out + [("norm", u, G - 1)]

    order = softmax(0)
    for u in range(len(UNITS)):
        nxt = softmax(u + 1) if u + 1 < len(UNITS) else []
        first, last = STEPS_OF[u]
        m, n = 0, last - first
        for k in range(n):
            order.append(("step", u, first + k))
            to = min(len(nxt), -(-len(nxt) * (k + 1) // max(1, n - LEAD)))
            order += nxt[m:to]
            m = to
            if k == LAG and u:
                order.append(("out", u - 1, 0))
        order += nxt[m:]
    return order + [("out", len(UNITS) - 1, 0)]


def build(nc, a):
    ring = plan()
    at, here = {}, [(nc.sbuf_base + 63) // 64 * 64]

    def sb(name, shape, dt=F32, offset=None):
        size = int(np.prod(shape[1:])) * (2 if dt == BF16 else 4)
        if offset is None:
            offset = here[0]
            here[0] += (size + 31) // 32 * 32
        assert offset + size <= nc.sbuf_usable_end, name
        at[name] = offset
        return nc.alloc_sbuf_tensor_at(name, shape, dt, offset=offset)

    resid = sb("resid", [P, TT, D])
    xt_hi = sb("xt_hi", [P, KT, SEQ], F32R)
    xt_lo = sb("xt_lo", [P, KT, SEQ], F32R)
    wt_hi = sb("wt_hi", [P, RING, D], F32R)
    wt_lo = sb("wt_lo", [P, RING, D], F32R)
    wt_raw = sb("wt_raw", [P, RAWS, D])
    ident = sb("ident", [P, P])
    ident_b = sb("ident_b", [P, P], BF16)
    ones_m = sb("ones_m", [P, P])
    far_mask = sb("far_mask", [P, P], BF16)
    cols = sb("cols", [P, 40])
    eps_c = sb("eps_c", [P, 1])
    sums = sb("sums", [P, 2, 2])
    neg_mean = sb("neg_mean", [P, 2])
    sq_sum = sb("sq_sum", [P, 2])
    rstd = sb("rstd", [P, 2])
    v_mean = sb("v_mean", [P, TT, 2])
    v_rstd = sb("v_rstd", [P, TT])
    v_stats = sb("v_stats", [P, TT, 6])
    w2 = sb("w2", [P, 2, DH])
    pe_col = sb("pe_col", [P, 2, CMP_BLOCK])
    hid = sb("hid", [P, 2, 64])
    row_ok = sb("row_ok", [P, 1])
    q_t = sb("q_t", [P, 4, SEQ])
    ks = sb("ks", [P, KV_HEADS, 2, SEQ], F32R)
    vg = sb("vg", [P, TT, VG])
    cr = sb("cr", [P, 2, SEQ])
    low = sb("low", [P, 2, G, 3])
    den = sb("den", [P, 2, G, 3])
    inv = sb("inv", [P, 2, G, 3])
    kc = sb("kc", [P, KV_HEADS, 64], F32R)
    vc = sb("vc", [64, KV_HEADS, DH])
    o = at["q_t"]
    gmlp_g = sb("gmlp_g", [P, A_WIDTH], F32, o)
    gmlp_b = sb("gmlp_b", [P, A_WIDTH], F32, o + 2048)
    gmlp_bs = sb("gmlp_bs", [P, GROUPS, P], F32, o + 4096)
    ws = sb("ws", [P, GROUPS, P], F32, o + 6144)
    ws_t = sb("ws_t", [P, GROUPS, P], F32, o + 8192)
    onehot = sb("onehot", [N_BUCKETS, BIAS_ROW], F32, o + 10240)
    u_act = sb("u_act", [P, SEQ], F32, o + 10240)
    o = at["vg"]
    bias_row = sb("bias_row", [HEADS, BIAS_ROW], F32, o)
    rbias = sb("rbias", [N_BUCKETS, HEADS], F32, o + 4608)
    pe_row = sb("pe_row", [2 * CMP_BLOCK, P], F32, o + 4640)
    rows = sb("rows", [40, P], F32, o + 5152)
    qs = sb("qs", [P, 2, 2, G, P], F32R, at["cr"])
    o = at["resid"]
    mix_a = sb("mix_a", [P, GROUPS, SEQ], F32, o)
    v_tok = sb("v_tok", [P, TT, A_WIDTH], F32, o + 16384)
    w1 = sb("w1", [P, 2, CMP_BLOCK, DH], F32, o + 16384)
    nbias = sb("nbias", [P, HEADS, SEQ], F32, o)
    WIN0, CMP0 = SEQ, SEQ + WINDOW + P
    probs_o = sb("probs", [P, 2, G, CMP0 + 64], F32, at["wt_hi"] + G * P * 4)
    probs = [probs_o[:, (u + 1) % 2] for u in range(2)]
    assert all((u - i) % 2 == 0 for u, (i, _) in enumerate(UNITS))
    probs_t = [sb("probs_t0", [P, G, P]), sb("probs_t1", [P, G, P], F32, at["wt_hi"]),
               probs[0][:, :, SEQ - P:SEQ]]
    misc = at["q_t"]
    h_hi_t = sb("h_hi_t", [P, 2, SEQ], F32R, misc)
    h_lo_t = sb("h_lo_t", [P, 2, SEQ], F32R, misc + 8192)
    gate_act = sb("gate_act", [P, SEQ], F32, misc + 16384)
    h_f = sb("h_f", [P, SEQ], F32, misc + 20480)
    ln_g = sb("ln_g", [P, D], F32, misc + 33792)
    ln_b = sb("ln_b", [P, D], F32, misc + 37888)
    acc = sb("acc", [P, KT, SEQ], F32, misc)
    taps = sb("taps", [P, KT, CONV_W], F32, misc + 32768)
    conv_x = sb("conv_x", [P, 2, PAD + SEQ], F32, misc + 33792)
    glu_g = sb("glu_g", [P, SEQ], F32, misc + 42240)
    out_b = sb("out_b", [P, D], F32, misc + 46336)
    tap_rows = sb("tap_rows", [CONV_W, D], F32, misc + 45056)
    square = sb("square", [P, 2, SEQ], F32, misc + 42240)
    conv_rs = sb("conv_rs", [P, SEQ], F32, misc + 33792)
    tap_sum = sb("tap_sum", [P, 2, SEQ], F32, at["wt_lo"] + 4 * D * 4)
    tap_w = sb("tap_w", [P, CONV_W + 1], F32, at["wt_hi"] + 4 * D * 4 + 2 * PE_TAPS * P * 4)
    diag = sb("diag", [P, 2, PE_TAPS, P], F32, at["wt_hi"] + 4 * D * 4)
    ps = nc.alloc_psum_tensor("ps", [P, 8, HALF], F32)

    def sem(*names):
        made = [nc.alloc_semaphore(n) for n in names]
        return made if len(made) > 1 else made[0]

    def sems(name, keys):
        return {k: nc.alloc_semaphore(f"{name}_{k}") for k in keys}

    x_in, w_in, w_used = sems("x_in", range(TT)), sems("w_in", range(RAWS)), sems("w_used", range(RING))
    w_hi, w_lo = sem("w_hi", "w_lo")
    par_in, const_ok, small_t, small_c, ws_ok = sem("par_in", "const_ok", "small_t", "small_c", "ws_ok")
    bias_out, nb_ok, w1_in = sem("bias_out", "nb_ok", "w1_in")
    nb_in = sems("nb_in", range(KV_HEADS))
    ln_in, ln_mean, ln_sq, ln_sd, ln_done = sem("ln_in", "ln_mean", "ln_sq", "ln_sd", "ln_done")
    turned, turned_hi, turned_lo, scaled = sem("turned", "turned_hi", "turned_lo", "scaled")
    v_step, g_step = sem("v_step", "g_step")
    v_done, v_gelu, v_mv, v_sd, v_norm = sem("v_done", "v_gelu", "v_mv", "v_sd", "v_norm")
    vg_done, vg_out, feat_act, feat_dve = sem("vg_done", "vg_out", "feat_act", "feat_dve")
    u_mul, mix_done, mix_add, a_hi, a_lo, gates_ok = sem("u_mul", "mix_done", "mix_add", "a_hi", "a_lo", "gates_ok")
    cmp_done, cmp_act, cmp_dve, cmp_half, cr_ok = sem("cmp_done", "cmp_act", "cmp_dve", "cmp_half", "cr_ok")
    qs_hi, qs_first = sem("qs_hi", "qs_first")
    qs_ok, s_done, s_min, p_exp, p_norm = sem("qs_ok", "s_done", "s_min", "p_exp", "p_norm")
    pt_done, pt_copied, pv_done, o_hi, o_lo = sem("pt_done", "pt_copied", "pv_done", "o_hi", "o_lo")
    y_done, y_free = sems("y_done", GROUP_COUNT), sems("y_free", GROUP_COUNT)
    silu_done, h_prod, h_hi, h_lo = (sems(n, range(DEPTH)) for n in ("silu_done", "h_prod", "h_hi", "h_lo"))
    tap_in, tap_t, tap_ok, outb_in, outb_ok = sem("tap_in", "tap_t", "tap_ok", "outb_in", "outb_ok")
    glu_sig, glu_free, conv_v, pad_ok = sem("glu_sig", "glu_free", "conv_v", "pad_ok")
    diag_ok, part_done, part_added, tap_w_ok = sem("diag_ok", "part_done", "part_added", "tap_w_ok")
    mean_ok, cen, sq_ok, sq_used, var_sd, nrm, act_ok, act_hi, act_lo = sem(
        "mean_ok", "cen", "sq_ok", "sq_used", "var_sd", "nrm", "act_ok", "act_hi", "act_lo")
    out_done = sem("out_done")

    w_in_ap, w_out_ap = a["hyb_w_in"], a["hyb_w_out"]
    PARAMS = 18

    def banks(b, n=2):
        return ps[:, b:b + n, :].rearrange("p b c -> p (b c)")

    def tile_cols(t):
        return slice(t * P, (t + 1) * P)

    def raw(c):
        return wt_raw[:, c.raw, :]

    def load_chunk(sp, c, pieces):
        if not (isinstance(c.number, int) and c.number <= RAWS):
            sp.wait_ge(w_lo, c.number - RAWS)
        for dst, src in pieces:
            sp.dma_start(dst, src).then_inc(w_in[c.raw], 16)

    def split_hi(act, c):
        act.wait_ge(w_in[c.raw], c.landed)
        if not (isinstance(c.before, int) and c.before == 0):
            act.wait_ge(w_used[c.slot], c.before)
        nc.scalar.copy(wt_hi[:, c.slot, :], raw(c)).then_inc(w_hi, 1)

    def split_lo(dve, c):
        dve.wait_ge(w_hi, c.number)
        nc.vector.tensor_tensor(wt_lo[:, c.slot, :], raw(c), wt_hi[:, c.slot, :], ALU.subtract).then_inc(w_lo, 1)

    def feature_product(pe, c, b):
        pe.wait_ge(w_lo, c.number)
        for k in range(KT):
            hi, lo = wt_hi[:, c.slot, tile_cols(k)], wt_lo[:, c.slot, tile_cols(k)]
            for n, (w, x) in enumerate(((hi, xt_hi), (hi, xt_lo), (lo, xt_hi))):
                for h in range(2):
                    last = nc.tensor.matmul(ps[:, b + h, :], w, x[:, k, h * HALF:(h + 1) * HALF],
                                            start=(k == 0 and n == 0), stop=(k == KT - 1 and n == 2))
        last.then_inc(w_used[c.slot], 1)

    def token_product(pe, name, cs, left, group, turn=False, ready=None):
        def product(q, j):
            c, bank = cs[j], ps[:, 4 + q % 4, :]
            cols_h = slice((q % 2) * HALF, (q % 2 + 1) * HALF)
            lh, ll = (x[:, tile_cols(q // 2)] for x in left[j])
            rh, rl = wt_hi[:, c.slot, cols_h], wt_lo[:, c.slot, cols_h]
            if j == 0:
                pe.wait_ge(y_free[name], 16 * group + (q + 1))
            nc.tensor.matmul(bank, lh, rh, start=(j == 0), stop=False)
            nc.tensor.matmul(bank, lh, rl, start=False, stop=False)
            last = nc.tensor.matmul(bank, ll, rh, start=False, stop=(j == 1))
            if q == 15:
                last.then_inc(w_used[c.slot], 1)
            elif j == 1:
                last.then_inc(y_done[name], 1)

        together = 4 if ready else 0
        if ready:
            pe.wait_ge(ready[0], ready[1])
            pe.wait_ge(w_lo, cs[0].number)
            for q in range(together):
                product(q, 0)
            pe.wait_ge(ready[0], ready[2])
        pe.wait_ge(w_lo, cs[1].number)
        for q in range(16):
            if q >= together:
                product(q, 0)
            product(q, 1)
            if turn and q % 2 and q // 2 >= 2:
                turn_tile(pe, NORM_OF[name], q // 2 - 2)
        if turn:
            turn_tile(pe, NORM_OF[name], TT - 2)
            turn_tile(pe, NORM_OF[name], TT - 1)
            pe.wait_ge(turned_lo, TT * (NORM_OF[name] + 1))

    def add_bank(dve, name, c, group, q, total=None):
        if q < 15:
            dve.wait_ge(y_done[name], 15 * group + (q + 1))
        else:
            dve.wait_ge(w_used[c.slot], c.used)
        r = resid[:, q // 2, (q % 2) * HALF:(q % 2 + 1) * HALF]
        if total is None:
            nc.vector.tensor_tensor(r, r, ps[:, 4 + q % 4, :], ALU.add).then_inc(y_free[name], 1)
        else:
            nc.vector.tensor_tensor_reduce(r, r, ps[:, 4 + q % 4, :], 1.0, 0.0, ALU.add, ALU.add,
                                           total).then_inc(y_free[name], 1)

    steps_of_v = [0]

    def v_wait(dve, *made):
        for ins in made:
            ins.then_inc(v_step, 1)
        steps_of_v[0] += len(made)
        dve.wait_ge(v_step, steps_of_v[0])

    def turn_tile(pe, event, t):
        if event == 0:
            pe.wait_ge(x_in[t], 16)
        else:
            pe.wait_ge(ln_done, TT * (event - 1) + t + 1)
        if t >= 2:
            pe.wait_ge(turned_lo, TT * event + t - 1)
        for k in range(KT):
            last = nc.tensor.transpose(ps[:, 2 * (t % 2) + k // 4, tile_cols(k % 4)], resid[:, t, tile_cols(k)], ident[:])
        last.then_inc(turned, 1)

    def turned_view(t):
        return ps[:, 2 * (t % 2):2 * (t % 2) + 2, :].rearrange("p b (k c) -> p (b k) c", c=P)

    def turn_hi(act, event, t):
        act.wait_ge(turned, TT * event + t + 1)
        nc.scalar.copy(xt_hi[:, :, tile_cols(t)], turned_view(t)).then_inc(turned_hi, 1)

    def turn_lo(dve, event, t):
        dve.wait_ge(turned_hi, TT * event + t + 1)
        nc.vector.tensor_tensor(xt_lo[:, :, tile_cols(t)], turned_view(t), xt_hi[:, :, tile_cols(t)],
                                ALU.subtract).then_inc(turned_lo, 1)

    def scale_tile(act, t):
        nc.scalar.mul(resid[:, t, :], resid[:, t, :], ALPHA).then_inc(scaled, 1)

    def amid_norm(chunks):
        first = chunks[:-2]
        return {**{4 + 2 * n: [c] for n, c in enumerate(first)}, TT + 2: chunks[-2:]}

    def norm_act(act, name, turn=True, chunks=()):
        splits = amid_norm(chunks)
        e = NORM_OF[name]
        for t in range(TT + 2):
            if t < TT:
                b, n = t % 2, TT * (e - 1) + t
                act.wait_ge(ln_mean, n + 1)
                if t >= 2:
                    act.wait_ge(ln_done, n - 1)
                nc.scalar.activation(gate_act[:], resid[:, t, :], ACT.Square, bias=neg_mean[:, b:b + 1],
                                     accum_out=sq_sum[:, b:b + 1]).then_inc(ln_sq, 1)
                act.wait_ge(ln_sq, n + 1)
                nc.scalar.activation(rstd[:, b:b + 1], sq_sum[:, b:b + 1], ACT.Sqrt, bias=eps_c[:, 0:1],
                                     scale=1.0 / D).then_inc(ln_sd, 1)
            if t >= 2 and turn:
                turn_hi(act, e, t - 2)
                scale_tile(act, t - 2)
            for c in splits.get(t, ()):
                split_hi(act, c)
        for c in splits[TT + 2]:
            split_hi(act, c)

    def norm_dve(dve, name, c, turn=True, chunks=()):
        e = NORM_OF[name]
        splits = amid_norm(chunks)
        for t in range(TT + 2):
            if t < TT:
                b = t % 2
                for h in range(2):
                    add_bank(dve, name, c, GROUP_COUNT[name] - 1, 2 * t + h, sums[:, b, h:h + 1])
                dve.wait_ge(y_free[name], 4 + 16 * (GROUP_COUNT[name] - 1) + 2 * t + 2)
                nc.vector.tensor_scalar(neg_mean[:, b:b + 1], sums[:, b, 0:1], sums[:, b, 1:2], -1.0 / D,
                                        ALU.add, ALU.mult).then_inc(ln_mean, 1)
            if 1 <= t <= TT:
                b, x, n = (t - 1) % 2, resid[:, t - 1, :], TT * (e - 1) + t - 1
                if t == 1:
                    dve.wait_ge(ln_in, 32 * e)
                dve.wait_ge(ln_sd, n + 1)
                nc.vector.reciprocal(rstd[:, b:b + 1], rstd[:, b:b + 1]).then_inc(v_step, 1)
                dve.wait_ge(ln_mean, n + 1)
                nc.vector.scalar_tensor_tensor(out=x, in0=x, scalar=neg_mean[:, b:b + 1], in1=ln_g[:],
                                               op0=ALU.add, op1=ALU.mult).then_inc(v_step, 1)
                steps_of_v[0] += 2
                dve.wait_ge(v_step, steps_of_v[0])
                nc.vector.scalar_tensor_tensor(out=x, in0=x, scalar=rstd[:, b:b + 1], in1=ln_b[:],
                                               op0=ALU.mult, op1=ALU.add).then_inc(ln_done, 1)
            if t >= 2 and turn:
                turn_lo(dve, e, t - 2)
            for chunk in splits.get(t, ()):
                split_lo(dve, chunk)
        for chunk in splits[TT + 2]:
            split_lo(dve, chunk)

    def load_small(pool):
        def par(dst, src):
            pool.dma_start(dst, src).then_inc(par_in, 16)
        par(ws[:], a["gmlp_w_s"].rearrange("g t s -> t g s"))
        par(rbias[:], a["rel_bias"])
        par(onehot[:], a["bucket_onehot"])
        for dst, name, n in ((gmlp_g[:], "gmlp_ln_g", A_WIDTH), (gmlp_b[:], "gmlp_ln_b", A_WIDTH),
                             (gmlp_bs[:], "gmlp_b_s", A_WIDTH)):
            src = bass.AP(a[name].tensor, 0, [[0, P], [1, n]])
            par(dst.rearrange("p g t -> p (g t)") if name == "gmlp_b_s" else dst, src)
        for kv, n in enumerate("kv"):
            for h in range(2):
                par(pe_row[kv * CMP_BLOCK:(kv + 1) * CMP_BLOCK, h * DH:(h + 1) * DH], a[f"cmp_pe_{n}"])
                par(w2[h * DH:(h + 1) * DH, kv, :], a[f"cmp_w2_{n}"])
        r = 0
        for n, k in (("conv_b_in", 2 * KT), ("conv_dw_b", KT)):
            par(rows[r:r + k, :], a[n].rearrange("(k p) -> k p", p=P))
            r += k
        par(rows[r:r + KT, :], a["conv_ln_g"].rearrange("(k p) -> k p", p=P))
        par(rows[r + KT:r + 2 * KT, :], a["conv_ln_b"].rearrange("(k p) -> k p", p=P))

    def norm_params(sp, name):
        layer, kind = divmod(NORM_OF[name] - 1, 2)
        for dst, n in ((ln_g, "g"), (ln_b, "b")):
            src = bass.AP(a[f"norm_{('mix', 'ffn')[kind]}_{n}"].tensor, layer * D, [[0, P], [1, D]])
            sp.dma_start(dst[:], src).then_inc(ln_in, 16)

    def ffn_loads(sp, layer):
        wg, wu, wd = (a[n][layer] for n in ("ffn_w_gate", "ffn_w_up", "ffn_w_down"))

        def columns(c, w, f):
            load_chunk(sp, c, [(raw(c).rearrange("p (k n) -> p k n", k=KT),
                                w[:, bass.ds(f * P, P)].rearrange("(k p) n -> p k n", p=P))])

        def down(c, f):
            load_chunk(sp, c, [(raw(c), wd[bass.ds(f * P, P), :])])

        c = ring[f"ffn{layer}_first"]
        columns(c[0], wg, 0)
        columns(c[1], wu, 0)
        columns(c[2], wg, 1)
        columns(c[3], wu, 1)
        if layer == 1:
            sp.wait_ge(act_ok, KT)
            norm_params(sp, "conv_out")
        sp.wait_ge(ln_done, TT * (2 * layer + 1))
        norm_params(sp, f"ffn{layer}")
        with sp.Fori(0, FG - 1) as n:
            c = ring[f"ffn{layer}"](n)
            columns(c[0], wg, 2 * n + 2)
            down(c[1], 2 * n)
            down(c[2], 2 * n + 1)
            columns(c[3], wu, 2 * n + 2)
            columns(c[4], wg, 2 * n + 3)
            columns(c[5], wu, 2 * n + 3)
        c = ring[f"ffn{layer}_last"]
        down(c[0], FT - 2)
        down(c[1], FT - 1)

    def sync_program(sp):
        def v_chunk(j):
            c, src = ring["v"][j], w_in_ap[2 * j * P:(2 * j + 2) * P, A_WIDTH:2 * A_WIDTH]
            load_chunk(sp, c, [(raw(c).rearrange("p (k n) -> p k n", k=2), src.rearrange("(k p) n -> p k n", p=P))])

        for t in range(TT):
            sp.dma_start(resid[:, t, :], a["x"][tile_cols(t), :]).then_inc(x_in[t], 16)
            if t in (3, 4):
                v_chunk(t - 3)
        v_chunk(2)
        v_chunk(3)
        for j, c in enumerate(ring["vg"]):
            nk = min(3, KT - 3 * j)
            dst = raw(c)[:, 0:nk * VG].rearrange("p (k n) -> p k n", k=nk)
            k0 = slice(3 * j * P, (3 * j + nk) * P)
            load_chunk(sp, c, [
                (dst[:, :, 0:P], w_in_ap[k0, COL_VSLC:COL_VSLC + P].rearrange("(k p) n -> p k n", p=P)),
                (dst[:, :, P:VG], w_in_ap[k0, COL_VWIN:COL_VWIN + P + GATES].rearrange("(k p) n -> p k n", p=P))])
        for n, (c, col) in enumerate(zip(ring["feat"], FEATURE_COLS)):
            load_chunk(sp, c, [(raw(c).rearrange("p (k n) -> p k n", k=KT),
                                w_in_ap[:, col:col + P].rearrange("(k p) n -> p k n", p=P))])
            if n == 7:
                sp.wait_ge(mix_done, 8)
                for kv, name in enumerate("kv"):
                    for h in range(2):
                        sp.dma_start(w1[h * DH:(h + 1) * DH, kv, :, :],
                                     a[f"cmp_w1_{name}"].rearrange("(j d) m -> d j m", d=DH)).then_inc(w1_in, 16)
        sp.wait_ge(bias_out, 16)
        sp.wait_ge(a_lo, GROUPS)
        for h0 in (0, G):
            if h0:
                sp.wait_ge(cmp_done, 3)
            src = bass.AP(a["bias_scratch"].tensor, h0 * P * BIAS_ROW + P - 1,
                          [[BIAS_ROW - 1, P], [P * BIAS_ROW, G], [1, SEQ]])
            sp.dma_start(nbias[:, h0:h0 + G, :], src).then_inc(nb_in[h0 // G], 16)
        sp.wait_ge(s_min, 3 * G * len(UNITS))
        sp.dma_start(tap_rows[:], a["conv_dw_w"]).then_inc(tap_in, 16)
        for k in range(TT):
            sp.dma_start(resid[:, k, :], a["x"][tile_cols(k), :]).then_inc(x_in[k], 16)
        sp.wait_ge(pt_done, STEPS_OF[-2][1])
        for k, c in enumerate(ring["w_out"]):
            if k == 1:
                sp.wait_ge(pv_done, len(STEPS))
            load_chunk(sp, c, [(raw(c), w_out_ap[tile_cols(k), :])])
            if k == 1:
                norm_params(sp, "w_out")
        sp.wait_ge(tap_ok, 1)
        sp.dma_start(out_b[:], bass.AP(a["conv_b_out"].tensor, 0, [[0, P], [1, D]])).then_inc(outb_in, 16)
        ffn_loads(sp, 0)
        with sp.Fori(0, KT // 2) as n:
            for j, c in enumerate(ring["conv_in"](n)):
                src = a["conv_w_in"][:, bass.ds((j % 2) * D + (2 * n + j // 2) * P, P)]
                load_chunk(sp, c, [(raw(c).rearrange("p (k n) -> p k n", k=KT), src.rearrange("(k p) n -> p k n", p=P))])
        for k, c in enumerate(ring["conv_out"]):
            load_chunk(sp, c, [(raw(c), a["conv_w_out"][tile_cols(k), :])])
        ffn_loads(sp, 1)
        for t in range(TT):
            sp.wait_ge(ln_done, 3 * TT + t + 1)
            sp.dma_start(a["out"][tile_cols(t), :], resid[:, t, :]).then_inc(out_done, 16)
        sp.wait_ge(out_done, 16 * TT)

    def ffn_pe(pe, layer):
        name = f"ffn{layer}"

        def gate(c, f):
            if not (isinstance(f, int) and f == 0):
                pe.wait_ge(silu_done[layer], f)
            feature_product(pe, c, 0)

        def up(c, f):
            if not (isinstance(f, int) and f == 0):
                pe.wait_ge(h_prod[layer], f)
            feature_product(pe, c, 2)

        def down(cs, group, turn=False, last=False):
            h = [(h_hi_t[:, j], h_lo_t[:, j]) for j in range(2)]
            if last:
                token_product(pe, name, cs, h, group, turn, (h_lo[layer], 2 * group + 1, 2 * group + 2))
            else:
                pe.wait_ge(h_lo[layer], 2 * group + 2)
                token_product(pe, name, cs, h, group)

        c = ring[name + "_first"]
        for f in range(2):
            gate(c[2 * f], f)
            up(c[2 * f + 1], f)

        def trip(n):
            c = ring[name](n)
            gate(c[0], 2 * n + 2)
            down(c[1:3], n)
            up(c[3], 2 * n + 2)
            gate(c[4], 2 * n + 3)
            up(c[5], 2 * n + 3)
        with pe.Fori(0, FG - 2) as n:
            trip(n)
        trip(FG - 2)
        down(ring[name + "_last"], FG - 1, turn=layer == 0, last=True)

    def attention_pe(pe):
        def logits(u, g, branch):
            i, kv = UNITS[u]
            piece = (u * G + g) * 2 + branch
            b = 2 * (piece % 2)
            if g == 0 and branch == 0:
                pe.wait_ge(qs_first if u < STAGED else qs_ok, u + 1 if u < STAGED else u - STAGED + 1)
            if piece >= 2:
                pe.wait_ge(s_min, 3 * ((piece - 2) // 2) + (1 if branch == 0 else 3))
            qh, ql = qs[:, u % 2, 0, g, :], qs[:, u % 2, 1, g, :]
            k0, nk = (0, (i + 1) * P) if branch == 0 else window(i)
            for c0 in range(0, nk, HALF):
                n = min(HALF, nk - c0)
                out, keys = ps[:, b + c0 // HALF, 0:n], ks[:, kv, branch, k0 + c0:k0 + c0 + n]
                far = branch == 1 and c0 == 0 and nk > WINDOW
                nc.tensor.matmul(out, qh, keys, start=True, stop=False)
                last = nc.tensor.matmul(out, ql, keys, start=False, stop=not far)
                if far:
                    nc.tensor.matmul(ps[:, b, 0:P], ident_b[:], far_mask[:], start=False, stop=True)
            if branch == 1:
                n = 8 * i + 8
                out = ps[:, b + 1, P:P + n]
                nc.tensor.matmul(out, qh, kc[:, kv, 0:n], start=True, stop=False)
                last = nc.tensor.matmul(out, ql, kc[:, kv, 0:n], start=False, stop=True)
            last.then_inc(s_done, 1)

        def turn(s):
            u, col, n, _, _ = STEPS[s]
            if s == STEPS_OF[u][0]:
                pe.wait_ge(p_norm, G * (u + 1))
            if s >= BUFS:
                copied(s - BUFS)
            for g in range(G):
                last = nc.tensor.transpose(ps[0:n, 4 + s % BUFS, tile_cols(g)], probs[u % 2][:, g, col:col + n], ident[:])
            last.then_inc(pt_done, 1)

        def copied(s):
            pe.wait_ge(pt_copied, s + 1)

        def values(s):
            u, _, n, branch, j = STEPS[s]
            _, kv = UNITS[u]
            copied(s)
            if s == STEPS_OF[u][0] and u >= 2:
                pe.wait_ge(o_lo, 2 * (u - 1))
            c0 = (P if branch == "win" else 0) + kv * DH
            v = vc[0:n, kv, :] if branch == "cmp" else vg[:, j, c0:c0 + DH]
            half = slice((u % 2) * DH, (u % 2 + 1) * DH)
            nc.tensor.matmul(ps[half, 7, :], v, probs_t[s % BUFS][0:n], start=(s == STEPS_OF[u][0]),
                             stop=(s == STEPS_OF[u][1] - 1)).then_inc(pv_done, 1)

        for what, u, n in attention_order():
            if what == "logits":
                logits(u, n, 0)
                logits(u, n, 1)
            elif what == "step":
                turn(n)
                if n >= LAG:
                    values(n - LAG)
        for n in range(len(STEPS) - LAG, len(STEPS)):
            values(n)

    def tensor_program(pe):
        pe.wait_ge(const_ok, 2)
        for t in range(TT):
            turn_tile(pe, 0, t)
        third = BIAS_ROW // 3

        def small_ones():
            pe.wait_ge(turned_lo, TT)
            pe.wait_ge(par_in, 16 * PARAMS)
            for g in range(GROUPS):
                nc.tensor.transpose(ps[:, 0, tile_cols(g)], ws[:, g, :], ident[:]).then_inc(small_t, 1)
            nc.tensor.transpose(ps[:, 1, 0:40], rows[:], ident[0:40, 0:40]).then_inc(small_t, 1)
            nc.tensor.transpose(ps[:, 1, 64:128], pe_row[:], ident[0:64, 0:64]).then_inc(small_t, 1)
            for n, out in enumerate((ps[0:HEADS, 2, 0:third], ps[0:HEADS, 3, 0:third], ps[0:HEADS, 1, P:P + third])):
                nc.tensor.matmul(out, rbias[:], onehot[:, n * third:(n + 1) * third], start=True, stop=True).then_inc(small_t, 1)

        c = ring["v"]
        for t in range(TT):
            pe.wait_ge(turned_lo, t + 1)
            if t >= 4:
                pe.wait_ge(v_gelu, t - 3)
            for k in range(KT):
                if t == 0 and k % 2 == 0:
                    pe.wait_ge(w_lo, c[k // 2].number)
                s, cut = c[k // 2].slot, slice((k % 2) * HALF, (k % 2 + 1) * HALF)
                xh, xl = xt_hi[:, k, tile_cols(t)], xt_lo[:, k, tile_cols(t)]
                out = ps[:, 4 + t % 4, :]
                nc.tensor.matmul(out, xh, wt_hi[:, s, cut], start=(k == 0), stop=False)
                nc.tensor.matmul(out, xh, wt_lo[:, s, cut], start=False, stop=False)
                last = nc.tensor.matmul(out, xl, wt_hi[:, s, cut], start=False, stop=(k == KT - 1))
                if t == TT - 1 and k % 2:
                    last.then_inc(w_used[s], 1)
            if t < TT - 1:
                last.then_inc(v_done, 1)
            if t == 2:
                small_ones()
        pe.wait_ge(small_c, 6)
        c = ring["vg"]
        pe.wait_ge(w_lo, c[1].number)

        def vg_product(t, ks_):
            for k in ks_:
                s, cut = c[k // 3].slot, slice((k % 3) * VG, (k % 3 + 1) * VG)
                xh, xl = xt_hi[:, k, tile_cols(t)], xt_lo[:, k, tile_cols(t)]
                out = ps[:, t % 4, 0:VG]
                nc.tensor.matmul(out, xh, wt_hi[:, s, cut], start=(k == 0), stop=False)
                nc.tensor.matmul(out, xh, wt_lo[:, s, cut], start=False, stop=False)
                last = nc.tensor.matmul(out, xl, wt_hi[:, s, cut], start=False, stop=(k == KT - 1))
                if t == TT - 1 and k in (2, 5, 7):
                    last.then_inc(w_used[s], 1)
            if t < TT - 1 and k == KT - 1:
                last.then_inc(vg_done, 1)
        for t in range(4):
            vg_product(t, range(6))
        pe.wait_ge(w_lo, c[2].number)
        for t in range(4):
            vg_product(t, range(6, KT))
        for t in range(4, TT):
            pe.wait_ge(vg_out, t - 3)
            vg_product(t, range(KT))

        def features(n):
            if n < 2:
                pe.wait_ge(vg_out, TT - 2 + 2 * n)
            if n >= 2:
                pe.wait_ge(feat_act, n - 1)
            if n in (4, 5):
                pe.wait_ge(feat_dve, n - 3)
            feature_product(pe, ring["feat"][n], 2 * (n % 2))
        features(0)
        features(1)
        pe.wait_ge(v_norm, TT)
        pe.wait_ge(ws_ok, 1)
        for g in range(GROUPS):
            for h in range(2):
                n = 2 * g + h
                if n >= 4:
                    pe.wait_ge(mix_add, n - 3)
                for m in range(4):
                    last = nc.tensor.matmul(ps[:, 4 + n % 4, tile_cols(m)], v_tok[:, 4 * h + m, tile_cols(g)],
                                            ws_t[:, g, :], start=True, stop=True)
                last.then_inc(mix_done, 1)
        for n in range(2, len(FEATURE_COLS)):
            features(n)
        pe.wait_ge(w1_in, 64)
        pe.wait_ge(feat_act, len(FEATURE_COLS))
        for half in range(2):
            for kv in range(2):
                pe.wait_ge(cr_ok, 2 * half + kv + 1)
                for h in range(KV_HEADS):
                    part = slice(h * DH, (h + 1) * DH)
                    for j in range(half * CMP_STRIDE, (half + 1) * CMP_STRIDE):
                        last = nc.tensor.matmul(ps[part, kv, 0:N_CMP], w1[part, kv, j, :],
                                                cr[part, kv, j:j + CMP_STRIDE * (N_CMP - 1) + 1:CMP_STRIDE],
                                                start=(j == 0), stop=(j == CMP_BLOCK - 1))
                last.then_inc(cmp_done if half else cmp_half, 1)
        pe.wait_ge(cmp_act, 2)
        for h in range(KV_HEADS):
            part = slice(h * DH, (h + 1) * DH)
            nc.tensor.matmul(ps[part, 4, 0:64], w2[part, 0, :], hid[part, 0, :], start=True, stop=True)
            last = nc.tensor.matmul(ps[0:64, 5 + h, 0:DH], hid[part, 1, :], w2[part, 1, :], start=True, stop=True)
        last.then_inc(cmp_done, 1)
        pe.wait_ge(cmp_act, 4)
        pe.wait_ge(cmp_dve, 4)
        attention_pe(pe)
        pe.wait_ge(o_lo, 2 * len(UNITS))
        pe.wait_ge(a_lo, GROUPS)

        def out_product(name):
            for n in range(GROUP_COUNT[name]):
                ready = None
                if n == 0:
                    ready = (o_lo, 2 * len(UNITS), 2 * len(UNITS)) if name == "w_out" else (act_lo, 1, 2)
                elif name == "conv_out":
                    pe.wait_ge(act_lo, 2 * n + 2)
                token_product(pe, name, ring[name][2 * n:2 * n + 2],
                              [(xt_hi[:, k], xt_lo[:, k]) for k in (2 * n, 2 * n + 1)], n,
                              n == GROUP_COUNT[name] - 1, ready)
        pe.wait_ge(tap_in, 16)
        for k in range(KT):
            last = nc.tensor.transpose(ps[:, 0, k * 32:k * 32 + CONV_W], tap_rows[:, tile_cols(k)], ident[0:CONV_W, 0:CONV_W])
        last.then_inc(tap_t, 1)
        out_product("w_out")
        ffn_pe(pe, 0)
        conv = ring["conv_in"]

        def values_and_gates(T, c):
            if T:
                pe.wait_ge(glu_free, T)
            feature_product(pe, c[0], 0)
            feature_product(pe, c[1], 2)

        def tap_products(T, count=PE_TAPS, sets=None):
            if T:
                pe.wait_ge(part_added, T)
            pe.wait_ge(glu_free, T + 1)
            for n, number in enumerate(sets or [T]):
                pe.wait_ge(diag_ok, number + 1)
                for j in range(n * PE_TAPS, min(count, (n + 1) * PE_TAPS)):
                    for h in range(2):
                        last = nc.tensor.matmul(ps[:, 4 + h, :], diag[:, number % 2, j % PE_TAPS, :],
                                                conv_x[:, T % 2, h * HALF + j:(h + 1) * HALF + j],
                                                start=(j == 0), stop=(j == count - 1))
                last.then_inc(part_done, 1)

        def mean_share(T, first=False, last=False):
            pe.wait_ge(part_added, T + 1)
            for h in range(2):
                ins = nc.tensor.matmul(ps[:, 6 + h, :], ones_m[:], acc[:, T, h * HALF:(h + 1) * HALF],
                                       start=first, stop=last)
            if last:
                ins.then_inc(mean_ok, 1)

        for T in range(KT):
            values_and_gates(T, conv(T // 2)[2 * (T % 2):2 * (T % 2) + 2])
            if T >= 2:
                mean_share(T - 2, first=T == 2)
            if 1 <= T < KT - 1:
                tap_products(T - 1)
        tap_products(KT - 2, LAST_PE_TAPS[0], [KT - 2, KT - 1])
        tap_products(KT - 1, LAST_PE_TAPS[1], [KT, KT + 1])
        mean_share(KT - 2)
        mean_share(KT - 1, last=True)
        for k in range(KT):
            pe.wait_ge(sq_ok, k + 1)
            for h in range(2):
                last = nc.tensor.matmul(ps[:, 2 + h, :], ones_m[:], square[:, k % 2, h * HALF:(h + 1) * HALF],
                                        start=(k == 0), stop=(k == KT - 1))
            last.then_inc(sq_used, 1)
        out_product("conv_out")
        ffn_pe(pe, 1)

    def ffn_act(act, layer):
        name = f"ffn{layer}"

        def silu(c, f):
            act.wait_ge(w_used[c.slot], c.used)
            if not (isinstance(f, int) and f == 0):
                act.wait_ge(h_prod[layer], f)
            nc.scalar.activation(gate_act[:], banks(0), ACT.Silu).then_inc(silu_done[layer], 1)

        def hi(f, j):
            act.wait_ge(h_prod[layer], f + 1)
            nc.scalar.copy(h_hi_t[:, j, :], h_f[:]).then_inc(h_hi[layer], 1)

        c = ring[name + "_first"]
        silu(c[0], 0)
        split_hi(act, ring[name](0)[0])
        hi(0, 0)
        silu(c[2], 1)
        hi(1, 1)

        def trip(n, more):
            c = ring[name](n)
            for j in (1, 2, 3):
                split_hi(act, c[j])
            silu(c[0], 2 * n + 2)
            split_hi(act, c[4])
            hi(2 * n + 2, 0)
            split_hi(act, c[5])
            silu(c[4], 2 * n + 3)
            for c in [ring[name](n + 1)[0]] if more else ring[name + "_last"]:
                split_hi(act, c)
            hi(2 * n + 3, 1)
        with act.Fori(0, FG - 2) as n:
            trip(n, True)
        trip(FG - 2, False)

    def query_parts(u):
        i, kv = UNITS[u]
        dst = qs[:, u % 2].rearrange("p l (t r) q -> p l r t q", r=2)
        out = []
        for r in range(2):
            src = q_t[r * DH:(r + 1) * DH, 2 * kv:2 * kv + 2, tile_cols(i)]
            for half in range(2):
                to = slice(half * DH, (half + 1) * DH)
                out.append((src, dst[to, 0, r], dst[to, 1, r], dst[r * DH:(r + 1) * DH, 0, r]))
        return out

    def stage_hi(act, u):
        for src, hi, _, _ in query_parts(u):
            nc.scalar.copy(hi, src).then_inc(qs_hi, 1)

    def stage_lo(dve, u):
        dve.wait_ge(qs_hi, 4 * (u + 1))
        for src, _, lo, hi in query_parts(u):
            last = nc.vector.tensor_tensor(lo, src, hi, ALU.subtract)
        last.then_inc(qs_first, 1)

    def turned_probs(s):
        return ps[0:STEPS[s][2], 4 + s % BUFS, :].rearrange("p (g q) -> p g q", q=P)

    def unit_out(u):
        return ps[(u % 2) * DH:(u % 2 + 1) * DH, 7, :].rearrange("p (t r q) -> p r t q", r=2, q=P)

    def attention_act(act):
        for what, u, n in attention_order():
            i, kv = UNITS[u]
            if what == "logits":
                k0, nk = window(i)
                pr = probs[u % 2][:, n]
                for b, part in ((1, pr[:, 0:(i + 1) * P]), (2, pr[:, WIN0:WIN0 + nk]),
                                (0, pr[:, CMP0:CMP0 + min(N_CMP, 8 * i + 7)])):
                    act.wait_ge(s_min, 3 * (u * G + n) + {1: 1, 2: 2, 0: 3}[b])
                    nc.scalar.activation(part, part, ACT.Exp, bias=low[:, u % 2, n, b:b + 1], scale=-1.0,
                                         accum_out=den[:, u % 2, n, b:b + 1]).then_inc(p_exp, 1)
            elif what == "step":
                keys = STEPS[n][2]
                act.wait_ge(pt_done, n + 1)
                if n >= BUFS:
                    act.wait_ge(pv_done, n - BUFS + 1)
                nc.scalar.copy(probs_t[n % BUFS][0:keys], turned_probs(n)).then_inc(pt_copied, 1)
            elif what == "out":
                act.wait_ge(pv_done, STEPS_OF[u][1])
                out = unit_out(u)
                for r in range(2):
                    nc.scalar.copy(xt_hi[r * DH:(r + 1) * DH, 4 + 2 * kv:6 + 2 * kv, tile_cols(i)], out[:, r]).then_inc(o_hi, 1)

    def scalar_program(act):
        for t in range(TT):
            turn_hi(act, 0, t)
            if t in V_SPLITS:
                split_hi(act, ring["v"][V_SPLITS.index(t)])
        for c in ring["vg"][:2]:
            split_hi(act, c)
        for t in range(TT):
            if t < TT - 1:
                act.wait_ge(v_done, t + 1)
            else:
                act.wait_ge(w_used[ring["v"][3].slot], ring["v"][3].used)
            nc.scalar.activation(v_tok[:, t, :], ps[:, 4 + t % 4, :], ACT.Gelu_apprx_tanh).then_inc(v_gelu, 1)
            if t == 3:
                act.wait_ge(small_c, 6)
                act.dma_start(a["bias_scratch"], bias_row[:].unsqueeze(1).broadcast_to([HEADS, P, BIAS_ROW])).then_inc(bias_out, 16)
        feat = ring["feat"]
        split_hi(act, ring["vg"][2])
        act.wait_ge(v_mv, TT)
        nc.scalar.activation(v_rstd[:], v_mean[:, :, 1], ACT.Sqrt, bias=eps_c[:, 0:1]).then_inc(v_sd, 1)
        for c in feat[:6]:
            split_hi(act, c)
        for n, c in enumerate(feat):
            act.wait_ge(w_used[c.slot], c.used)
            got = banks(2 * (n % 2))
            if n < 2:
                last = nc.scalar.copy(cr[:, n, :], got)
            elif n < F_U:
                for kv in range(KV_HEADS):
                    last = nc.scalar.copy(ks[0:DH, kv, n - 2, :], got[kv * DH:(kv + 1) * DH, :])
            elif n < F_Q:
                if n > F_U:
                    act.wait_ge(u_mul, n - F_U)
                last = nc.scalar.activation(u_act[:], got, ACT.Gelu_apprx_tanh)
            else:
                if n == F_Q:
                    act.wait_ge(u_mul, GROUPS)
                last = nc.scalar.mul(q_t[:, n - F_Q, :], got, -SCALE)
            last.then_inc(feat_act, 1)
            if n + 6 < len(feat):
                split_hi(act, feat[n + 6])
        for g in range(GROUPS):
            nc.scalar.copy(xt_hi[:, g, :], mix_a[:, g, :]).then_inc(a_hi, 1)
        for kv in range(2):
            act.wait_ge(cmp_done, kv + 1)
            nc.scalar.activation(hid[:, kv, 0:N_CMP], ps[:, kv, 0:N_CMP], ACT.Gelu_apprx_tanh).then_inc(cmp_act, 1)
        stage_hi(act, 0)
        act.wait_ge(cmp_done, 3)
        for kv in range(KV_HEADS):
            nc.scalar.copy(kc[0:DH, kv, :], ps[kv * DH:(kv + 1) * DH, 4, 0:64]).then_inc(cmp_act, 1)
        stage_hi(act, 1)
        act.wait_ge(vg_out, TT)
        gates = vg[:, :, 2 * P:VG]
        nc.scalar.activation(gates, gates, ACT.Sigmoid).then_inc(gates_ok, 1)
        attention_act(act)

        def out_act(name, done, following):
            cs = ring[name]
            for k in range(KT):
                if done <= k < 6:
                    split_hi(act, cs[k])
                if name == "w_out":
                    act.wait_ge(x_in[k], 32)
                    scale_tile(act, k)
            for c in cs[6:] + following[:2]:
                split_hi(act, c)

        act.wait_ge(pv_done, len(STEPS))
        out_act("w_out", 0, ring["ffn0_first"])
        norm_act(act, "w_out", chunks=ring["ffn0_first"][2:])
        ffn_act(act, 0)
        norm_act(act, "ffn0", chunks=ring["conv_in"](0))

        def conv_trip(n, more):
            c, nxt = ring["conv_in"](n), ring["conv_in"](n + 1) if more else None
            for j in range(2):
                act.wait_ge(w_used[c[2 * j + 1].slot], c[2 * j + 1].used)
                if not (isinstance(n, int) and 2 * n + j == 0):
                    act.wait_ge(glu_free, 2 * n + j)
                act.nop()
                nc.scalar.activation(glu_g[:], banks(2), ACT.Sigmoid,
                                     bias=cols[:, bass.ds(2 * n + (KT + j), 1)]).then_inc(glu_sig, 1)
                if more:
                    split_hi(act, nxt[2 * j])
                    split_hi(act, nxt[2 * j + 1])
        conv_trip(0, True)
        with act.Fori(1, KT // 2 - 1) as n:
            conv_trip(n, True)
        conv_trip(KT // 2 - 1, False)
        act.wait_ge(part_done, KT + 2)
        for k in range(KT):
            act.wait_ge(cen, k + 1)
            if k >= 2:
                act.wait_ge(sq_used, k - 1)
            nc.scalar.activation(square[:, k % 2, :], acc[:, k, :], ACT.Square).then_inc(sq_ok, 1)
            if k in (4, 5):
                split_hi(act, ring["conv_out"][k - 4])
        split_hi(act, ring["conv_out"][2])
        act.wait_ge(sq_used, KT)
        nc.scalar.activation(conv_rs[:], banks(2), ACT.Sqrt, bias=eps_c[:, 0:1]).then_inc(var_sd, 1)
        for k in range(KT):
            act.wait_ge(nrm, k + 1)
            nc.scalar.activation(acc[:, k, :], acc[:, k, :], ACT.Silu, scale=cols[:, 3 * KT + k:3 * KT + k + 1],
                                 bias=cols[:, 4 * KT + k:4 * KT + k + 1]).then_inc(act_ok, 1)
            act.wait_ge(act_ok, k + 1)
            nc.scalar.copy(xt_hi[:, k, :], acc[:, k, :]).then_inc(act_hi, 1)
            if k in (0, 2, 4):
                split_hi(act, ring["conv_out"][3 + k // 2])
        out_act("conv_out", 6, ring["ffn1_first"])
        norm_act(act, "conv_out", chunks=ring["ffn1_first"][2:])
        ffn_act(act, 1)
        norm_act(act, "ffn1", turn=False)

    def ffn_dve(dve, layer):
        name = f"ffn{layer}"

        def prod(c, f):
            dve.wait_ge(w_used[c.slot], c.used)
            dve.wait_ge(silu_done[layer], f + 1)
            if not (isinstance(f, int) and f == 0):
                dve.wait_ge(h_lo[layer], f)
            nc.vector.tensor_tensor(h_f[:], banks(2), gate_act[:], ALU.mult).then_inc(h_prod[layer], 1)

        def lo(f, j):
            dve.wait_ge(h_hi[layer], f + 1)
            nc.vector.tensor_tensor(h_lo_t[:, j, :], h_f[:], h_hi_t[:, j, :], ALU.subtract).then_inc(h_lo[layer], 1)

        dve.sem_inc(y_free[name], 4)
        c = ring[name + "_first"]
        split_lo(dve, ring[name](0)[0])
        for f in range(2):
            prod(c[2 * f + 1], f)
            lo(f, f)
        dve.wait_ge(scaled, TT * NORM_OF[name])

        def trip(n, more):
            c = ring[name](n)
            for j in (1, 2, 3):
                split_lo(dve, c[j])
            for q in range(16):
                add_bank(dve, name, c[2], n, q)
            split_lo(dve, c[4])
            prod(c[3], 2 * n + 2)
            lo(2 * n + 2, 0)
            split_lo(dve, c[5])
            up_chunk = c[5]
            for c in [ring[name](n + 1)[0]] if more else ring[name + "_last"]:
                split_lo(dve, c)
            prod(up_chunk, 2 * n + 3)
            lo(2 * n + 3, 1)
        with dve.Fori(0, FG - 2) as n:
            trip(n, True)
        trip(FG - 2, False)

    def attention_dve(dve):
        for what, u, n in attention_order():
            i, kv = UNITS[u]
            par = u % 2
            if what == "logits":
                g, h = n, kv * G + n
                k0, nk = window(i)
                nc_ = min(N_CMP, 8 * i + 7)
                if g == 0 and u >= 2:
                    dve.wait_ge(pt_done, STEPS_OF[u - 2][1])
                if i == 0 and g == 0:
                    dve.wait_ge(nb_ok, kv + 1)
                pr = probs[par][:, g]
                for branch in range(2):
                    piece = (u * G + g) * 2 + branch
                    b = 2 * (piece % 2)
                    dve.wait_ge(s_done, piece + 1)
                    s = banks(b)
                    todo = [(1, pr[:, 0:(i + 1) * P], s[:, 0:(i + 1) * P], nbias[:, h, SEQ - (i + 1) * P:SEQ])]
                    if branch:
                        c0 = SEQ - P - P * i + CMP_BLOCK - 1
                        todo = [(2, pr[:, WIN0:WIN0 + nk], s[:, 0:nk], nbias[:, h, SEQ - nk:SEQ]),
                                (0, pr[:, CMP0:CMP0 + nc_], s[:, HALF + P:HALF + P + nc_],
                                 nbias[:, h, c0:c0 + CMP_STRIDE * (nc_ - 1) + 1:CMP_STRIDE])]
                    for col, out, logit, bias in todo:
                        nc.vector.tensor_tensor_reduce(out, logit, bias, 1.0, 3.0e38, ALU.add, ALU.min,
                                                       low[:, par, g, col:col + 1]).then_inc(s_min, 1)
            elif what == "norm":
                g, h = n, kv * G + n
                k0, nk = window(i)
                nc_ = min(N_CMP, 8 * i + 7)
                r = inv[:, par, g, :]
                dve.wait_ge(p_exp, 3 * (u * G + g) + 3)
                v_wait(dve, nc.vector.reciprocal(r, den[:, par, g, :]))
                if u == 0 and g == 0:
                    dve.wait_ge(gates_ok, 1)
                v_wait(dve, nc.vector.tensor_tensor(r, r, vg[:, i, 2 * P + 3 * h:2 * P + 3 * h + 3], ALU.mult))
                if i == 0:
                    v_wait(dve, nc.vector.tensor_tensor(r[:, 0:1], r[:, 0:1], row_ok[:], ALU.mult))
                pr = probs[par][:, g]
                for col, part in ((1, pr[:, 0:(i + 1) * P]), (2, pr[:, WIN0:WIN0 + nk]), (0, pr[:, CMP0:CMP0 + nc_])):
                    last = nc.vector.tensor_scalar(part, part, r[:, col:col + 1], None, ALU.mult)
                last.then_inc(p_norm, 1)
            elif what == "out":
                out = unit_out(u)
                for r in range(2):
                    dve.wait_ge(o_hi, 2 * u + 2)
                    to = (slice(r * DH, (r + 1) * DH), slice(4 + 2 * kv, 6 + 2 * kv), tile_cols(i))
                    nc.vector.tensor_tensor(xt_lo[to], out[:, r], xt_hi[to], ALU.subtract).then_inc(o_lo, 1)

    def vector_program(dve):
        for t in range(TT):
            turn_lo(dve, 0, t)
            if t in V_SPLITS:
                split_lo(dve, ring["v"][V_SPLITS.index(t)])
        for c in ring["vg"][:2]:
            split_lo(dve, c)
        third = BIAS_ROW // 3
        dve.wait_ge(small_t, 4)
        nc.vector.tensor_copy(ws_t[:].rearrange("p g t -> p (g t)"), ps[:, 0, :]).then_inc(small_c, 1)
        dve.wait_ge(small_t, 9)
        nc.vector.tensor_copy(cols[:], ps[:, 1, 0:40]).then_inc(small_c, 1)
        nc.vector.tensor_copy(pe_col[:].rearrange("p k j -> p (k j)"), ps[:, 1, 64:128]).then_inc(small_c, 1)
        for n, src in enumerate((ps[0:HEADS, 2, 0:third], ps[0:HEADS, 3, 0:third], ps[0:HEADS, 1, P:P + third])):
            nc.vector.tensor_scalar(bias_row[:, n * third:(n + 1) * third], src, -1.0, None, ALU.mult).then_inc(small_c, 1)
        dve.wait_ge(small_c, 3)
        for kv in range(2):
            x = pe_col[:, kv, CMP_STRIDE:]
            v_wait(dve, nc.vector.tensor_tensor(x, x, pe_col[:, kv, 0:CMP_STRIDE], ALU.subtract))
        for t in range(TT):
            dve.wait_ge(v_gelu, t + 1)
            v_wait(dve, nc.vector.bn_stats(v_stats[:, t, :], v_tok[:, t, :]))
            nc.vector.bn_aggr(v_mean[:, t, :], v_stats[:, t, :]).then_inc(v_mv, 1)
        feat = ring["feat"]
        split_lo(dve, ring["vg"][2])
        dve.wait_ge(v_sd, 1)
        v_wait(dve, nc.vector.reciprocal(v_rstd[:], v_rstd[:]))
        dve.wait_ge(bias_out, 16)
        for t in range(TT):
            if t < TT - 1:
                dve.wait_ge(vg_done, t + 1)
            else:
                dve.wait_ge(w_used[ring["vg"][2].slot], ring["vg"][2].used)
            nc.vector.tensor_copy(vg[:, t, :], ps[:, t % 4, 0:VG]).then_inc(vg_out, 1)
            x = v_tok[:, t, :]
            v_wait(dve, nc.vector.tensor_scalar(x, x, v_mean[:, t, 0:1], v_rstd[:, t:t + 1], ALU.subtract, ALU.mult))
            v_wait(dve, nc.vector.tensor_tensor(x, x, gmlp_g[:], ALU.mult))
            nc.vector.tensor_tensor(x, x, gmlp_b[:], ALU.add).then_inc(v_norm, 1)
            if t % 2 == 0 and t < 6:
                split_lo(dve, feat[t // 2])
        for c in feat[3:8]:
            split_lo(dve, c)
        for g in range(GROUPS):
            for h in range(2):
                n = 2 * g + h
                dve.wait_ge(mix_done, n + 1)
                nc.vector.tensor_tensor(mix_a[:, g, h * HALF:(h + 1) * HALF].rearrange("p (m t) -> p m t", t=P),
                                        ps[:, 4 + n % 4, :].rearrange("p (m t) -> p m t", t=P),
                                        gmlp_bs[:, g:g + 1, :].broadcast_to([P, 4, P]), ALU.add).then_inc(mix_add, 1)
        def encode(kv, half):
            x = cr[:, kv, :].rearrange("p (b j) -> p b j", j=CMP_STRIDE)
            share = pe_col[:, kv:kv + 1, half * CMP_STRIDE:(half + 1) * CMP_STRIDE]
            nc.vector.tensor_tensor(x, x, share.broadcast_to([P, SEQ // CMP_STRIDE, CMP_STRIDE]), ALU.add).then_inc(cr_ok, 1)

        for kv in range(2):
            dve.wait_ge(feat_act, kv + 1)
            encode(kv, 0)
        for n in range(2, F_Q):
            dve.wait_ge(feat_act, n + 1)
            if n < F_U:
                for kv in range(KV_HEADS):
                    last = nc.vector.tensor_tensor(ks[DH:P, kv, n - 2, :], banks(2 * (n % 2))[kv * DH:(kv + 1) * DH, :],
                                                   ks[0:DH, kv, n - 2, :], ALU.subtract)
                last.then_inc(feat_dve, 1)
            else:
                x = mix_a[:, n - F_U, :]
                if n == F_U:
                    dve.wait_ge(mix_add, 2 * GROUPS)
                nc.vector.tensor_tensor(x, x, u_act[:], ALU.mult).then_inc(u_mul, 1)
            if n + 6 < len(feat):
                split_lo(dve, feat[n + 6])
        for g in range(GROUPS):
            dve.wait_ge(a_hi, g + 1)
            nc.vector.tensor_tensor(xt_lo[:, g, :], mix_a[:, g, :], xt_hi[:, g, :], ALU.subtract).then_inc(a_lo, 1)
        for kv in range(2):
            dve.wait_ge(cmp_half, kv + 1)
            encode(kv, 1)
        stage_lo(dve, 0)
        for kv in range(KV_HEADS):
            dve.wait_ge(cmp_act, 3 + kv)
            nc.vector.tensor_tensor(kc[DH:P, kv, :], ps[kv * DH:(kv + 1) * DH, 4, 0:64], kc[0:DH, kv, :],
                                    ALU.subtract).then_inc(cmp_dve, 1)
        for kv in range(KV_HEADS):
            nc.vector.tensor_copy(vc[:, kv, :], ps[0:64, 5 + kv, 0:DH]).then_inc(cmp_dve, 1)
        stage_lo(dve, 1)
        attention_dve(dve)
        dve.wait_ge(tap_t, 1)
        nc.vector.tensor_copy(taps[:], ps[:, 0, 0:KT * 32].rearrange("p (k j) -> p k j", j=32)[:, :, 0:CONV_W]).then_inc(tap_ok, 1)

        def out_dve(name, done, following, added=0):
            cs = ring[name]
            if name == "w_out":
                dve.sem_inc(y_free[name], 4)
            for c in cs[done:2]:
                split_lo(dve, c)
            for t in range(TT):
                if name == "w_out":
                    dve.wait_ge(scaled, t + 1)
                for q in range(max(added, 2 * t), 2 * t + 2):
                    add_bank(dve, name, cs[1], 0, q)
                if max(2, done) <= t + 2 < 6:
                    split_lo(dve, cs[t + 2])
            for n in (1, 2):
                for c in (cs[6:] if n == 1 else following[:2]):
                    split_lo(dve, c)
                for q in range(16):
                    add_bank(dve, name, cs[2 * n + 1], n, q)
            norm_dve(dve, name, cs[7], chunks=following[2:])

        out_dve("w_out", 0, ring["ffn0_first"])
        ffn_dve(dve, 0)
        norm_dve(dve, "ffn0", ring["ffn0_last"][1], chunks=ring["conv_in"](0))
        dve.wait_ge(pad_ok, 2)

        def tap(n, m, j, first):
            out, x, w = tap_sum[:, m, :], conv_x[:, m, j:j + SEQ], tap_w[:, j:j + 1]
            if j == first:
                nc.vector.tensor_scalar(out, x, w, tap_w[:, CONV_W:], ALU.mult, ALU.add).then_inc(conv_v, 1)
            else:
                nc.vector.scalar_tensor_tensor(out=out, in0=x, scalar=w, in1=out, op0=ALU.mult, op1=ALU.add).then_inc(conv_v, 1)
            if isinstance(n, int) and 2 * n + m == KT - 1:
                dve.wait_ge(conv_v, DVE_TAPS * (KT - 2) + CONV_W - LAST_PE_TAPS[0] + j - first + 1)
            else:
                dve.wait_ge(conv_v, 2 * DVE_TAPS * n + (DVE_TAPS * m + j - first + 1))

        def add_part(T, m):
            sets_done = T + 1 if not isinstance(T, int) or T < KT - 2 else 2 * T + 4 - KT
            dve.wait_ge(part_done, sets_done)
            nc.vector.tensor_tensor(acc[:, bass.ds(T, 1), :], tap_sum[:, m:m + 1, :], banks(4).unsqueeze(1),
                                    ALU.add).then_inc(part_added, 1)

        def conv_trip(n, more):
            c, nxt = ring["conv_in"](n), ring["conv_in"](n + 1) if more else None
            for j in range(2):
                dve.wait_ge(glu_sig, 2 * n + (j + 1))
                if not (isinstance(n, int) and n == 0):
                    dve.wait_ge(part_done, 2 * n + (j - 1))
                nc.vector.scalar_tensor_tensor(out=conv_x[:, j, PAD:], in0=banks(0),
                                               scalar=cols[:, bass.ds(2 * n + j, 1)], in1=glu_g[:],
                                               op0=ALU.add, op1=ALU.mult).then_inc(glu_free, 1)
                if more:
                    split_lo(dve, nxt[2 * j])
                    split_lo(dve, nxt[2 * j + 1])
                nc.vector.tensor_copy(tap_w[:, 0:CONV_W].unsqueeze(1), taps[:, bass.ds(2 * n + j, 1), :]).then_inc(tap_w_ok, 1)
                nc.vector.tensor_copy(tap_w[:, CONV_W:], cols[:, bass.ds(2 * n + (2 * KT + j), 1)]).then_inc(tap_w_ok, 1)
                dve.wait_ge(tap_w_ok, 4 * n + (2 * j + 2))
                dve.wait_ge(glu_free, 2 * n + (j + 1))
                first = PE_TAPS if more else LAST_PE_TAPS[j]
                for m in range(first, CONV_W):
                    tap(n, j, m, first)
                    if m == first + 8 and not (isinstance(n, int) and 2 * n + j == 0):
                        add_part(2 * n + (j - 1), 1 - j)
        conv_trip(0, True)
        with dve.Fori(1, KT // 2 - 1) as n:
            conv_trip(n, True)
        conv_trip(KT // 2 - 1, False)
        add_part(KT - 1, 1)
        dve.wait_ge(mean_ok, 1)
        for k in range(KT):
            nc.vector.tensor_tensor(acc[:, k, :], acc[:, k, :], banks(6), ALU.subtract).then_inc(cen, 1)
        for c in ring["conv_out"][:3]:
            split_lo(dve, c)
        dve.wait_ge(cen, KT)
        dve.sem_inc(y_free["conv_out"], 4)
        dve.wait_ge(outb_ok, TT)
        dve.wait_ge(var_sd, 1)
        v_wait(dve, nc.vector.reciprocal(conv_rs[:], conv_rs[:]))
        added = 0
        for k in range(KT + 1):
            if k < KT:
                nc.vector.tensor_tensor(acc[:, k, :], acc[:, k, :], conv_rs[:], ALU.mult).then_inc(nrm, 1)
            if k:
                dve.wait_ge(act_hi, k)
                nc.vector.tensor_tensor(xt_lo[:, k - 1, :], acc[:, k - 1, :], xt_hi[:, k - 1, :], ALU.subtract).then_inc(act_lo, 1)
            if k in (1, 3, 5):
                split_lo(dve, ring["conv_out"][3 + k // 2])
            if k >= 3:
                for _ in range(2):
                    add_bank(dve, "conv_out", ring["conv_out"][1], 0, added)
                    added += 1
        out_dve("conv_out", 6, ring["ffn1_first"], added)
        ffn_dve(dve, 1)
        norm_dve(dve, "ffn1", ring["ffn1_last"][1], turn=False)

    def pool_program(pool):
        steps = [0]

        def g_wait(ins):
            ins.then_inc(g_step, 1)
            steps[0] += 1
            pool.wait_ge(g_step, steps[0])

        g_wait(nc.gpsimd.memset(ident[:], 0.0))
        nc.gpsimd.affine_select(out=ident[:], in_=ident[:], compare_op=ALU.not_equal, fill=1.0, base=0,
                                pattern=[[-1, P]], channel_multiplier=1).then_inc(const_ok, 1)
        pool.wait_ge(const_ok, 1)
        nc.gpsimd.memset(eps_c[:], EPS).then_inc(const_ok, 1)
        pool.wait_ge(const_ok, 2)
        load_small(pool)
        g_wait(nc.gpsimd.tensor_copy(ident_b[:], ident[:]))
        g_wait(nc.gpsimd.memset(far_mask[:], 0.0))
        g_wait(nc.gpsimd.affine_select(out=far_mask[:], in_=far_mask[:], compare_op=ALU.is_ge, fill=BIG, base=-1,
                                       pattern=[[1, P]], channel_multiplier=-1))
        g_wait(nc.gpsimd.memset(row_ok[:], 1.0))
        g_wait(nc.gpsimd.affine_select(out=row_ok[:], in_=row_ok[:], compare_op=ALU.is_ge, fill=0.0,
                                       base=1 - CMP_BLOCK, pattern=[[0, 1]], channel_multiplier=1))
        g_wait(nc.gpsimd.memset(hid[:], 0.0))
        pool.wait_ge(small_c, 1)
        nc.gpsimd.affine_select(out=ws_t[:], in_=ws_t[:], compare_op=ALU.is_ge, fill=0.0, base=0,
                                pattern=[[0, GROUPS], [1, P]], channel_multiplier=-1).then_inc(ws_ok, 1)
        pool.wait_ge(ws_ok, 1)

        def causal(kv):
            pool.wait_ge(nb_in[kv], 16)
            x = nbias[:, kv * G:(kv + 1) * G, SEQ - P:]
            nc.gpsimd.affine_select(out=x, in_=x, compare_op=ALU.is_ge, fill=BIG, base=0,
                                    pattern=[[0, G], [-1, P]], channel_multiplier=1).then_inc(nb_ok, 1)
            pool.wait_ge(nb_ok, kv + 1)

        causal(0)
        pool.wait_ge(cmp_done, 2)
        pool.wait_ge(feat_act, len(FEATURE_COLS))
        for u in range(STAGED, len(UNITS)):
            pool.wait_ge(s_done, 2 * G * (u - 1))
            parts = query_parts(u)
            for src, hi, _, _ in parts:
                g_wait(nc.gpsimd.tensor_copy(hi, src))
            for src, _, lo, hi in parts[:-1]:
                g_wait(nc.gpsimd.tensor_tensor(lo, src, hi, ALU.subtract))
            src, _, lo, hi = parts[-1]
            nc.gpsimd.tensor_tensor(lo, src, hi, ALU.subtract).then_inc(qs_ok, 1)
            pool.wait_ge(qs_ok, u - STAGED + 1)
            if u == STAGED:
                causal(1)
        pool.wait_ge(ln_done, 2 * TT)
        nc.gpsimd.memset(conv_x[:, 0, 0:PAD], 0.0).then_inc(pad_ok, 1)
        pool.wait_ge(pad_ok, 1)
        nc.gpsimd.memset(conv_x[:, 1, 0:PAD], 0.0).then_inc(pad_ok, 1)
        pool.wait_ge(pad_ok, 2)
        g_wait(nc.gpsimd.memset(ones_m[:], 1.0 / D))

        def diagonals(number, T, tap0=0):
            if number >= 2:
                pool.wait_ge(part_done, number - 1)
            nc.gpsimd.tensor_tensor(diag[:, number % 2], ident[:].unsqueeze(1).broadcast_to([P, PE_TAPS, P]),
                                    taps[:, T, tap0:tap0 + PE_TAPS].unsqueeze(2).broadcast_to([P, PE_TAPS, P]),
                                    ALU.mult).then_inc(diag_ok, 1)
            pool.wait_ge(diag_ok, number + 1)
        for c in ring["ffn0_last"]:
            pool.wait_ge(w_used[c.slot], c.used)
        diagonals(0, 0)
        diagonals(1, 1)
        pool.wait_ge(outb_in, 16)
        for t in range(TT):
            pool.wait_ge(scaled, 2 * TT + t + 1)
            nc.gpsimd.tensor_tensor(resid[:, t, :], resid[:, t, :], out_b[:], ALU.add).then_inc(outb_ok, 1)
            pool.wait_ge(outb_ok, t + 1)
        for T in range(2, KT - 2):
            diagonals(T, T)
        for n in range(2):
            diagonals(KT - 2 + 2 * n, KT - 2 + n)
            diagonals(KT - 1 + 2 * n, KT - 2 + n, PE_TAPS)

    with nc.Block() as block:
        @block.sync
        def _(sp):
            sync_program(sp)

        @block.scalar
        def _(act):
            scalar_program(act)

        @block.vector
        def _(dve):
            vector_program(dve)

        @block.tensor
        def _(pe):
            tensor_program(pe)

        @block.gpsimd
        def _(pool):
            pool_program(pool)


def bucket_onehot():
    n = np.maximum(np.arange(SEQ - 1, SEQ - 1 - BIAS_ROW, -1), 0)
    exact = N_BUCKETS // 2
    nf = np.maximum(n, 1).astype(np.float32)
    ratio = np.log(nf / np.float32(exact)) / np.float32(np.log(MAX_DISTANCE / exact))
    large = np.minimum(exact + (ratio * np.float32(N_BUCKETS - exact)).astype(np.int32), N_BUCKETS - 1)
    bucket = np.where(n < exact, n, large)
    return (bucket[None, :] == np.arange(N_BUCKETS)[:, None]).astype(np.float32)


def kernel(**inputs):
    import concourse.bacc as bacc
    from concourse.bass_utils import run_bass_kernel_spmd

    nc = bacc.Bacc("TRN2", target_bir_lowering=False, num_devices=1)
    arrays, aps = {}, {}
    for name, x in {**inputs, "bucket_onehot": bucket_onehot()}.items():
        x = np.ascontiguousarray(x)
        if x.shape[0] == 1:
            x = x.reshape(x.shape[1:])
        arrays[f"in_{name}"] = x
        aps[name] = nc.dram_tensor(f"in_{name}", x.shape, mybir.dt.from_np(x.dtype), kind="ExternalInput").ap()
    aps["out"] = nc.dram_tensor("out_y", [SEQ, D], F32, kind="ExternalOutput").ap()
    aps["bias_scratch"] = nc.dram_tensor("bias_scratch", [HEADS, P, BIAS_ROW], F32, kind="Internal").ap()
    build(nc, aps)
    result = run_bass_kernel_spmd(nc, [arrays], core_ids=[0])
    return result.results[0]["out_y"].reshape(1, SEQ, D)
```
